# Optimizing a Trainium2 kernel written in Bass

```python
import jax, jax.numpy as jnp
from jax import lax
import numpy as np
import jax
import jax.numpy as jnp

D_MODEL = 1024
BATCH = 1
SEQ = 256
DEPTH = 2

N_MIXERS = 2
N_MLSTM = (DEPTH + 1) // 2
N_HGRN = DEPTH // 2
CHUNK = 64
M_HEADS = 8
M_DV = D_MODEL // M_HEADS
M_DQK = M_DV // 2
M_QK = M_HEADS * M_DQK
M_V = M_HEADS * M_DV
M_PROJ = 2 * M_QK + 2 * M_V + 2 * M_HEADS
CONV_K = 4
IGATE_CAP = 15.0
HG_EXPAND = 128
HG_HEADS = D_MODEL // HG_EXPAND
HG_DK = HG_EXPAND
HG_DV = D_MODEL // HG_HEADS
HG_PROJ = 2 * HG_HEADS * HG_DK + 2 * D_MODEL
D_FF = 2816
N_EXPERTS = 8
TOP_K = 2
D_FF_EXPERT = D_FF // 2
EPS = 1e-6
NEG = -1e30
F_FLOOR = 1e-30


def rmsnorm(x, w):
    x32 = x.astype(jnp.float32)
    y = x32 * lax.rsqrt(jnp.mean(x32 * x32, axis=-1, keepdims=True) + EPS)
    return (y * w.astype(jnp.float32)).astype(x.dtype)

def head_rmsnorm(h, w):
    nh, dh = h.shape[1], h.shape[3]
    y = h * lax.rsqrt(jnp.mean(h * h, axis=-1, keepdims=True) + EPS)
    return y * w.astype(jnp.float32).reshape(1, nh, 1, dh)

def split_heads(a, nh):
    b, s, _ = a.shape
    return a.reshape(b, s, nh, -1).transpose(0, 2, 1, 3)

def merge_heads(a):
    b, h, s, d = a.shape
    return a.transpose(0, 2, 1, 3).reshape(b, s, h * d)

def to_chunks(a):
    b, h, s = a.shape[:3]
    return jnp.moveaxis(a.reshape((b, h, s // CHUNK, CHUNK) + a.shape[3:]), 2, 0)

def from_chunks(a):
    a = jnp.moveaxis(a, 0, 2)
    b, h, nc, l = a.shape[:4]
    return a.reshape((b, h, nc * l) + a.shape[4:])

def causal_conv(x, w, b):
    ch = x.shape[-1]
    y = lax.conv_general_dilated(x, w[:, None, :].astype(x.dtype), window_strides=(1,),
                                 padding=[(w.shape[0] - 1, 0)],
                                 dimension_numbers=('NWC', 'WIO', 'NWC'),
                                 feature_group_count=ch)
    return y + b.astype(x.dtype)

def mlstm_chunkwise(q, k, v, li, f_pre):
    bsz, nh, _, dk = q.shape
    dv = v.shape[-1]
    lf = jax.nn.log_sigmoid(f_pre)
    mask = jnp.tril(jnp.ones((CHUNK, CHUNK), dtype=bool))

    def step(carry, xs):
        c_st, n_st, m_st = carry
        qc, kc, vc, lic, lfc = xs
        b = jnp.cumsum(lfc, axis=-1)
        d = jnp.where(mask, b[..., :, None] - b[..., None, :] + lic[..., None, :], NEG)
        inter = b + m_st[..., None]
        m_t = jnp.maximum(inter, jnp.max(d, axis=-1))
        w_inter = jnp.exp(inter - m_t)
        s = jnp.einsum('bhtd,bhsd->bhts', qc, kc) * jnp.exp(d - m_t[..., None])
        num = (w_inter[..., None] * jnp.einsum('bhtd,bhdv->bhtv', qc, c_st)
               + jnp.einsum('bhts,bhsv->bhtv', s, vc))
        den = w_inter * jnp.einsum('bhtd,bhd->bht', qc, n_st) + jnp.sum(s, axis=-1)
        h = num / jnp.maximum(jnp.abs(den), jnp.exp(-m_t))[..., None]
        b_last = b[..., -1]
        dl = b_last[..., None] - b + lic
        m_new = jnp.maximum(b_last + m_st, jnp.max(dl, axis=-1))
        wk = jnp.exp(dl - m_new[..., None])
        decay = jnp.exp(b_last + m_st - m_new)
        c_new = decay[..., None, None] * c_st + jnp.einsum('bhs,bhsd,bhsv->bhdv', wk, kc, vc)
        n_new = decay[..., None] * n_st + jnp.einsum('bhs,bhsd->bhd', wk, kc)
        return (c_new, n_new, m_new), h

    init = (jnp.zeros((bsz, nh, dk, dv), jnp.float32),
            jnp.zeros((bsz, nh, dk), jnp.float32),
            jnp.zeros((bsz, nh), jnp.float32))
    _, hs = lax.scan(step, init, (to_chunks(q), to_chunks(k), to_chunks(v), to_chunks(li), to_chunks(lf)))
    return from_chunks(hs)

def hgrn2_chunkwise(q, k, log_f, v):
    bsz, nh, _, dk = q.shape
    dv = v.shape[-1]
    mask = jnp.tril(jnp.ones((CHUNK, CHUNK), dtype=bool))

    def step(s_st, xs):
        qc, kc, gc, vc = xs
        bc = jnp.cumsum(gc, axis=2)
        diff = bc[:, :, :, None, :] - bc[:, :, None, :, :]
        decay = jnp.exp(jnp.where(mask[:, :, None], diff, NEG))
        a = jnp.einsum('bhtd,bhsd,bhtsd->bhts', qc, kc, decay)
        o = (jnp.einsum('bhtd,bhdv->bhtv', qc * jnp.exp(bc), s_st)
             + jnp.einsum('bhts,bhsv->bhtv', a, vc))
        b_last = bc[:, :, -1]
        s_new = (jnp.exp(b_last)[..., None] * s_st
                 + jnp.einsum('bhsd,bhsv->bhdv', kc * jnp.exp(b_last[:, :, None] - bc), vc))
        return s_new, o

    init = jnp.zeros((bsz, nh, dk, dv), jnp.float32)
    _, os_ = lax.scan(step, init, (to_chunks(q), to_chunks(k), to_chunks(log_f), to_chunks(v)))
    return from_chunks(os_)

def mlstm_mixer(h, w_in, i_bias, f_bias, conv_w, conv_b, norm_w, w_out):
    proj = h @ w_in
    qk = jax.nn.silu(causal_conv(proj[..., :2 * M_QK], conv_w, conv_b))
    q = split_heads(qk[..., :M_QK], M_HEADS).astype(jnp.float32)
    k = split_heads(qk[..., M_QK:], M_HEADS).astype(jnp.float32) * (M_DQK ** -0.5)
    v = split_heads(proj[..., 2 * M_QK:2 * M_QK + M_V], M_HEADS).astype(jnp.float32)
    o = proj[..., 2 * M_QK + M_V:2 * M_QK + 2 * M_V]
    gates = proj[..., 2 * M_QK + 2 * M_V:].astype(jnp.float32)
    i_pre = gates[..., :M_HEADS] + i_bias.astype(jnp.float32)
    i_pre = IGATE_CAP * jnp.tanh(i_pre / IGATE_CAP)
    f_pre = gates[..., M_HEADS:] + f_bias.astype(jnp.float32)
    hh = mlstm_chunkwise(q, k, v, jnp.swapaxes(i_pre, 1, 2), jnp.swapaxes(f_pre, 1, 2))
    hh = merge_heads(head_rmsnorm(hh, norm_w)).astype(h.dtype) * jax.nn.sigmoid(o)
    return hh @ w_out

def hgrn2_mixer(h, w_in, lb, norm_w, w_out):
    proj = h @ w_in
    fd = HG_HEADS * HG_DK
    q = jax.nn.silu(proj[..., :fd]).astype(jnp.float32)
    f = proj[..., fd:2 * fd].astype(jnp.float32)
    i = proj[..., 2 * fd:2 * fd + D_MODEL].astype(jnp.float32)
    g = proj[..., 2 * fd + D_MODEL:]
    lb = lb.astype(jnp.float32)
    f_t = lb + (1.0 - lb) * jax.nn.sigmoid(f)
    log_f = jnp.log(jnp.maximum(f_t, F_FLOOR))
    k = (1.0 - lb) * jax.nn.sigmoid(-f)
    o = hgrn2_chunkwise(split_heads(q, HG_HEADS), split_heads(k, HG_HEADS),
                        split_heads(log_f, HG_HEADS), split_heads(i, HG_HEADS))
    o = merge_heads(head_rmsnorm(o, norm_w)).astype(h.dtype) * jax.nn.silu(g)
    return o @ w_out

def swiglu(t, wg, wu, wd):
    return (jax.nn.silu(t @ wg) * (t @ wu)) @ wd

def moe_swiglu(h, router_w, wg, wu, wd):
    bsz, s, d = h.shape
    t = h.reshape(bsz * s, d)
    logits = (t @ router_w).astype(jnp.float32)
    top_logits, top_idx = lax.top_k(logits, TOP_K)
    top_w = jax.nn.softmax(top_logits, axis=-1)
    gates = jnp.einsum('tk,tke->te', top_w, jax.nn.one_hot(top_idx, N_EXPERTS, dtype=jnp.float32)).astype(h.dtype)
    y = jnp.zeros_like(t)
    for e in range(N_EXPERTS):
        y = y + gates[:, e:e + 1] * swiglu(t, wg[e], wu[e], wd[e])
    return y.reshape(bsz, s, d)

def first_inputs(seed: int = 0) -> dict:
    key = jax.random.key(seed)
    ks = iter(jax.random.split(key, 32))

    def nrm(shape, scale):
        return jax.random.normal(next(ks), shape, jnp.float32) * scale

    d = D_MODEL
    return {
        'x': nrm((BATCH, SEQ, d), 1.0),
        'c': nrm((BATCH, d), 1.0),
        'ada_w': nrm((DEPTH, d, 6 * d), 0.5 * d ** -0.5),
        'ada_b': nrm((DEPTH, 6 * d), 0.02),
        'norm1_w': 1.0 + nrm((DEPTH, d), 0.02),
        'norm2_w': 1.0 + nrm((DEPTH, d), 0.02),
        'final_norm_w': 1.0 + nrm((d,), 0.02),
        'm_w_in': nrm((N_MLSTM, d, M_PROJ), d ** -0.5),
        'm_i_bias': nrm((N_MLSTM, M_HEADS), 0.1),
        'm_f_bias': jnp.linspace(3.0, 6.0, M_HEADS, dtype=jnp.float32)[None, :] + nrm((N_MLSTM, M_HEADS), 0.1),
        'm_conv_w': nrm((N_MLSTM, CONV_K, 2 * M_QK), CONV_K ** -0.5),
        'm_conv_b': nrm((N_MLSTM, 2 * M_QK), 0.01),
        'm_norm_w': 1.0 + nrm((N_MLSTM, M_V), 0.02),
        'm_w_out': nrm((N_MLSTM, M_V, d), M_V ** -0.5),
        'h_w_in': nrm((N_HGRN, d, HG_PROJ), d ** -0.5),
        'h_lb_logits': nrm((N_HGRN, HG_HEADS * HG_DK), 0.5),
        'h_norm_w': 1.0 + nrm((N_HGRN, d), 0.02),
        'h_w_out': nrm((N_HGRN, d, d), d ** -0.5),
        'ffn_w_gate': nrm((N_MLSTM, d, D_FF), d ** -0.5),
        'ffn_w_up': nrm((N_MLSTM, d, D_FF), d ** -0.5),
        'ffn_w_down': nrm((N_MLSTM, D_FF, d), D_FF ** -0.5),
        'moe_router': nrm((N_HGRN, d, N_EXPERTS), d ** -0.5),
        'moe_w_gate': nrm((N_HGRN, N_EXPERTS, d, D_FF_EXPERT), d ** -0.5),
        'moe_w_up': nrm((N_HGRN, N_EXPERTS, d, D_FF_EXPERT), d ** -0.5),
        'moe_w_down': nrm((N_HGRN, N_EXPERTS, D_FF_EXPERT, d), D_FF_EXPERT ** -0.5),
    }

def first_block(x, c, ada_w, ada_b, norm1_w, norm2_w, final_norm_w,
              m_w_in, m_i_bias, m_f_bias, m_conv_w, m_conv_b, m_norm_w, m_w_out,
              h_w_in, h_lb_logits, h_norm_w, h_w_out,
              ffn_w_gate, ffn_w_up, ffn_w_down,
              moe_router, moe_w_gate, moe_w_up, moe_w_down):
    cond = jax.nn.silu(c)
    gam = jax.nn.softmax(h_lb_logits.astype(jnp.float32), axis=0)
    lower_bounds = jnp.cumsum(gam, axis=0) - gam[:1]
    for layer in range(DEPTH):
        j = layer // N_MIXERS
        mod = (cond @ ada_w[layer] + ada_b[layer])[:, None, :]
        shift1, scale1, gate1, shift2, scale2, gate2 = jnp.split(mod, 6, axis=-1)
        hn = rmsnorm(x, norm1_w[layer]) * (1 + scale1) + shift1
        if layer % N_MIXERS == 0:
            y = mlstm_mixer(hn, m_w_in[j], m_i_bias[j], m_f_bias[j], m_conv_w[j], m_conv_b[j],
                            m_norm_w[j], m_w_out[j])
        else:
            y = hgrn2_mixer(hn, h_w_in[j], lower_bounds[j], h_norm_w[j], h_w_out[j])
        x = x + gate1 * y
        hn = rmsnorm(x, norm2_w[layer]) * (1 + scale2) + shift2
        if layer % 2 == 0:
            y = swiglu(hn, ffn_w_gate[j], ffn_w_up[j], ffn_w_down[j])
        else:
            y = moe_swiglu(hn, moe_router[j], moe_w_gate[j], moe_w_up[j], moe_w_down[j])
        x = x + gate2 * y
    return rmsnorm(x, final_norm_w)


DEPTH_2 = 1

MEM_LEN = 256
MOBA_HEADS = 8
MOBA_HEAD_DIM = 64
MOBA_BLOCK = 256
MOBA_TOPK = 3
FOX_HEADS = 8
FOX_HEAD_DIM = 64
MEM_HEADS = 4
MEM_HEAD_DIM = 128
Q_BLOCK = 128
ROPE_THETA = 500000.0
ROPE_FRACTION_DIV = 4
N_BRANCHES = 3
D_FF_2 = ((-((-8 * D_MODEL) // 3)) + 255) // 256 * 256
NORM_EPS = 1e-6
MOBA_WIDTH = MOBA_HEADS * MOBA_HEAD_DIM
FOX_WIDTH = FOX_HEADS * FOX_HEAD_DIM
MEM_WIDTH = MEM_HEADS * MEM_HEAD_DIM
IN_SIZES = (MOBA_WIDTH,) * 3 + (FOX_WIDTH,) * 3 + (FOX_HEADS, MEM_WIDTH) + (D_MODEL,) * N_BRANCHES
D_IN = sum(IN_SIZES)


def rms_norm(x, gain):
    xf = x.astype(jnp.float32)
    y = xf * lax.rsqrt(jnp.mean(xf * xf, axis=-1, keepdims=True) + NORM_EPS)
    return (y * gain.astype(jnp.float32)).astype(x.dtype)

def split_heads_2(t, n_heads):
    b, s, _ = t.shape
    return t.reshape(b, s, n_heads, -1).transpose(0, 2, 1, 3)

def merge_heads_2(t):
    b, h, s, d = t.shape
    return t.transpose(0, 2, 1, 3).reshape(b, s, h * d)

def partial_rope(t):
    seq, dim = t.shape[2], t.shape[3]
    rot = dim // ROPE_FRACTION_DIV
    half = rot // 2
    inv_freq = 1.0 / (ROPE_THETA ** (jnp.arange(half, dtype=jnp.float32) * 2.0 / rot))
    ang = jnp.arange(seq, dtype=jnp.float32)[:, None] * inv_freq[None, :]
    cos, sin = jnp.cos(ang), jnp.sin(ang)
    tf = t.astype(jnp.float32)
    x1, x2 = tf[..., :half], tf[..., half:rot]
    out = jnp.concatenate([x1 * cos - x2 * sin, x2 * cos + x1 * sin, tf[..., rot:]], axis=-1)
    return out.astype(t.dtype)

def moba_attention(q, k, v):
    b, h, s, d = q.shape
    scale = d ** -0.5
    n_blocks = -(-s // MOBA_BLOCK)
    pad = n_blocks * MOBA_BLOCK - s
    kp = jnp.pad(k, ((0, 0), (0, 0), (0, pad), (0, 0)))
    vp = jnp.pad(v, ((0, 0), (0, 0), (0, pad), (0, 0)))
    kb = kp.reshape(b, h, n_blocks, MOBA_BLOCK, d)
    vb = vp.reshape(b, h, n_blocks, MOBA_BLOCK, d)
    k_mean = jnp.mean(kb.astype(jnp.float32), axis=3)
    topk = min(MOBA_TOPK, n_blocks)
    b_idx = jnp.arange(b)[:, None, None, None]
    h_idx = jnp.arange(h)[None, :, None, None]
    key_off = jnp.arange(MOBA_BLOCK)
    q_off = jnp.arange(Q_BLOCK)
    block_ids = jnp.arange(n_blocks)

    def chunk(ci):
        t0 = ci * Q_BLOCK
        cur = t0 // MOBA_BLOCK
        qc = lax.dynamic_slice_in_dim(q, t0, Q_BLOCK, axis=2)
        gate = jnp.einsum('bhqd,bhnd->bhqn', qc.astype(jnp.float32), k_mean)
        gate = jnp.where(block_ids < cur, gate, -jnp.inf)
        _, sel = lax.top_k(gate, topk)
        sel_valid = sel < cur
        k_sel = kb[b_idx, h_idx, sel]
        v_sel = vb[b_idx, h_idx, sel]
        s_sel = jnp.einsum('bhqd,bhqnkd->bhqnk', qc, k_sel).astype(jnp.float32) * scale
        s_sel = jnp.where(sel_valid[..., None], s_sel, -jnp.inf)
        k_own = lax.dynamic_slice_in_dim(kp, cur * MOBA_BLOCK, MOBA_BLOCK, axis=2)
        v_own = lax.dynamic_slice_in_dim(vp, cur * MOBA_BLOCK, MOBA_BLOCK, axis=2)
        s_own = jnp.einsum('bhqd,bhkd->bhqk', qc, k_own).astype(jnp.float32) * scale
        causal = (key_off[None, :] + cur * MOBA_BLOCK) <= (q_off[:, None] + t0)
        s_own = jnp.where(causal, s_own, -jnp.inf)
        scores = jnp.concatenate([s_sel.reshape(b, h, Q_BLOCK, topk * MOBA_BLOCK), s_own], axis=-1)
        p = jax.nn.softmax(scores, axis=-1).astype(v.dtype)
        p_sel = p[..., :topk * MOBA_BLOCK].reshape(b, h, Q_BLOCK, topk, MOBA_BLOCK)
        p_own = p[..., topk * MOBA_BLOCK:]
        return (jnp.einsum('bhqnk,bhqnkd->bhqd', p_sel, v_sel)
                + jnp.einsum('bhqk,bhkd->bhqd', p_own, v_own))

    out = lax.map(chunk, jnp.arange(s // Q_BLOCK))
    return jnp.moveaxis(out, 0, 2).reshape(b, h, s, d)

def fox_attention(q, k, v, log_f):
    b, h, s, d = q.shape
    scale = d ** -0.5
    cum = jnp.cumsum(log_f, axis=-1)
    key_pos = jnp.arange(s)
    q_off = jnp.arange(Q_BLOCK)

    def chunk(ci):
        t0 = ci * Q_BLOCK
        qc = lax.dynamic_slice_in_dim(q, t0, Q_BLOCK, axis=2)
        cq = lax.dynamic_slice_in_dim(cum, t0, Q_BLOCK, axis=2)
        scores = (jnp.einsum('bhqd,bhkd->bhqk', qc, k).astype(jnp.float32) * scale
                  + cq[..., None] - cum[:, :, None, :])
        causal = key_pos[None, :] <= (q_off[:, None] + t0)
        scores = jnp.where(causal, scores, -jnp.inf)
        p = jax.nn.softmax(scores, axis=-1).astype(v.dtype)
        return jnp.einsum('bhqk,bhkd->bhqd', p, v)

    out = lax.map(chunk, jnp.arange(s // Q_BLOCK))
    return jnp.moveaxis(out, 0, 2).reshape(b, h, s, d)

def memory_attention(q, mk, mv):
    scale = q.shape[-1] ** -0.5
    scores = jnp.einsum('bhsd,bhmd->bhsm', q, mk).astype(jnp.float32) * scale
    p = jax.nn.softmax(scores, axis=-1).astype(mv.dtype)
    return jnp.einsum('bhsm,bhmd->bhsd', p, mv)

def second_inputs(seed: int = 0) -> dict:
    key = jax.random.key(seed)
    ks = jax.random.split(key, 24)
    L = DEPTH_2

    def normal(k, shape, scale):
        return jax.random.normal(k, shape, jnp.float32) * scale

    def gain(k, shape):
        return 1.0 + 0.1 * jax.random.normal(k, shape, jnp.float32)

    return {
        "x": normal(ks[0], (BATCH, SEQ, D_MODEL), 1.0),
        "mem": normal(ks[1], (BATCH, MEM_LEN, D_MODEL), 1.0),
        "g_mix": gain(ks[2], (L, D_MODEL)),
        "w_in": normal(ks[3], (L, D_MODEL, D_IN), D_MODEL ** -0.5),
        "b_forget": 4.0 + 0.5 * jax.random.normal(ks[4], (L, FOX_HEADS), jnp.float32),
        "g_q_moba": gain(ks[5], (L, MOBA_HEAD_DIM)),
        "g_k_moba": gain(ks[6], (L, MOBA_HEAD_DIM)),
        "g_q_fox": gain(ks[7], (L, FOX_HEAD_DIM)),
        "g_k_fox": gain(ks[8], (L, FOX_HEAD_DIM)),
        "g_q_mem": gain(ks[9], (L, MEM_HEAD_DIM)),
        "g_k_mem": gain(ks[10], (L, MEM_HEAD_DIM)),
        "g_mem": gain(ks[11], (L, D_MODEL)),
        "w_mem_kv": normal(ks[12], (L, D_MODEL, 2 * MEM_WIDTH), D_MODEL ** -0.5),
        "w_br_moba": normal(ks[13], (L, MOBA_WIDTH, D_MODEL), MOBA_WIDTH ** -0.5),
        "w_br_fox": normal(ks[14], (L, FOX_WIDTH, D_MODEL), FOX_WIDTH ** -0.5),
        "w_br_mem": normal(ks[15], (L, MEM_WIDTH, D_MODEL), MEM_WIDTH ** -0.5),
        "w_out": normal(ks[16], (L, D_MODEL, D_MODEL), D_MODEL ** -0.5),
        "g_ffn": gain(ks[17], (L, D_MODEL)),
        "w_gate": normal(ks[18], (L, D_MODEL, D_FF_2), D_MODEL ** -0.5),
        "w_up": normal(ks[19], (L, D_MODEL, D_FF_2), D_MODEL ** -0.5),
        "w_down": normal(ks[20], (L, D_FF_2, D_MODEL), D_FF_2 ** -0.5),
    }

def second_block(x, mem, g_mix, w_in, b_forget, g_q_moba, g_k_moba, g_q_fox, g_k_fox, g_q_mem, g_k_mem,
              g_mem, w_mem_kv, w_br_moba, w_br_fox, w_br_mem, w_out, g_ffn, w_gate, w_up, w_down):
    split_points = np.cumsum(IN_SIZES)[:-1].tolist()
    for layer in range(DEPTH_2):
        h = rms_norm(x, g_mix[layer])
        proj = h @ w_in[layer]
        (q_m, k_m, v_m, q_f, k_f, v_f, f_logit, q_c, a_m, a_f, a_c) = jnp.split(proj, split_points, axis=-1)

        q_m = partial_rope(rms_norm(split_heads_2(q_m, MOBA_HEADS), g_q_moba[layer]))
        k_m = partial_rope(rms_norm(split_heads_2(k_m, MOBA_HEADS), g_k_moba[layer]))
        y_m = moba_attention(q_m, k_m, split_heads_2(v_m, MOBA_HEADS))

        log_f = jax.nn.log_sigmoid(f_logit.astype(jnp.float32)
                                   + b_forget[layer].astype(jnp.float32)).transpose(0, 2, 1)
        q_f = rms_norm(split_heads_2(q_f, FOX_HEADS), g_q_fox[layer])
        k_f = rms_norm(split_heads_2(k_f, FOX_HEADS), g_k_fox[layer])
        y_f = fox_attention(q_f, k_f, split_heads_2(v_f, FOX_HEADS), log_f)

        mkv = rms_norm(mem, g_mem[layer]) @ w_mem_kv[layer]
        mk, mv = jnp.split(mkv, 2, axis=-1)
        mk = rms_norm(split_heads_2(mk, MEM_HEADS), g_k_mem[layer])
        q_c = rms_norm(split_heads_2(q_c, MEM_HEADS), g_q_mem[layer])
        y_c = memory_attention(q_c, mk, split_heads_2(mv, MEM_HEADS))

        merged = (jax.nn.sigmoid(a_m) * (merge_heads_2(y_m) @ w_br_moba[layer])
                  + jax.nn.sigmoid(a_f) * (merge_heads_2(y_f) @ w_br_fox[layer])
                  + jax.nn.sigmoid(a_c) * (merge_heads_2(y_c) @ w_br_mem[layer]))
        x = x + merged @ w_out[layer]

        h2 = rms_norm(x, g_ffn[layer])
        x = x + (jax.nn.silu(h2 @ w_gate[layer]) * (h2 @ w_up[layer])) @ w_down[layer]
    return x


def setup_inputs(seed=0):
    out = dict(first_inputs(seed))
    for name, value in second_inputs(seed + 1).items():
        if name != "x":
            out[name + "_2"] = value
    return out


def reference(
    x, c, ada_w, ada_b, norm1_w, norm2_w, final_norm_w, m_w_in, m_i_bias, m_f_bias, m_conv_w,
    m_conv_b, m_norm_w, m_w_out, h_w_in, h_lb_logits, h_norm_w, h_w_out, ffn_w_gate, ffn_w_up,
    ffn_w_down, moe_router, moe_w_gate, moe_w_up, moe_w_down, mem_2, g_mix_2, w_in_2,
    b_forget_2, g_q_moba_2, g_k_moba_2, g_q_fox_2, g_k_fox_2, g_q_mem_2, g_k_mem_2, g_mem_2,
    w_mem_kv_2, w_br_moba_2, w_br_fox_2, w_br_mem_2, w_out_2, g_ffn_2, w_gate_2, w_up_2,
    w_down_2,
):
    x = first_block(
        x, c, ada_w, ada_b, norm1_w, norm2_w, final_norm_w, m_w_in, m_i_bias, m_f_bias,
        m_conv_w, m_conv_b, m_norm_w, m_w_out, h_w_in, h_lb_logits, h_norm_w, h_w_out,
        ffn_w_gate, ffn_w_up, ffn_w_down, moe_router, moe_w_gate, moe_w_up, moe_w_down,
    )
    return second_block(
        x, mem_2, g_mix_2, w_in_2, b_forget_2, g_q_moba_2, g_k_moba_2, g_q_fox_2, g_k_fox_2,
        g_q_mem_2, g_k_mem_2, g_mem_2, w_mem_kv_2, w_br_moba_2, w_br_fox_2, w_br_mem_2, w_out_2,
        g_ffn_2, w_gate_2, w_up_2, w_down_2,
    )


_drawn_inputs = setup_inputs


def setup_inputs(seed=0):
    import zlib

    import numpy as np

    out = dict(_drawn_inputs(seed))
    spreads = {}
    factors = {'norm1_w': 3.685,
     'norm2_w': 2.859,
     'm_i_bias': 8.0,
     'm_conv_b': 8.0,
     'm_norm_w': 6.537,
     'h_norm_w': 4.588,
     'g_q_moba_2': 4.199,
     'g_k_moba_2': 5.651,
     'g_q_fox_2': 4.697,
     'g_k_fox_2': 4.615,
     'g_q_mem_2': 8.0,
     'g_k_mem_2': 8.0,
     'g_mem_2': 5.847,
     'b_forget_2': 32.272}
    for name, (base, spread) in spreads.items():
        noise = np.random.default_rng([zlib.crc32(name.encode()), seed]).standard_normal(out[name].shape)
        drawn = base * np.exp(spread * noise) if base else spread * noise
        out[name] = jnp.asarray(drawn.astype(out[name].dtype))
    for name, factor in factors.items():
        out[name] = (out[name] * factor).astype(out[name].dtype)
    return out
```

```python
from contextlib import ExitStack

import numpy as np
import concourse.bass as bass
from concourse import mybir

SEQ, D = 256, 1024
KT = D // 128
TT = SEQ // 128
M_HEADS, M_DQK, M_DV = 8, 64, 128
M_QK, M_V = M_HEADS * M_DQK, M_HEADS * M_DV
H_HEADS, H_D = 8, 128
D_FF, N_EXPERTS = 2816, 8
D_GROUP = D_FF // 2
FT = D_GROUP // 128
CONV_K = 4
EPS = 1e-6
F_FLOOR = 1e-30
BIG = 1e30
A_HEADS, A_D, C_HEADS, C_D = 8, 64, 4, 128
N_RAW, N_HL = 3, 2
UNIT = 2048
LEVELS = 7
LN_SHIFT = 2.0 ** 50

V_NORM1, V_NORM2, V_C, V_CONVW, V_CONVB, V_MNORM, V_LB, V_HNORM, V_GMIX, V_GMEM, V_GFFN = \
    0, 16, 32, 40, 72, 80, 88, 96, 104, 112, 120
C_ID, C_CAUSAL, C_CAUSALT, C_COS, C_SIN, C_FOX, C_RANK, C_LEVEL = 0, 128, 256, 384, 400, 416, 434, 448
C_COLS = C_LEVEL + (LEVELS + 1) * 128

BRANCHES = ((0, A_HEADS, A_D, True, False), (A_HEADS, A_HEADS, A_D, True, True),
            (2 * A_HEADS, C_HEADS, C_D, False, False))
NORMED = ((0, 0, A_D), (1, A_D, A_D), (3, 2 * A_D, A_D), (4, 3 * A_D, A_D),
          (6, 4 * A_D, C_D), (None, 4 * A_D + C_D, C_D))

PAIR_HEADS = 2 + 2 + 2 + 4 + 1 + 1
PAIR_FFN = PAIR_HEADS + 2 * M_HEADS + 2 + 3 + 2 + 2
PAIR_LEVELS = PAIR_FFN + 16 + 4 + 2 + 4 + 4
PAIR_MOE = PAIR_LEVELS + 2 * LEVELS + 3 + 2 + 2 + 2 + 2 + 1
PAIR_ATT = PAIR_MOE + 8 * N_EXPERTS + 2 + 2 + 2 + 7 + 1 + 6
PAIR_FFN2 = PAIR_ATT + 12 + 12 + 8 + 12 + 2 + 2 + 2


def m_bank_s(h):
    return 2 * ((PAIR_HEADS + (2 * h - 1 if h else 0)) % 4)


def t_bank_s(gh):
    b = 0 if gh < A_HEADS else 1 if gh < 2 * A_HEADS else 2
    i = gh - BRANCHES[b][0]
    before = max(0, i - 2) if b == 2 else max(0, (i - 1) // 2)
    return 2 * ((PAIR_ATT + 12 * b + i + before) % 4)


def shape_constants():
    c = np.zeros((128, C_COLS), np.float32)
    c[:, C_ID:C_ID + 128] = np.eye(128)
    row, col = np.arange(128)[:, None], np.arange(128)[None, :]
    c[:, C_CAUSAL:C_CAUSAL + 128] = np.where(col > row, -BIG, 0.0)
    c[:, C_CAUSALT:C_CAUSALT + 128] = np.where(row > col, BIG, 0.0)
    rot = A_D // 4
    half = rot // 2
    inv = (1.0 / (np.float32(500000.0) ** (np.arange(half, dtype=np.float32) * np.float32(2.0) / np.float32(rot))))
    ang = np.arange(SEQ, dtype=np.float32)[:, None] * inv.astype(np.float32)[None, :]
    for i in range(TT):
        c[:, C_COS + half * i:C_COS + half * (i + 1)] = np.cos(ang[128 * i:128 * (i + 1)])
        c[:, C_SIN + half * i:C_SIN + half * (i + 1)] = np.sin(ang[128 * i:128 * (i + 1)])
    for h in range(A_HEADS):
        c[h, C_FOX] = -8.0
        c[32 + h, C_FOX + 1] = 1.0
        c[32 + h, C_FOX + 2 + h] = 8.0
        c[h, C_FOX + 10 + h] = 1.0
    c[:, C_RANK:C_RANK + 8] = 8 - np.arange(8)
    for lev in range(LEVELS):
        b = 64 >> lev
        ok = (row // (2 * b) == col // (2 * b)) & (row % (2 * b) < b) & (col % (2 * b) >= b)
        c[:, C_LEVEL + 128 * lev:C_LEVEL + 128 * (lev + 1)] = ok
    c[:, C_LEVEL + 128 * LEVELS:] = row == col
    return c


def build(nc, t, out):
    fp, fr, bf, i32 = mybir.dt.float32, mybir.dt.float32r, mybir.dt.bfloat16, mybir.dt.int32
    ALU, ACT, AX = mybir.AluOpType, mybir.ActivationFunctionType, mybir.AxisListType

    ctx = ExitStack()
    with ctx:
        ctx.enter_context(nc.allow_non_contiguous_dma(reason="small parameters"))

        def sb(name, shape, dt=fp):
            return ctx.enter_context(nc.sbuf_tensor(name, shape, dt))

        def sem(name):
            return ctx.enter_context(nc.semaphore(name))

        raw = sb("raw", [128, N_RAW, UNIT])
        whi = sb("whi", [128, N_HL, UNIT], fr)
        wlo = sb("wlo", [128, N_HL, UNIT], fr)
        X = sb("X", [128, TT, D])
        AF = sb("AF", [128, KT, SEQ])
        AH = sb("AH", [128, KT, SEQ], fr)
        AL = sb("AL", [128, KT, SEQ], fr)
        HH = sb("HH", [128, 12, SEQ], fr)
        HL = sb("HL", [128, 12, SEQ], fr)
        acc = sb("acc", [128, 3, UNIT])
        TS = sb("TS", [128, TT, D])
        GB = sb("GB", [128, 2, D])
        Z = sb("Z", [128, 10240])
        cst = sb("cst", [128, C_COLS])
        ones = sb("ones", [128, SEQ])
        identb = sb("identb", [128, 128], bf)
        maskb = sb("maskb", [128, 2, 128], bf)
        vec = sb("vec", [128, 128])
        adab = sb("adab", [128, 96])
        mod = sb("mod", [128, 4, KT])
        cond = sb("cond", [128, KT])
        wsm = sb("wsm", [128, KT, 64])
        gains = sb("gains", [128, 4 * A_D + 2 * C_D])
        col = sb("col", [128, 288])
        ident = cst[:, C_ID:C_ID + 128]
        ps = ctx.enter_context(nc.psum_tensor("ps", [128, 8, 512], fp))

        ss, rs = col[:, 0:16], col[:, 16:32]
        nmx, rsum = col[:, 32:40], col[:, 40:48]
        gcol = col[:, 48:64].rearrange("p (i h) -> p i h", i=TT)
        ecol = col[:, 64:80].rearrange("p (i h) -> p i h", i=TT)
        dcol = col[:, 80:96]
        gates = col[:, 96:112].rearrange("p (i e) -> p i e", i=TT)
        gcur = col[:, 112:114]
        bias8 = col[:, 114:118]
        lbc = col[:, 120:136]
        lgt = col[:, 136:152].rearrange("p (i e) -> p i e", i=TT)
        oh = col[:, 152:184].rearrange("p (w i e) -> p w i e", w=2, i=TT)
        lg2 = col[:, 184:200].rearrange("p (i e) -> p i e", i=TT)
        io8 = col[:, 200:208]
        mm2 = col[:, 208:224].rearrange("p (w i) -> p w i", w=8)
        scl = col[:, 224:232]
        ones2 = col[:, 232:234]
        ms, nt = col[:, 240:256], col[:, 256:272]

        raw_full = [sem(f"raw_full{i}") for i in range(N_RAW)]
        w_hi, w_lo = sem("w_hi"), sem("w_lo")
        w_used = sem("w_used")
        ada_used = sem("ada_used")
        ada_init, ada_sum = sem("ada_init"), sem("ada_sum")
        ps_free = sem("ps_free")
        silu_done, hid_done = sem("silu_done"), sem("hid_done")
        rows_in, small_in, cst_in, x_in, late_in = (sem("rows_in"), sem("small_in"), sem("cst_in"), sem("x_in"),
                                                    sem("late_in"))
        vec_step, act_step = sem("vec_step"), sem("act_step")
        cleared, ones_set, consts_set = sem("cleared"), sem("ones_set"), sem("consts_set")
        rows_t, vec_set, cond_set = sem("rows_t"), sem("vec_set"), sem("cond_set")
        x_ready = sem("x_ready")
        sq_done = sem("sq_done")
        ts_ready, tp_done, a_ready = sem("ts_ready"), sem("tp_done"), sem("a_ready")
        small_mm = sem("small_mm")
        g_vec, g_act = sem("g_vec"), sem("g_act")
        conv_done, og_set, ogs_set, qk_silu = sem("conv_done"), sem("og_set"), sem("ogs_set"), sem("qk_silu")
        col_tp, cols_set = sem("col_tp"), sem("cols_set")
        m_sc, m_exp, m_pt, m_o, heads_done = (sem("m_sc"), sem("m_exp"), sem("m_pt"), sem("m_o"), sem("heads_done"))
        h_raw, h_act, h_vec = sem("h_raw"), sem("h_act"), sem("h_vec")
        l_sub, l_exp, l_kq, l_mm = sem("l_sub"), sem("l_exp"), sem("l_kq"), sem("l_mm")
        h_o = sem("h_o")
        qk_raw, qk_ready, qk_set = sem("qk_raw"), sem("qk_ready"), sem("qk_set")
        fox_set = sem("fox_set")
        t_s, t_max, t_exp, t_p, t_tp, t_pt, t_o, t_y = (sem("t_s"), sem("t_max"), sem("t_exp"), sem("t_p"),
                                                        sem("t_tp"), sem("t_pt"), sem("t_o"), sem("t_y"))
        b_raw, b_sig = sem("b_raw"), sem("b_sig")
        root_in, root_out = sem("root_in"), sem("root_out")
        out_ready, out_done = sem("out_ready"), sem("out_done")

        def tok(ap):
            return ap.rearrange("p (i n) -> p i n", i=TT)

        qk = Z[:, 0:2048].rearrange("p (k t) -> p k t", k=KT)
        vx = Z[:, 2048:2048 + TT * M_HEADS * 129].rearrange("p (i h e) -> p i h e", i=TT, h=M_HEADS)
        og = tok(Z[:, 4352:6400])
        em = Z[:, 6400:7168].rearrange("p (b n) -> p b n", b=2)
        pt = Z[:, 7168:7936].rearrange("p (b n) -> p b n", b=2)
        rows = Z[0:8, 7936:7936 + 8 * SEQ].rearrange("p (r t) -> p r t", r=8)
        hv = tok(Z[:, 2048:4096])
        at = Z[:, 6400:8448].rearrange("p (g n) -> p g n", g=16)
        ax = Z[:, 8448:9472].rearrange("p (h n) -> p h n", h=H_HEADS)
        flatA = AF[:, :, :].rearrange("p k t -> p (k t)")
        flatT = TS[:, :, :].rearrange("p i n -> p (i n)")
        hq, hk, hb = acc[:, 0, :], acc[:, 1, :], acc[:, 2, :]
        level_buf = [flatA, flatT, Z[:, 0:2048]]
        Y = tok(Z[:, 0:2048])
        sil = Z[:, 2048:3072].rearrange("p (b n) -> p b n", b=2)
        hid = Z[:, 3072:4096].rearrange("p (b n) -> p b n", b=2)
        fwb = Z[:, 4096:5120]
        qkv = Z[:, 0:7168].rearrange("p (j i n) -> p j i n", j=7, i=TT)
        mkv = Z[:, 7168:9216].rearrange("p (j i n) -> p j i n", j=2, i=TT)
        prb = Z[:, 9216:10240].rearrange("p (b n) -> p b n", b=2)
        pts = GB[:, 0, :].rearrange("p (b n) -> p b n", b=2)
        memx = tok(acc[:, 0, :])
        sg = tok(Z[:, 0:2048])
        fox_l = AF[:, :, :]
        fox_r = GB[:, 1, 0:SEQ]
        fcum = TS[:, 1, 768:1024]
        frow = TS[0:40, 1, :].rearrange("p (r t) -> p r t", r=4)

        def wview(w):
            return w.rearrange("(k p) n -> p k n", p=128)

        ada_w = [t["ada_w"][l].rearrange("(k p) n -> k p n", p=128) for l in range(2)]
        m_in, m_out = wview(t["m_w_in"][0]), wview(t["m_w_out"][0])
        h_in, h_out = wview(t["h_w_in"][0]), wview(t["h_w_out"][0])
        w_in2, w_mkv, w_out2 = wview(t["w_in_2"][0]), wview(t["w_mem_kv_2"][0]), wview(t["w_out_2"][0])
        w_br = [wview(t[n][0]) for n in ("w_br_moba_2", "w_br_fox_2", "w_br_mem_2")]
        M_GATES = 2 * M_QK + 2 * M_V
        F_LOGIT = 6 * 512
        Q_MEM = F_LOGIT + A_HEADS
        A_COL = Q_MEM + 512

        class Walk:

            def __init__(self):
                self.slot, self.uses = 0, [0] * N_RAW
                self.unit, self.hl = 0, 0
                self.pair, self.pb = 0, 0
                self.ada = self.hidden = 0
                self.freed = []

            def next_raw(self):
                s = self.slot
                self.slot = (s + 1) % N_RAW
                self.uses[s] = self.uses[s] + 1
                return s, self.uses[s] * 16

            def next_unit(self):
                u, h = self.unit, self.hl
                self.unit, self.hl = u + 1, (h + 1) % N_HL
                return u, h

            def next_pair(self):
                p, b = self.pair, self.pb
                self.pair, self.pb = p + 1, (b + 1) % 4
                return p, 2 * b

            def after_groups(self, n):
                w = Walk()
                w.slot, w.hl, w.pb, w.ada = self.slot, self.hl, self.pb, self.ada
                w.uses = [c + n * (18 // N_RAW) for c in self.uses]
                w.unit, w.pair = self.unit + n * 18, self.pair + n * 8
                w.hidden = self.hidden + n * 6
                w.freed = [(w_lo, w.unit - 2), (w_lo, w.unit - 1), (w_lo, w.unit)]
                return w

        COLS = [(256 * c, min(256, D_GROUP - 256 * c)) for c in range(6)]
        KS = [(4 * g, min(4, FT - 4 * g)) for g in range(3)]
        JOBS = [KT * COLS[j // 2][1] for j in range(12)] + [512 * KS[j % 3][1] for j in range(6)]

        def at_least(eng, s, v):
            if not isinstance(v, int) or v > 0:
                eng.wait_ge(s, v)

        block = ctx.enter_context(nc.Block())

        @block.sync
        def _(sp):
            w = Walk()

            def load(w, src, n, view):
                if len(w.freed) >= N_RAW:
                    s, v = w.freed[-N_RAW]
                    sp.wait_ge(s, v)
                slot, _ = w.next_raw()
                sp.dma_start(view(raw[:, slot, 0:n]), src).then_inc(raw_full[slot], 16)

            def t_unit(w, wm, c0, n):
                load(w, wm[:, 0:KT, c0:c0 + n], KT * n, lambda r: r.rearrange("p (k n) -> p k n", k=KT))
                u, _ = w.next_unit()
                w.freed.append((w_lo, u + 1))

            def m_unit(w, wm, k0, nk, c0):
                load(w, wm[:, k0:k0 + nk, c0:c0 + 512], nk * 512, lambda r: r.rearrange("p (k n) -> p k n", k=nk))
                u, _ = w.next_unit()
                w.freed.append((w_lo, u + 1))

            def ada_unit(w, layer, chunk, k):
                load(w, ada_w[layer][k, :, chunk * UNIT:(chunk + 1) * UNIT], UNIT, lambda r: r)
                w.ada += 1
                w.freed.append((ada_used, w.ada))

            def m_matrix(w, wm, c0, chunks, kts=KT):
                for c in range(chunks):
                    for k0 in range(0, kts, 4):
                        m_unit(w, wm, k0, 4, c0 + 512 * c)

            def group(w, wg, wu, wd, side=lambda j: None):
                for c, (c0, n) in enumerate(COLS):
                    t_unit(w, wg, c0, n)
                    side(2 * c)
                    t_unit(w, wu, c0, n)
                    side(2 * c + 1)
                for c in range(2):
                    for k0, nk in KS:
                        m_unit(w, wd, k0, nk, 512 * c)

            def half(w, names, e, side=lambda j: None):
                g, u, d = (t[n][0] for n in names)
                cut = slice(e * D_GROUP, (e + 1) * D_GROUP) if isinstance(e, int) else bass.ds(e * D_GROUP, D_GROUP)
                group(w, wview(g[:, cut]), wview(u[:, cut]), wview(d[cut, :]), side)

            for k in range(KT):
                ada_unit(w, 0, 0, k)
            for c in range(4):
                t_unit(w, m_in, 256 * c, 256)
            m_matrix(w, m_in, 2 * M_QK, 4)
            for chunk in (1, 2):
                for k in range(KT):
                    ada_unit(w, 0, chunk, k)
            m_matrix(w, m_out, 0, 2)
            for e in range(2):
                half(w, ("ffn_w_gate", "ffn_w_up", "ffn_w_down"), e,
                     lambda j: ada_unit(w, 1, (12 * e + j) // 8, (12 * e + j) % 8))
            for c in range(8):
                t_unit(w, h_in, 256 * c, 256)
            m_matrix(w, h_in, 2 * D, 4)
            m_matrix(w, h_out, 0, 2)
            with sp.Fori(0, N_EXPERTS) as e:
                group(w.after_groups(e), *(wview(t[n][0][bass.ds(e, 1)].rearrange("o k n -> (o k) n"))
                                           for n in ("moe_w_gate", "moe_w_up", "moe_w_down")))
            w = w.after_groups(N_EXPERTS)
            m_matrix(w, w_mkv, 0, 2)
            m_matrix(w, w_in2, 0, 6)
            m_matrix(w, w_in2, Q_MEM, 1)
            for b in range(3):
                m_matrix(w, w_in2, A_COL + D * b, 2)
                m_matrix(w, w_br[b], 0, 2, 4)
            m_matrix(w, w_out2, 0, 2)
            with sp.Fori(0, 2) as e:
                half(w.after_groups(e), ("w_gate_2", "w_up_2", "w_down_2"), e)
            sp.wait_ge(out_ready, 1)
            sp.dma_start(out[0].rearrange("(i p) n -> p i n", p=128), X[:, :, :]).then_inc(out_done, 16)
            sp.wait_ge(out_done, 16)

        @block.gpsimd
        def _(pool):
            pool.memset(ones[:, :], 1.0).then_inc(ones_set, 1)

        @block.scalar
        def _(act):
            steps = [0]

            def link(ins):
                steps[0] += 1
                ins.then_inc(act_step, 1)
                act.wait_ge(act_step, steps[0])

            act.dma_start(cst[:, :], t["shape_consts"]).then_inc(cst_in, 16)
            for name, r0, n in (("norm1_w", V_NORM1, 16), ("norm2_w", V_NORM2, 16), ("c", V_C, 8),
                                ("m_conv_w", V_CONVW, 32), ("m_conv_b", V_CONVB, 8), ("m_norm_w", V_MNORM, 8),
                                ("h_lb_logits", V_LB, 8), ("h_norm_w", V_HNORM, 8), ("g_mix_2", V_GMIX, 8),
                                ("g_mem_2", V_GMEM, 8), ("g_ffn_2", V_GFFN, 8)):
                flat = "a b c -> (a b c)" if len(t[name].shape) == 3 else "a b -> (a b)"
                act.dma_start(TS[r0:r0 + n, 1, 0:128],
                              t[name].rearrange(flat).rearrange("(r p) -> r p", p=128)).then_inc(rows_in, 16)
            act.dma_start(TS[0:96, 1, 128:256],
                          t["ada_b"].rearrange("l n -> (l n)").rearrange("(r p) -> r p", p=128)).then_inc(rows_in, 16)
            act.dma_start(X[:, :, :], t["x"][0].rearrange("(i p) n -> p i n", p=128)).then_inc(x_in, 16)
            act.wait_ge(cleared, 2)
            act.dma_start(bias8[0:8, 0:1], t["m_i_bias"].rearrange("o h -> h o")).then_inc(small_in, 16)
            act.dma_start(bias8[0:8, 1:2], t["m_f_bias"].rearrange("o h -> h o")).then_inc(small_in, 16)
            act.dma_start(bias8[0:8, 3:4], t["b_forget_2"].rearrange("o h -> h o")).then_inc(small_in, 16)
            act.dma_start(bias8[32:40, 3:4], t["b_forget_2"].rearrange("o h -> h o")).then_inc(small_in, 16)
            act.dma_start(wsm[:, :, 0:16], m_in[:, :, M_GATES:M_GATES + 16]).then_inc(small_in, 16)
            act.dma_start(wsm[:, :, 16:24], wview(t["moe_router"][0])).then_inc(small_in, 16)
            act.dma_start(wsm[:, :, 24:32], w_in2[:, :, F_LOGIT:F_LOGIT + 8]).then_inc(small_in, 16)
            act.dma_start(wsm[:, :, 56:64], w_in2[:, :, F_LOGIT:F_LOGIT + 8]).then_inc(small_in, 16)
            for j, name in enumerate(("g_q_moba_2", "g_k_moba_2", "g_q_fox_2", "g_k_fox_2")):
                act.dma_start(gains[:, A_D * j:A_D * (j + 1)], t[name].to_broadcast([128, A_D])).then_inc(small_in, 16)
            for j, name in enumerate(("g_q_mem_2", "g_k_mem_2")):
                act.dma_start(gains[:, 4 * A_D + C_D * j:4 * A_D + C_D * (j + 1)],
                              t[name].to_broadcast([128, C_D])).then_inc(small_in, 16)

            def hi(w, n=UNIT):
                s, full = w.next_raw()
                u, h = w.next_unit()
                act.wait_ge(raw_full[s], full)
                at_least(act, w_used, u - N_HL + 1)
                act.activation(whi[:, h, 0:n], raw[:, s, 0:n], ACT.Copy).then_inc(w_hi, 1)

            def his(w, k):
                for _ in range(k):
                    hi(w)

            def skip_raw(w, n):
                for _ in range(n):
                    w.next_raw()

            roots = [0]

            def root(n):
                roots[0] += 1
                act.wait_ge(root_in, roots[0])
                act.activation(rs[:, 0:n], rs[:, 0:n], ACT.Sqrt).then_inc(root_out, 1)

            def squares(src):
                for i in range(TT):
                    act.activation(AF[:, 4 * i:4 * i + 4, :].rearrange("p k t -> p (k t)"), src[:, i, :], ACT.Square,
                                   accum_out=ss[:, i:i + 1]).then_inc(sq_done, 1)
                root(2)

            def group(w, side=lambda j: None):
                first_unit, first_pb, done = w.unit, w.pb, w.hidden

                def silu(c):
                    act.wait_ge(w_used, first_unit + 2 * c + 2)
                    at_least(act, hid_done, done + c - 1)
                    n, bank = 2 * COLS[c][1], 2 * ((first_pb + c) % 4)
                    act.activation(sil[:, c % 2, 0:n], ps[:, bank, 0:n], ACT.Silu).then_inc(silu_done, 1)

                for j in range(18):
                    hi(w, JOBS[j])
                    if j < 12:
                        side(j)
                    if 3 <= j <= 13 and j % 2:
                        silu((j - 3) // 2)
                w.hidden = done + 6
                for _ in range(8):
                    w.next_pair()

            w = Walk()
            act.wait_ge(vec_set, 1)
            act.activation(cond[:, :], vec[:, V_C:V_C + 8], ACT.Silu).then_inc(cond_set, 1)
            act.wait_ge(x_in, 16)
            squares(X)
            skip_raw(w, 8)
            his(w, 12)
            act.wait_ge(conv_done, 1)
            act.activation(qk, qk, ACT.Silu).then_inc(qk_silu, 1)
            act.wait_ge(og_set, 1)
            act.activation(og, og, ACT.Sigmoid).then_inc(ogs_set, 1)
            act.wait_ge(g_vec, 1)
            act.activation(rows[:, 0, :], rows[:, 0, :], ACT.Tanh, bias=bias8[0:8, 2:3], scale=1.0 / 15.0)
            link(act.activation(rows[:, 3, :], rows[:, 2, :], ACT.Exp, scale=-1.0))
            act.activation(rows[:, 3, :], rows[:, 3, :], ACT.Ln, bias=1.0).then_inc(g_act, 1)
            act.wait_ge(g_vec, 2)
            act.activation(rows[:, 7, :], rows[:, 7, :], ACT.Exp, scale=-1.0).then_inc(g_act, 1)
            act.wait_ge(cols_set, 1)
            skip_raw(w, 16)
            for h in range(M_HEADS):
                act.wait_ge(m_sc, h + 1)
                at_least(act, m_pt, h - 1)
                bank = m_bank_s(h)
                act.activation(em[:, h % 2, 0:256], ps[:, bank, 0:256], ACT.Exp, bias=gcol[:, 0, h:h + 1], scale=-1.0)
                act.activation(em[:, h % 2, 256:384], ps[:, bank, 256:384], ACT.Exp, bias=gcol[:, 1, h:h + 1],
                               scale=-1.0).then_inc(m_exp, 1)
            act.wait_ge(heads_done, 1)
            act.activation(flatA, flatT, ACT.Square).then_inc(sq_done, 1)
            root(16)
            his(w, 4)
            act.wait_ge(x_ready, 1)
            squares(X)
            w.pair, w.pb = PAIR_FFN, PAIR_FFN % 4
            for e in range(2):
                group(w, lambda j: skip_raw(w, 1))
            act.wait_ge(x_ready, 2)
            squares(X)
            his(w, 6)
            act.wait_ge(h_raw, 1)
            act.activation(hq, hq, ACT.Silu)
            his(w, 4)
            act.wait_ge(h_raw, 2)
            act.activation(flatA, hk, ACT.Sigmoid).then_inc(h_act, 1)
            act.activation(hk, hk, ACT.Sigmoid, scale=-1.0).then_inc(h_act, 1)
            his(w, 6)
            act.wait_ge(h_vec, 1)
            act.activation(lbc[:, 0:8], lbc[:, 0:8], ACT.Exp).then_inc(h_act, 1)
            act.wait_ge(h_vec, 2)
            act.activation(flatT, flatA, ACT.Ln)
            act.activation(level_buf[2], flatA, ACT.Ln, scale=LN_SHIFT).then_inc(h_act, 1)
            act.wait_ge(og_set, 2)
            act.activation(og, og, ACT.Silu).then_inc(ogs_set, 1)
            for lev in range(LEVELS + 1):
                act.wait_ge(l_sub, lev + 1)
                act.activation(level_buf[lev % 3], level_buf[lev % 3], ACT.Exp).then_inc(l_exp, 1)
            act.wait_ge(heads_done, 2)
            act.activation(flatA, flatT, ACT.Square).then_inc(sq_done, 1)
            root(16)
            his(w, 4)
            act.wait_ge(x_ready, 3)
            squares(X)
            act.dma_start(memx, t["mem_2"][0].rearrange("(i p) n -> p i n", p=128)).then_inc(late_in, 16)
            act.dma_start(fwb, t["final_norm_w"].rearrange("(o n) -> o n", o=1).to_broadcast([128, D])).then_inc(late_in, 16)
            act.wait_ge(g_vec, 3)
            act.activation(mm2[:, 3, :], mm2[:, 2, :], ACT.Exp).then_inc(g_act, 1)
            w.pair, w.pb = PAIR_MOE, PAIR_MOE % 4
            with act.Fori(0, N_EXPERTS) as e:
                group(w.after_groups(e))
            w = w.after_groups(N_EXPERTS)
            act.wait_ge(x_ready, 4)
            squares(X)
            act.wait_ge(late_in, 32)
            act.wait_ge(ts_ready, 7)
            squares(memx)
            his(w, 4)
            act.wait_ge(x_ready, 5)
            act.wait_ge(a_ready, 2 * 7)
            squares(X)
            his(w, 14)
            act.wait_ge(g_vec, 4)
            link(act.activation(frow[:, 2, :], frow[:, 1, :], ACT.Exp, scale=-1.0))
            act.activation(frow[:, 2, :], frow[:, 2, :], ACT.Ln, bias=1.0).then_inc(g_act, 1)
            act.wait_ge(qk_raw, 1)
            for n in range(len(NORMED) + 1):
                if n < len(NORMED):
                    at_least(act, qk_ready, n - 1)
                    src = mkv[:, 0] if NORMED[n][0] is None else qkv[:, NORMED[n][0]]
                    act.activation(tok(flatA[:, 1024 * (n % 2):1024 * (n % 2) + 1024]), src, ACT.Square)\
                       .then_inc(sq_done, 1)
                if n:
                    root(2 * (512 // NORMED[n - 1][2]))
            for gh0, heads, dh, causal, fox in BRANCHES:
                for i in range(heads):
                    gh = gh0 + i
                    act.wait_ge(t_max, gh + 1)
                    at_least(act, t_tp, gh - 1)
                    bank = t_bank_s(gh)
                    n0 = 128 if causal else 256
                    for k, (c0, n) in enumerate(((0, n0), (n0, 256))):
                        ins = act.activation(prb[:, gh % 2, c0:c0 + n], ps[:, bank, c0:c0 + n], ACT.Exp,
                                             bias=nmx[:, 2 * (gh % 2) + k:2 * (gh % 2) + k + 1], scale=dh ** -0.5,
                                             accum_out=rsum[:, 2 * (gh % 2) + k:2 * (gh % 2) + k + 1])
                    ins.then_inc(t_exp, 1)
            for b in range(3):
                his(w, 4)
                act.wait_ge(b_raw, b + 1)
                act.activation(sg, sg, ACT.Sigmoid).then_inc(b_sig, 1)
                his(w, 2)
            his(w, 4)
            act.wait_ge(x_ready, 6)
            squares(X)
            w.pair, w.pb = PAIR_FFN2, PAIR_FFN2 % 4
            with act.Fori(0, 2) as e:
                group(w.after_groups(e))

        @block.tensor
        def _(pe):
            w = Walk()
            stage = [0]

            def pair(w):
                p, bank = w.next_pair()
                at_least(pe, ps_free, p - 3)
                return bank

            def three(o, sh, sl, mh, ml, first, last):
                pe.matmul(o, sh, mh, start=first, stop=False)
                pe.matmul(o, sh, ml, start=False, stop=False)
                return pe.matmul(o, sl, mh, start=False, stop=last)

            def t_unit(w, bank, n=256):
                u, h = w.next_unit()
                pe.wait_ge(w_lo, u + 1)
                wh = whi[:, h, 0:KT * n].rearrange("p (k n) -> p k n", k=KT)
                wl = wlo[:, h, 0:KT * n].rearrange("p (k n) -> p k n", k=KT)
                for f in range(n // 128):
                    for k in range(KT):
                        ins = three(ps[:, bank, SEQ * f:SEQ * (f + 1)], wh[:, k, 128 * f:128 * (f + 1)],
                                    wl[:, k, 128 * f:128 * (f + 1)], AH[:, k, :], AL[:, k, :], k == 0, k == KT - 1)
                ins.then_inc(w_used, 1)

            def m_unit(w, bank, k0, nk, kts, sh=AH, sl=AL, s0=0):
                u, h = w.next_unit()
                pe.wait_ge(w_lo, u + 1)
                wh = whi[:, h, 0:nk * 512].rearrange("p (k n) -> p k n", k=nk)
                wl = wlo[:, h, 0:nk * 512].rearrange("p (k n) -> p k n", k=nk)
                for i in range(TT):
                    for k in range(nk):
                        kk = k0 + k
                        ins = three(ps[:, bank + i, :], sh[:, s0 + kk, 128 * i:128 * (i + 1)],
                                    sl[:, s0 + kk, 128 * i:128 * (i + 1)], wh[:, k, :], wl[:, k, :],
                                    kk == 0, kk == kts - 1)
                ins.then_inc(w_used, 1)

            def m_matrix(w, chunks, kts=KT, sh=AH, sl=AL, s0=0):
                for _ in range(chunks):
                    bank = pair(w)
                    for k0 in range(0, kts, 4):
                        m_unit(w, bank, k0, 4, kts, sh, sl, s0)

            def transposes(w):
                stage[0] += 1
                pe.wait_ge(ts_ready, stage[0])
                for q in range(2):
                    bank = pair(w)
                    for k in range(4):
                        for i in range(TT):
                            ins = pe.transpose(ps[:, bank + k // 2, SEQ * (k % 2) + 128 * i:SEQ * (k % 2) + 128 * (i + 1)],
                                               TS[:, i, 512 * q + 128 * k:512 * q + 128 * (k + 1)], ident)
                    ins.then_inc(tp_done, 1)

            def a_wait():
                pe.wait_ge(a_ready, 2 * stage[0])

            def ada_cols(bank, c0, chunk, n0, n):
                for f in range(n):
                    ins = pe.matmul(ps[:, bank, c0 + f:c0 + f + 1], acc[:, chunk, n0 + 128 * f:n0 + 128 * (f + 1)],
                                    ones[:, 0:1], start=True, stop=True)
                return ins

            def ada_rows(bank, chunk, n0):
                for c in range(2):
                    ins = pe.matmul(ps[:, bank + c, :], ones[:, 0:128], acc[:, chunk, n0 + 512 * c:n0 + 512 * (c + 1)],
                                    start=True, stop=True)
                return ins

            def ada_gates(w):
                bank = pair(w)
                ada_rows(bank, 1, 0).then_inc(ada_sum, 1)
                bank = pair(w)
                ada_cols(bank, 0, 1, 1024, 8)
                ada_cols(bank, 8, 2, 0, 8).then_inc(ada_sum, 1)
                bank = pair(w)
                ada_rows(bank, 2, 1024).then_inc(ada_sum, 1)

            def group(w):
                done = w.hidden
                for c, (_, n) in enumerate(COLS):
                    bank = pair(w)
                    t_unit(w, bank, n)
                    t_unit(w, bank + 1, n)
                for c in range(2):
                    bank = pair(w)
                    for k0, nk in KS:
                        if c == 0:
                            pe.wait_ge(hid_done, done + min(6, (k0 + nk + 1) // 2))
                        m_unit(w, bank, k0, nk, FT, HH, HL)
                w.hidden = done + 6

            pe.wait_ge(cst_in, 16)
            pe.wait_ge(rows_in, 12 * 16)
            bank = pair(w)
            pe.transpose(ps[:, bank, 0:128], TS[:, 1, 0:128], ident)
            pe.transpose(ps[:, bank + 1, 0:96], TS[0:96, 1, 128:256], cst[0:96, C_ID:C_ID + 96]).then_inc(rows_t, 1)
            pe.wait_ge(ones_set, 1)
            pe.wait_ge(ada_used, 8)
            bank = pair(w)
            ada_cols(bank, 0, 0, 0, 16).then_inc(ada_sum, 1)
            transposes(w)
            a_wait()
            for _ in range(2):
                bank = pair(w)
                t_unit(w, bank)
                t_unit(w, bank + 1)
            m_matrix(w, 4)
            pe.wait_ge(small_in, 14 * 16)
            bank = pair(w)
            for g in range(2):
                for k in range(KT):
                    ins = pe.matmul(ps[0:8, bank + g, 0:SEQ], wsm[:, k, 8 * g:8 * g + 8], AF[:, k, :],
                                    start=k == 0, stop=k == KT - 1)
            ins.then_inc(small_mm, 1)
            pe.wait_ge(g_act, 2)
            bank = pair(w)
            for r, row in ((0, 5), (1, 7)):
                for i in range(TT):
                    ins = pe.transpose(ps[:, bank, 16 * r + 8 * i:16 * r + 8 * i + 8], rows[:, row, 128 * i:128 * (i + 1)],
                                       cst[0:8, C_ID:C_ID + 8])
            ins.then_inc(col_tp, 1)
            pe.wait_ge(consts_set, 1)
            pe.wait_ge(qk_silu, 1)
            pe.wait_ge(ps_free, w.pair)
            for step in range(M_HEADS + 1):
                if step < M_HEADS:
                    h = step
                    bank = pair(w)
                    assert bank == m_bank_s(h)
                    ro, kt = 64 * (h % 2), h // 2
                    pick = cst[0:8, C_ID + h:C_ID + h + 1].to_broadcast([8, 128])
                    M = rows[:, 6, :]
                    pe.matmul(ps[:, bank, 0:256], pick, M, start=True, stop=False)
                    pe.matmul(ps[:, bank, 0:128], identb[:, :], maskb[:, 1, :], start=False, stop=True)
                    pe.matmul(ps[:, bank, 256:384], pick, M[:, 128:256], start=True, stop=False)
                    pe.matmul(ps[:, bank, 256:384], identb[:, :], maskb[:, 1, :], start=False, stop=True)
                    q, k = qk[ro:ro + 64, kt, :], qk[ro:ro + 64, 4 + kt, :]
                    pe.matmul(ps[:, bank + 1, 0:256], k[:, 0:128], q, start=True, stop=True)
                    pe.matmul(ps[:, bank + 1, 256:384], k[:, 128:256], q[:, 128:256], start=True, stop=True)\
                      .then_inc(m_sc, 1)
                if step >= 1:
                    h = step - 1
                    bank = pair(w)
                    pe.wait_ge(m_pt, h + 1)
                    p = pt[:, h % 2, :]
                    pe.matmul(ps[:, bank, 0:129], p[:, 0:128], vx[:, 0, h, :], start=True, stop=True)
                    pe.matmul(ps[:, bank, 256:385], p[:, 128:256], vx[:, 0, h, :], start=True, stop=False)
                    pe.matmul(ps[:, bank, 256:385], p[:, 256:384], vx[:, 1, h, :], start=False, stop=True)\
                      .then_inc(m_o, 1)
            transposes(w)
            pe.wait_ge(ada_used, 24)
            ada_gates(w)
            a_wait()
            m_matrix(w, 2)
            transposes(w)
            a_wait()
            assert w.pair == PAIR_FFN
            for e in range(2):
                group(w)
            pe.wait_ge(ada_used, 48)
            bank = pair(w)
            ada_cols(bank, 0, 0, 0, 16).then_inc(ada_sum, 1)
            ada_gates(w)
            transposes(w)
            a_wait()
            for _ in range(4):
                bank = pair(w)
                t_unit(w, bank)
                t_unit(w, bank + 1)
            m_matrix(w, 4)
            for lev in range(-1, LEVELS + 1):
                n = lev + 1
                if lev < LEVELS:
                    pe.wait_ge(l_kq, n + 1)
                    lhs = rhs = level_buf[n % 3].rearrange("p (g t) -> p g t", g=16)
                else:
                    lhs, rhs = (a.rearrange("p (g t) -> p g t", g=16) for a in (hk, hq))
                for half_ in range(1 if lev < 0 else 2):
                    bank = pair(w)
                    for g in range(8):
                        if lev < 0:
                            l_ap, r_ap = lhs[:, 2 * g, :], rhs[:, 2 * g + 1, :]
                        else:
                            l_ap, r_ap = lhs[:, 8 * half_ + g, :], rhs[:, 8 * half_ + g, :]
                        ins = pe.matmul(ps[:, bank + g // 4, 128 * (g % 4):128 * (g % 4) + 128], l_ap, r_ap,
                                        start=True, stop=True)
                    ins.then_inc(l_mm, 1)
            for i in range(TT):
                bank = pair(w)
                if i == 0:
                    pe.wait_ge(ps_free, w.pair - 1)
                for h in range(H_HEADS):
                    o = ps[:, bank + h // 4, 128 * (h % 4):128 * (h % 4) + 128]
                    ins = pe.matmul(o, at[:, 2 * h + i, :], hv[:, i, 128 * h:128 * h + 128], start=True, stop=i == 0)
                    if i:
                        ins = pe.matmul(o, ax[:, h, :], hv[:, 0, 128 * h:128 * h + 128], start=False, stop=True)
                ins.then_inc(h_o, 1)
            transposes(w)
            a_wait()
            m_matrix(w, 2)
            transposes(w)
            a_wait()
            bank = pair(w)
            for i in range(TT):
                for k in range(KT):
                    ins = pe.matmul(ps[:, bank, 8 * i:8 * i + 8], AF[:, k, 128 * i:128 * (i + 1)], wsm[:, k, 16:24],
                                    start=k == 0, stop=k == KT - 1)
            ins.then_inc(small_mm, 1)
            assert w.pair == PAIR_MOE
            with pe.Fori(0, N_EXPERTS) as e:
                group(w.after_groups(e))
            w = w.after_groups(N_EXPERTS)
            stage[0] += 1
            transposes(w)
            a_wait_n = 2 * 7
            pe.wait_ge(a_ready, a_wait_n)
            m_matrix(w, 2)
            transposes(w)
            pe.wait_ge(a_ready, a_wait_n + 2)
            m_matrix(w, 7)
            bank = pair(w)
            for k in range(KT):
                ins = pe.matmul(ps[0:40, bank, 0:SEQ], wsm[:, k, 24:64], AF[:, k, :], start=k == 0, stop=k == KT - 1)
            ins.then_inc(small_mm, 1)
            for b in range(3):
                for which in range(2):
                    src = mkv[:, 0] if (b, which) == (2, 1) else qkv[:, (0, 3, 6)[b] + which]
                    pe.wait_ge(qk_ready, 2 * b + which + 1)
                    bank = pair(w)
                    for k in range(4):
                        for i in range(TT):
                            ins = pe.transpose(ps[:, bank + k // 2, SEQ * (k % 2) + 128 * i:SEQ * (k % 2) + 128 * (i + 1)],
                                               src[:, i, 128 * k:128 * (k + 1)], ident)
                    ins.then_inc(tp_done, 1)
            pe.wait_ge(qk_set, 6)
            pe.wait_ge(fox_set, 1)
            for b, (gh0, heads, dh, causal, fox) in enumerate(BRANCHES):
                per = 128 // dh
                qT = acc[:, b, 0:1024].rearrange("p (k t) -> p k t", k=4)
                kT = acc[:, b, 1024:2048].rearrange("p (k t) -> p k t", k=4)
                s_bank = {}
                o_bank = {}
                n0 = 128 if causal else 256
                for step in range(heads + 2):
                    if step < heads:
                        h = step
                        s_bank[h] = bank = pair(w)
                        assert bank == t_bank_s(gh0 + h)
                        ro, kt = dh * (h % per), h // per
                        q, k = qT[ro:ro + dh, kt, :], kT[ro:ro + dh, kt, :]
                        for i, (c0, n) in enumerate(((0, n0), (n0, 256))):
                            o = ps[:, bank, c0:c0 + n]
                            ins = pe.matmul(o, q[:, 128 * i:128 * (i + 1)], k[:, 0:n], start=True, stop=not causal)
                            if fox:
                                pe.matmul(o, fox_l[:, h, 128 * i:128 * (i + 1)], fox_r[:, 0:n], start=False, stop=False)
                            if causal:
                                ins = pe.matmul(ps[:, bank, c0 + n - 128:c0 + n], identb[:, :], maskb[:, 0, :],
                                                start=False, stop=True)
                        ins.then_inc(t_s, 1)
                    if 1 <= step <= heads:
                        h = step - 1
                        bank = s_bank[h] + 1
                        pe.wait_ge(t_p, gh0 + h + 1)
                        p = prb[:, (gh0 + h) % 2, :]
                        cuts = ((0, 0), (128, 128), (256, 256)) if causal else ((0, 0), (256, 128), (128, 256), (384, 384))
                        for c_in, c_out in cuts:
                            ins = pe.transpose(ps[:, bank, c_out:c_out + 128], p[:, c_in:c_in + 128], ident)
                        ins.then_inc(t_tp, 1)
                    if step >= 2:
                        h = step - 2
                        ro, kt = dh * (h % per), h // per
                        if kt not in o_bank:
                            o_bank[kt] = pair(w)
                        bank = o_bank[kt]
                        pe.wait_ge(t_pt, gh0 + h + 1)
                        p = pts[:, (gh0 + h) % 2, :]
                        v = mkv[:, 1] if b == 2 else qkv[:, 3 * b + 2]
                        q0 = 128 if causal else 0
                        pe.matmul(ps[ro:ro + dh, bank, 0:256], v[:, 0, dh * h:dh * (h + 1)], p[:, 0:256],
                                  start=True, stop=False)
                        pe.matmul(ps[ro:ro + dh, bank, q0:256], v[:, 1, dh * h:dh * (h + 1)], p[:, 256:512 - q0],
                                  start=False, stop=True).then_inc(t_o, 1)
            pe.wait_ge(t_y, 12)
            for b in range(3):
                m_matrix(w, 2)
                m_matrix(w, 2, 4, HH, HL, 4 * b)
            pe.wait_ge(ts_ready, 10)
            for q in range(2):
                bank = pair(w)
                for k in range(4):
                    for i in range(TT):
                        ins = pe.transpose(ps[:, bank + k // 2, SEQ * (k % 2) + 128 * i:SEQ * (k % 2) + 128 * (i + 1)],
                                           TS[:, i, 512 * q + 128 * k:512 * q + 128 * (k + 1)], ident)
                ins.then_inc(tp_done, 1)
            pe.wait_ge(a_ready, 18)
            m_matrix(w, 2)
            stage[0] = 10
            transposes(w)
            pe.wait_ge(a_ready, 20)
            assert w.pair == PAIR_FFN2 and w.pb == PAIR_FFN2 % 4
            with pe.Fori(0, 2) as e:
                group(w.after_groups(e))

        @block.vector
        def _(dve):
            steps = [0]

            def link(ins):
                steps[0] = steps[0] + 1
                ins.then_inc(vec_step, 1)
                dve.wait_ge(vec_step, steps[0])

            def both(ins, s, n):
                ins.then_inc(s, 1)
                dve.wait_ge(s, n)

            def free(w, ins):
                w.next_pair()
                ins.then_inc(ps_free, 1)
                dve.wait_ge(ps_free, w.pair)

            def bank_of(w):
                return 2 * w.pb

            def lo(w, n=UNIT):
                s, _ = w.next_raw()
                u, h = w.next_unit()
                dve.wait_ge(w_hi, u + 1)
                dve.tensor_tensor(wlo[:, h, 0:n], raw[:, s, 0:n], whi[:, h, 0:n].bitcast(fp), ALU.subtract)\
                   .then_inc(w_lo, 1)

            def los(w, k):
                for _ in range(k):
                    lo(w)

            def ada_unit(w, layer, chunk, k):
                if k == 0:
                    dve.tensor_tensor(acc[:, chunk, :].rearrange("p (f n) -> p f n", f=16),
                                      ident.rearrange("p (o n) -> p o n", o=1).to_broadcast([128, 16, 128]),
                                      adab[:, 48 * layer + 16 * chunk:48 * layer + 16 * chunk + 16]
                                      .rearrange("p (f o) -> p f o", o=1).to_broadcast([128, 16, 128]),
                                      ALU.mult).then_inc(ada_init, 1)
                    dve.wait_ge(ada_init, 3 * layer + chunk + 1)
                s, full = w.next_raw()
                at_least(dve, ada_used, w.ada)
                dve.wait_ge(raw_full[s], full)
                dve.scalar_tensor_tensor(acc[:, chunk, :], raw[:, s, :], cond[:, k:k + 1], acc[:, chunk, :],
                                         ALU.mult, ALU.add).then_inc(ada_used, 1)
                w.ada += 1

            def root(n, width):
                m, y, s = ms[:, 0:n], rs[:, 0:n], nt[:, 0:n]
                link(dve.tensor_scalar(m, ss[:, 0:n], 1.0 / width, EPS, ALU.mult, ALU.add))
                dve.reciprocal(y, m).then_inc(root_in, 1)
                counts["root"] += 1
                dve.wait_ge(root_out, counts["root"])
                link(dve.tensor_tensor(s, y, y, ALU.mult))
                link(dve.tensor_tensor(s, s, m, ALU.mult))
                link(dve.tensor_scalar(s, s, -0.5, 1.5, ALU.mult, ALU.add))
                link(dve.tensor_tensor(y, y, s, ALU.mult))

            counts = dict(root=0, sq=0, ts=0, tp=0, a=0)

            def normalise(src):
                counts["sq"] += 2
                dve.wait_ge(sq_done, counts["sq"])
                root(2, D)
                for i in range(TT):
                    ins = dve.tensor_scalar(TS[:, i, :], src[:, i, :], rs[:, i:i + 1], None, ALU.mult)
                counts["ts"] += 1
                ins.then_inc(ts_ready, 1)

            def to_features(w, scale=None, shift=None):
                for q in range(2):
                    counts["tp"] += 1
                    dve.wait_ge(tp_done, counts["tp"])
                    bank = bank_of(w)
                    for k in range(4):
                        kk = 4 * q + k
                        src = ps[:, bank + k // 2, SEQ * (k % 2):SEQ * (k % 2) + SEQ]
                        if scale is None:
                            ins = dve.tensor_copy(AF[:, kk, :], src)
                        elif shift is None:
                            ins = dve.tensor_scalar(AF[:, kk, :], src, scale[:, kk:kk + 1], None, ALU.mult)
                        else:
                            ins = dve.tensor_scalar(AF[:, kk, :], src, scale[:, kk:kk + 1], shift[:, kk:kk + 1],
                                                    ALU.mult, ALU.add)
                    free(w, ins)
                    half_ = slice(4 * q, 4 * q + 4)
                    link(dve.tensor_copy(AH[:, half_, :], AF[:, half_, :]))
                    dve.tensor_tensor(AL[:, half_, :], AF[:, half_, :], AH[:, half_, :].bitcast(fp), ALU.subtract)\
                       .then_inc(a_ready, 1)
                    counts["a"] += 1
                dve.wait_ge(a_ready, counts["a"])

            def norm_scale(scale_cols, norm_cols):
                link(dve.scalar_tensor_tensor(scl, scale_cols, 1.0, norm_cols, ALU.add, ALU.mult))

            def head_norm(w, norm_cols):
                counts["sq"] += 1
                dve.wait_ge(sq_done, counts["sq"])
                link(dve.tensor_reduce(ss, flatA.rearrange("p (g n) -> p g n", g=16), AX.X, ALU.add))
                root(16, M_DV)
                dve.wait_ge(ogs_set, 1 if norm_cols == V_MNORM else 2)
                link(dve.tensor_tensor(flatT.rearrange("p (g n) -> p g n", g=16),
                                       flatT.rearrange("p (g n) -> p g n", g=16),
                                       rs.rearrange("p (g o) -> p g o", o=1).to_broadcast([128, 16, 128]), ALU.mult))
                counts["ts"] += 1
                dve.tensor_tensor(TS[:, :, :], TS[:, :, :], og, ALU.mult).then_inc(ts_ready, 1)

            def out_matrix(w, n_ready):
                for c in range(2):
                    los(w, 2)
                    dve.wait_ge(w_used, w.unit)
                    bank = bank_of(w)
                    cut = slice(512 * c, 512 * c + 512)
                    tmp = tok(flatA[:, 1024 * c:1024 * c + 1024])
                    for i in range(TT):
                        ins = dve.tensor_tensor(tmp[:, i, :], ps[:, bank + i, :], GB[:, 0, cut], ALU.mult)
                    free(w, ins)
                    ins = dve.tensor_tensor(X[:, :, cut], X[:, :, cut], tmp, ALU.add)
                both(ins, x_ready, n_ready)

            def ada_gates(w, n):
                for g in range(3):
                    dve.wait_ge(ada_sum, n + g)
                    bank = bank_of(w)
                    if g == 1:
                        ins = dve.tensor_copy(mod[:, 2:4, :], ps[:, bank, 0:16].rearrange("p (a k) -> p a k", a=2))
                    else:
                        ins = dve.tensor_copy(GB[:, g // 2, :].rearrange("p (b n) -> p b n", b=2), ps[:, bank:bank + 2, :])
                    free(w, ins)

            def evac_t(w, c, done):
                dve.wait_ge(silu_done, done + c + 1)
                bank = bank_of(w)
                n = 2 * COLS[c][1]
                free(w, dve.tensor_tensor(hid[:, c % 2, 0:n], sil[:, c % 2, 0:n], ps[:, bank + 1, 0:n], ALU.mult))
                hh = HH[:, 2 * c:2 * c + n // SEQ, :].rearrange("p k t -> p (k t)")
                hl = HL[:, 2 * c:2 * c + n // SEQ, :].rearrange("p k t -> p (k t)")
                link(dve.tensor_copy(hh, hid[:, c % 2, 0:n]))
                dve.tensor_tensor(hl, hid[:, c % 2, 0:n], hh.bitcast(fp), ALU.subtract).then_inc(hid_done, 1)

            def evac_d(w, first_unit, c):
                dve.wait_ge(w_used, first_unit + 12 + 3 * (c + 1))
                bank = bank_of(w)
                cut = slice(512 * c, 512 * c + 512)
                for i in range(TT):
                    ins = dve.scalar_tensor_tensor(Y[:, i, cut], ps[:, bank + i, :], gcur[:, i:i + 1], Y[:, i, cut],
                                                   ALU.mult, ALU.add)
                free(w, ins)

            def group_from(w, first, first_unit, done, side):
                for j in range(first, 18):
                    lo(w, JOBS[j])
                    if j < 12:
                        side(j)
                    if 3 <= j <= 13 and j % 2:
                        evac_t(w, (j - 3) // 2, done)
                evac_d(w, first_unit, 0)

            def groups(w, n, gate=None, side=lambda e, j: None, loop=False):
                LINKS = 6 + (gate is not None)
                first_unit, done = w.unit, w.hidden
                for j in range(2):
                    lo(w, JOBS[j])
                    side(0, j)

                def rest(w, e, first_unit, done):
                    if gate is not None:
                        gate(e)
                    group_from(w, 2, first_unit, done, lambda j: side(e, j))

                def next_start(w, e):
                    for j in range(2):
                        lo(w, JOBS[j])
                        side(e, j)

                if loop:
                    base = steps[0]
                    with dve.Fori(0, n - 1) as e:
                        v = w.after_groups(e)
                        steps[0] = base + e * LINKS
                        rest(v, e, first_unit + e * 18, done + e * 6)
                        next_start(v, e)
                        evac_d(v, first_unit + e * 18, 1)
                    steps[0] = base + (n - 1) * LINKS
                    w = w.after_groups(n - 1)
                else:
                    for e in range(n - 1):
                        rest(w, e, first_unit + e * 18, done + e * 6)
                        next_start(w, e + 1)
                        evac_d(w, first_unit + e * 18, 1)
                e = n - 1
                rest(w, e, first_unit + e * 18, done + e * 6)
                evac_d(w, first_unit + e * 18, 1)
                w.hidden = done + 6 * n
                return w

            w = Walk()
            dve.memset(wsm[:, :, :], 0.0).then_inc(cleared, 1)
            dve.memset(col[:, :], 0.0).then_inc(cleared, 1)
            dve.memset(vx[:, :, :, 128:129].rearrange("p i h o -> p (i h) o"), 1.0)
            dve.wait_ge(cleared, 2)
            dve.memset(ones2, 1.0)
            dve.wait_ge(cst_in, 16)
            dve.tensor_copy(identb[:, :], ident)
            dve.tensor_copy(maskb[:, :, :], cst[:, C_CAUSAL:C_CAUSAL + 256].rearrange("p (a n) -> p a n", a=2))\
               .then_inc(consts_set, 1)
            dve.wait_ge(rows_t, 1)
            dve.tensor_copy(vec[:, :], ps[:, 0, 0:128]).then_inc(vec_set, 1)
            free(w, dve.tensor_copy(adab[:, :], ps[:, 1, 0:96]))
            dve.wait_ge(cond_set, 1)
            for k in range(KT):
                ada_unit(w, 0, 0, k)
            dve.wait_ge(ada_sum, 1)
            free(w, dve.tensor_copy(mod[:, 0:2, :], ps[:, 2, 0:16].rearrange("p (a k) -> p a k", a=2)))
            norm_scale(mod[:, 1, :], vec[:, V_NORM1:V_NORM1 + 8])
            normalise(X)
            to_features(w, scl, mod[:, 0, :])
            dve.wait_ge(small_in, 14 * 16)
            link(dve.tensor_scalar(bias8[0:8, 2:3], bias8[0:8, 0:1], 1.0 / 15.0, None, ALU.mult))
            los(w, 2)
            for q in range(2):
                los(w, 2)
                dve.wait_ge(w_used, 2 * q + 2)
                bank = bank_of(w)
                for tap in range(CONV_K):
                    for k in range(4):
                        kk = 4 * q + k
                        x_ = ps[:, bank + k // 2, SEQ * (k % 2):SEQ * (k % 2) + SEQ - tap]
                        wc = vec[:, V_CONVW + 8 * (CONV_K - 1 - tap) + kk:V_CONVW + 8 * (CONV_K - 1 - tap) + kk + 1]
                        if tap == 0:
                            ins = dve.tensor_scalar(qk[:, kk, :], x_, wc, vec[:, V_CONVB + kk:V_CONVB + kk + 1],
                                                    ALU.mult, ALU.add)
                        else:
                            ins = dve.scalar_tensor_tensor(qk[:, kk, tap:], x_, wc, qk[:, kk, tap:], ALU.mult, ALU.add)
                    if tap < CONV_K - 1:
                        link(ins)
                free(w, ins)
            dve.sem_inc(conv_done, 1)
            for c in range(4):
                if c < 3:
                    los(w, 2)
                dve.wait_ge(w_used, 4 + 2 * c + 2)
                bank = bank_of(w)
                cc = c % 2
                for i in range(TT):
                    if c < 2:
                        ins = dve.tensor_copy(vx[:, i, 4 * cc:4 * cc + 4, 0:128],
                                              ps[:, bank + i, :].rearrange("p (h n) -> p h n", h=4))
                    else:
                        ins = dve.tensor_copy(og[:, i, 512 * cc:512 * cc + 512], ps[:, bank + i, :])
                free(w, ins)
            dve.sem_inc(og_set, 1)
            dve.wait_ge(small_mm, 1)
            bank = bank_of(w)
            dve.tensor_copy(rows[:, 0, :], ps[0:8, bank, 0:SEQ])
            free(w, dve.tensor_scalar(rows[:, 1, :], ps[0:8, bank + 1, 0:SEQ], bias8[0:8, 1:2], None, ALU.add))
            dve.scalar_tensor_tensor(rows[:, 2, :], rows[:, 1, :], -1.0, rows[:, 1, :], ALU.mult, ALU.max).then_inc(g_vec, 1)
            dve.wait_ge(g_act, 1)
            link(dve.scalar_tensor_tensor(rows[:, 4, :], rows[:, 1, :], 0.0, rows[:, 3, :], ALU.min, ALU.subtract))
            link(dve.tensor_tensor_scan(rows[:, 2, :], ones[0:8, :], rows[:, 4, :], 0.0, ALU.mult, ALU.add))
            link(dve.scalar_tensor_tensor(rows[:, 5, :], rows[:, 0, :], 15.0, rows[:, 2, :], ALU.mult, ALU.subtract))
            link(dve.tensor_tensor_scan(rows[:, 6, :], ones[0:8, :], rows[:, 5, :], 0.0, ALU.mult, ALU.max))
            dve.tensor_tensor(rows[:, 7, :], rows[:, 2, :], rows[:, 6, :], ALU.add).then_inc(g_vec, 1)
            dve.wait_ge(col_tp, 1)
            bank = bank_of(w)
            free(w, dve.tensor_copy(col[:, 48:80], ps[:, bank, 0:32]))
            dve.sem_inc(cols_set, 1)
            for step in range(M_HEADS + 1):
                if step < M_HEADS:
                    h = step
                    dve.wait_ge(m_exp, h + 1)
                    at_least(dve, m_o, h - 1)
                    bank = bank_of(w)
                    w.next_pair()
                    dve.scalar_tensor_tensor(pt[:, h % 2, :], ps[:, bank + 1, 0:384], M_DQK ** -0.5, em[:, h % 2, :],
                                             ALU.mult, ALU.mult).then_inc(m_pt, 1)
                    dve.wait_ge(m_pt, h + 1)
                    dve.sem_inc(ps_free, 1)
                if step >= 1:
                    h = step - 1
                    dve.wait_ge(m_o, h + 1)
                    bank = bank_of(w)
                    d = dcol[:, 8 + 2 * (h % 2):10 + 2 * (h % 2)]
                    link(dve.scalar_tensor_tensor(d, ps[:, bank, 128:512:256], -1.0, ecol[:, :, h], ALU.mult, ALU.max))
                    link(dve.tensor_tensor(d, ps[:, bank, 128:512:256], d, ALU.max))
                    link(dve.reciprocal(d, d))
                    for i in range(TT):
                        ins = dve.tensor_scalar(TS[:, i, 128 * h:128 * h + 128], ps[:, bank, 256 * i:256 * i + 128],
                                                d[:, i:i + 1], None, ALU.mult)
                    free(w, ins)
                    for k in range(2 * h, 2 * h + 2):
                        ada_unit(w, 0, 1 + k // 8, k % 8)
            dve.sem_inc(heads_done, 1)
            head_norm(w, V_MNORM)
            to_features(w, vec[:, V_MNORM:V_MNORM + 8])
            ada_gates(w, 2)
            out_matrix(w, 1)
            norm_scale(mod[:, 3, :], vec[:, V_NORM2:V_NORM2 + 8])
            normalise(X)
            to_features(w, scl, mod[:, 2, :])
            dve.memset(Y, 0.0)
            link(dve.tensor_copy(gcur, ones2))
            w = groups(w, 2, side=lambda e, j: ada_unit(w, 1, (12 * e + j) // 8, (12 * e + j) % 8))

            def add_layer(n_ready, gate_row=None, s=x_ready):
                if gate_row is not None:
                    for i in range(TT):
                        ins = dve.tensor_tensor(Y[:, i, :], Y[:, i, :], gate_row, ALU.mult)
                    link(ins)
                both(dve.tensor_tensor(X[:, :, :], X[:, :, :], Y, ALU.add), s, n_ready)

            add_layer(2, GB[:, 1, :])
            dve.wait_ge(ada_sum, 5)
            bank = bank_of(w)
            free(w, dve.tensor_copy(mod[:, 0:2, :], ps[:, bank, 0:16].rearrange("p (a k) -> p a k", a=2)))
            ada_gates(w, 6)
            norm_scale(mod[:, 1, :], vec[:, V_NORM1 + 8:V_NORM1 + 16])
            normalise(X)
            to_features(w, scl, mod[:, 0, :])
            first_unit = w.unit
            los(w, 2)
            for q in range(4):
                los(w, 2)
                dve.wait_ge(w_used, first_unit + 2 * q + 2)
                bank = bank_of(w)
                dst = (hq if q < 2 else hk)[:, 1024 * (q % 2):1024 * (q % 2) + 1024]
                free(w, dve.tensor_copy(dst.rearrange("p (b n) -> p b n", b=2), ps[:, bank:bank + 2, :]))
                if q % 2:
                    dve.sem_inc(h_raw, 1)
            for c in range(4):
                if c < 3:
                    los(w, 2)
                dve.wait_ge(w_used, first_unit + 8 + 2 * c + 2)
                bank = bank_of(w)
                dst = (hv if c < 2 else og)[:, :, 512 * (c % 2):512 * (c % 2) + 512]
                free(w, dve.tensor_copy(dst, ps[:, bank:bank + 2, :]))
            dve.sem_inc(og_set, 1)
            dve.tensor_tensor(lbc[:, 0:8], vec[:, V_LB:V_LB + 8], vec[:, V_LB:V_LB + 8], ALU.subtract)\
               .then_inc(h_vec, 1)
            dve.wait_ge(h_act, 3)
            link(dve.reciprocal(lbc[:, 8:16], lbc[:, 0:8]))
            link(dve.tensor_tensor(lbc[:, 0:8], lbc[:, 0:8], lbc[:, 8:16], ALU.mult))
            link(dve.tensor_tensor(lbc[:, 0:8], lbc[:, 0:8], lbc[:, 0:8], ALU.subtract))
            link(dve.tensor_scalar(lbc[:, 8:16], lbc[:, 0:8], -1.0, 1.0, ALU.mult, ALU.add))
            for k in range(KT):
                cut = slice(SEQ * k, SEQ * (k + 1))
                dve.tensor_scalar(hk[:, cut], hk[:, cut], lbc[:, 8 + k:9 + k], None, ALU.mult)
                ins = dve.tensor_scalar(flatA[:, cut], flatA[:, cut], lbc[:, 8 + k:9 + k], lbc[:, k:k + 1],
                                        ALU.mult, ALU.add)
            link(ins)
            both(dve.tensor_scalar(flatA, flatA, F_FLOOR, None, ALU.max), h_vec, 2)
            dve.wait_ge(h_act, 4)
            kq = level_buf[2]
            dve.tensor_scalar(flatA, flatA, 2.0 ** -40, None, ALU.is_lt)
            link(dve.tensor_scalar(kq, kq, float(np.log(LN_SHIFT)), None, ALU.subtract))
            link(dve.copy_predicated(flatT, flatA.bitcast(i32), kq))
            dve.memset(at, 0.0)
            link(dve.memset(kq, 1.0))
            link(dve.memset(kq.rearrange("p (g n) -> p g n", g=16)[:, :, 0:1], 0.0))
            link(dve.tensor_tensor_scan(hb, kq, flatT, 0.0, ALU.mult, ALU.add))

            def halves(a, blk):
                v = a.rearrange("p (n two b) -> p n two b", two=2, b=blk)
                return v[:, :, 0, :], v[:, :, 1, :]

            def sub(n):
                blk = 128 >> n
                left, right = halves(level_buf[n % 3], blk)
                bl, br = halves(hb, blk)
                ref = bl[:, :, blk - 1:blk].to_broadcast([128, 1024 // blk, blk])
                dve.tensor_tensor(left, ref, bl, ALU.subtract)
                if n == 0:
                    dve.tensor_copy(right, br).then_inc(l_sub, 1)
                else:
                    dve.tensor_tensor(right, br, ref, ALU.subtract).then_inc(l_sub, 1)

            mm_count = 0
            sub(0)
            for n in range(LEVELS + 2):
                if n < LEVELS:
                    sub(n + 1)
                if n <= LEVELS:
                    dve.wait_ge(l_exp, n + 1)
                    blk = 128 >> n
                    left, right = halves(level_buf[n % 3], blk)
                    dve.tensor_tensor(left, left, halves(hk, blk)[0], ALU.mult)
                    dve.tensor_tensor(right, right, halves(hq, blk)[1], ALU.mult).then_inc(l_kq, 1)
                for m in ([n - 1] if n <= LEVELS else [n - 1, n]):
                    if m < 0:
                        continue
                    for half_ in range(1 if m == 0 else 2):
                        mm_count += 1
                        dve.wait_ge(l_mm, mm_count)
                        bank = bank_of(w)
                        src = ps[:, bank:bank + 2, :]
                        if m == 0:
                            ins = dve.tensor_copy(ax.rearrange("p (b h) n -> p b (h n)", b=2), src)
                        else:
                            c0 = C_LEVEL + 128 * (m - 1)
                            mask = cst[:, c0:c0 + 128].bitcast(i32).rearrange("p (o n) -> p o n", o=1)\
                                .to_broadcast([128, 8, 128])
                            ins = dve.copy_predicated(at[:, 8 * half_:8 * half_ + 8, :], mask,
                                                      src.rearrange("p b (g n) -> p (b g) n", g=4))
                        free(w, ins)
            for i in range(TT):
                dve.wait_ge(h_o, i + 1)
                bank = bank_of(w)
                free(w, dve.tensor_copy(TS[:, i, :].rearrange("p (b n) -> p b n", b=2), ps[:, bank:bank + 2, :]))
            dve.sem_inc(heads_done, 1)
            head_norm(w, V_HNORM)
            to_features(w, vec[:, V_HNORM:V_HNORM + 8])
            out_matrix(w, 3)
            norm_scale(mod[:, 3, :], vec[:, V_NORM2 + 8:V_NORM2 + 16])
            normalise(X)
            to_features(w, scl, mod[:, 2, :])
            dve.wait_ge(small_mm, 2)
            bank = bank_of(w)
            free(w, dve.tensor_copy(lgt, ps[:, bank, 0:16].rearrange("p (i e) -> p i e", i=TT)))

            def over(a):
                return a.rearrange("p (i o) -> p i o", o=1).to_broadcast([128, TT, N_EXPERTS])

            rank = cst[:, C_RANK:C_RANK + 8].rearrange("p (o e) -> p o e", o=1).to_broadcast([128, TT, N_EXPERTS])
            for which, src in ((0, lgt), (1, lg2)):
                link(dve.tensor_reduce(mm2[:, which, :], src, AX.X, ALU.max))
                link(dve.tensor_tensor(oh[:, which], src, over(mm2[:, which, :]), ALU.is_equal))
                link(dve.tensor_tensor(oh[:, which], oh[:, which], rank, ALU.mult))
                link(dve.tensor_reduce(mm2[:, 7, :], oh[:, which], AX.X, ALU.max))
                link(dve.tensor_tensor(oh[:, which], rank, over(mm2[:, 7, :]), ALU.is_equal))
                if which == 0:
                    link(dve.scalar_tensor_tensor(lg2, oh[:, 0], -BIG, lgt, ALU.mult, ALU.add))
            dve.tensor_tensor(mm2[:, 2, :], mm2[:, 1, :], mm2[:, 0, :], ALU.subtract).then_inc(g_vec, 1)
            dve.wait_ge(g_act, 3)
            link(dve.tensor_scalar(mm2[:, 4, :], mm2[:, 3, :], 1.0, None, ALU.add))
            link(dve.reciprocal(mm2[:, 5, :], mm2[:, 4, :]))
            link(dve.tensor_tensor(mm2[:, 6, :], mm2[:, 5, :], mm2[:, 3, :], ALU.mult))
            link(dve.tensor_tensor(oh[:, 0], oh[:, 0], over(mm2[:, 5, :]), ALU.mult))
            link(dve.tensor_tensor(oh[:, 1], oh[:, 1], over(mm2[:, 6, :]), ALU.mult))
            link(dve.tensor_tensor(gates, oh[:, 0], oh[:, 1], ALU.add))
            link(dve.memset(Y, 0.0))

            def pick_gate(e):
                cut = slice(e, e + 1) if isinstance(e, int) else bass.ds(e, 1)
                link(dve.tensor_copy(gcur, gates[:, :, cut].rearrange("p i o -> p (i o)")))

            w = groups(w, N_EXPERTS, gate=pick_gate, loop=True)
            add_layer(4, GB[:, 1, :])
            normalise(X)
            dve.wait_ge(ts_ready, counts["ts"])
            dve.wait_ge(late_in, 32)
            for i in range(TT):
                ins = dve.tensor_tensor(X[:, i, :], TS[:, i, :], fwb, ALU.mult)
            both(ins, x_ready, 5)
            normalise(memx)
            to_features(w, vec[:, V_GMEM:V_GMEM + 8])
            first_unit = w.unit
            los(w, 2)
            for c in range(2):
                if c == 0:
                    los(w, 2)
                dve.wait_ge(w_used, first_unit + 2 * c + 2)
                bank = bank_of(w)
                free(w, dve.tensor_copy(mkv[:, c], ps[:, bank:bank + 2, :]))
            normalise(X)
            to_features(w, vec[:, V_GMIX:V_GMIX + 8])
            first_unit = w.unit
            los(w, 2)
            for j in range(7):
                if j < 6:
                    los(w, 2)
                dve.wait_ge(w_used, first_unit + 2 * j + 2)
                bank = bank_of(w)
                free(w, dve.tensor_copy(qkv[:, j], ps[:, bank:bank + 2, :]))
            dve.wait_ge(small_mm, 3)
            bank = bank_of(w)
            free(w, dve.tensor_scalar(frow[:, 0, :], ps[0:40, bank, 0:SEQ], bias8[0:40, 3:4], None, ALU.add))
            both(dve.scalar_tensor_tensor(frow[:, 1, :], frow[:, 0, :], -1.0, frow[:, 0, :], ALU.mult, ALU.max), g_vec, 4)
            dve.sem_inc(qk_raw, 1)
            dve.wait_ge(g_act, 4)
            link(dve.scalar_tensor_tensor(frow[:, 1, :], frow[:, 0, :], 0.0, frow[:, 2, :], ALU.min, ALU.subtract))
            link(dve.memset(fcum, 0.0))
            link(dve.tensor_tensor_scan(frow[:, 3, :], ones[0:40, :], frow[:, 1, :], 0.0, ALU.mult, ALU.add))
            dve.tensor_scalar(fox_r, fcum, cst[:, C_FOX:C_FOX + 1], cst[:, C_FOX + 1:C_FOX + 2],
                              ALU.mult, ALU.add)
            for n, (blk, g0, dh) in enumerate(NORMED):
                counts["sq"] += 1
                dve.wait_ge(sq_done, counts["sq"])
                nh = 512 // dh
                a = (mkv[:, 0] if blk is None else qkv[:, blk]).rearrange("p i (h d) -> p i h d", d=dh)
                sq = flatA[:, 1024 * (n % 2):1024 * (n % 2) + 1024].rearrange("p (g d) -> p g d", d=dh)
                link(dve.tensor_reduce(ss[:, 0:2 * nh], sq, AX.X, ALU.add))
                root(2 * nh, dh)
                fa = a.rearrange("p i h d -> p (i h) d")
                link(dve.tensor_tensor(fa, fa, rs[:, 0:2 * nh].rearrange("p (g o) -> p g o", o=1)
                                       .to_broadcast([128, 2 * nh, dh]), ALU.mult))
                ins = dve.tensor_tensor(fa, fa, gains[:, g0:g0 + dh].rearrange("p (o d) -> p o d", o=1)
                                        .to_broadcast([128, 2 * nh, dh]), ALU.mult)
                if blk in (0, 1):
                    link(ins)
                    x1, x2 = a[:, :, :, 0:8], a[:, :, :, 8:16]
                    tr = TS[:, 0, 0:512].rearrange("p (r i h d) -> p r i h d", r=4, i=TT, h=A_HEADS)

                    def table(c0):
                        return cst[:, c0:c0 + 16].rearrange("p (i o d) -> p i o d", i=TT, o=1)\
                            .to_broadcast([128, TT, A_HEADS, 8])
                    for r, (x_, c0) in enumerate(((x1, C_COS), (x2, C_SIN), (x2, C_COS), (x1, C_SIN))):
                        ins = dve.tensor_tensor(tr[:, r], x_, table(c0), ALU.mult)
                    link(ins)
                    dve.tensor_tensor(x1, tr[:, 0], tr[:, 1], ALU.subtract)
                    ins = dve.tensor_tensor(x2, tr[:, 2], tr[:, 3], ALU.add)
                both(ins, qk_ready, n + 1)
            for h in range(A_HEADS):
                ins = dve.tensor_scalar(fox_l[:, h, :], fcum, cst[:, C_FOX + 2 + h:C_FOX + 3 + h],
                                        cst[:, C_FOX + 10 + h:C_FOX + 11 + h], ALU.mult, ALU.add)
            ins.then_inc(fox_set, 1)
            for b in range(3):
                for which in range(2):
                    counts["tp"] += 1
                    dve.wait_ge(tp_done, counts["tp"])
                    bank = bank_of(w)
                    free(w, dve.tensor_copy(acc[:, b, 1024 * which:1024 * which + 1024]
                                            .rearrange("p (b n) -> p b n", b=2), ps[:, bank:bank + 2, :]))
                    dve.sem_inc(qk_set, 1)
            outs = 0
            for b, (gh0, heads, dh, causal, fox) in enumerate(BRANCHES):
                n0 = 128 if causal else 256
                per = 128 // dh
                for step in range(heads + 4):
                    if step < heads:
                        gh = gh0 + step
                        dve.wait_ge(t_s, gh + 1)
                        at_least(dve, t_exp, gh - 1)
                        bank = t_bank_s(gh)
                        m0 = 2 * (gh % 2)
                        dve.tensor_reduce(nmx[:, 4 + m0:5 + m0], ps[:, bank, 0:n0], AX.X, ALU.max)
                        link(dve.tensor_reduce(nmx[:, 5 + m0:6 + m0], ps[:, bank, n0:n0 + 256], AX.X, ALU.max))
                        dve.tensor_scalar(nmx[:, m0:m0 + 2], nmx[:, 4 + m0:6 + m0], -(dh ** -0.5), None, ALU.mult)\
                           .then_inc(t_max, 1)
                    if 1 <= step <= heads:
                        gh = gh0 + step - 1
                        m0 = 2 * (gh % 2)
                        dve.wait_ge(t_exp, gh + 1)
                        link(dve.reciprocal(rsum[:, 4 + m0:6 + m0], rsum[:, m0:m0 + 2]))
                        dve.tensor_scalar(prb[:, gh % 2, 0:n0], prb[:, gh % 2, 0:n0], rsum[:, 4 + m0:5 + m0], None, ALU.mult)
                        dve.tensor_scalar(prb[:, gh % 2, n0:n0 + 256], prb[:, gh % 2, n0:n0 + 256],
                                          rsum[:, 5 + m0:6 + m0], None, ALU.mult).then_inc(t_p, 1)
                    if 2 <= step <= heads + 1:
                        gh = gh0 + step - 2
                        dve.wait_ge(t_tp, gh + 1)
                        at_least(dve, t_o, gh - 1)
                        bank = t_bank_s(gh) + 1
                        assert bank == bank_of(w) + 1
                        w.next_pair()
                        n = 384 if causal else 512
                        dve.tensor_copy(pts[:, gh % 2, 0:n], ps[:, bank, 0:n]).then_inc(t_pt, 1)
                        dve.wait_ge(t_pt, gh + 1)
                        dve.sem_inc(ps_free, 1)
                    h = step - 4
                    if 0 <= h and h % per == 0:
                        kt = h // per
                        dve.wait_ge(t_o, gh0 + h + per)
                        bank = bank_of(w)
                        outs += 1
                        hh, hl = HH[:, 4 * b + kt, :], HL[:, 4 * b + kt, :]
                        link(dve.tensor_copy(hh, ps[:, bank, 0:SEQ]))
                        both(dve.tensor_tensor(hl, ps[:, bank, 0:SEQ], hh.bitcast(fp), ALU.subtract), t_y, outs)
                        w.next_pair()
                        dve.sem_inc(ps_free, 1)
            first_unit = w.unit
            for b in range(3):
                for c in range(2):
                    los(w, 2)
                    dve.wait_ge(w_used, w.unit)
                    bank = bank_of(w)
                    free(w, dve.tensor_copy(sg[:, :, 512 * c:512 * c + 512], ps[:, bank:bank + 2, :]))
                dve.sem_inc(b_raw, 1)
                los(w, 1)
                dve.wait_ge(b_sig, b + 1)
                for c in range(2):
                    if c == 0:
                        los(w, 1)
                    dve.wait_ge(w_used, first_unit + 6 * b + 4 + c + 1)
                    bank = bank_of(w)
                    cut = slice(512 * c, 512 * c + 512)
                    dst = TS[:, :, cut] if b == 0 else tok(flatA[:, 0:1024])
                    free(w, dve.tensor_tensor(dst, ps[:, bank:bank + 2, :], sg[:, :, cut], ALU.mult))
                    if b:
                        link(dve.tensor_tensor(TS[:, :, cut], TS[:, :, cut], dst, ALU.add))
            counts["ts"] += 1
            dve.sem_inc(ts_ready, 1)
            to_features(w)
            for c in range(2):
                los(w, 2)
                dve.wait_ge(w_used, w.unit)
                bank = bank_of(w)
                cut = slice(512 * c, 512 * c + 512)
                free(w, dve.tensor_tensor(X[:, :, cut], X[:, :, cut], ps[:, bank:bank + 2, :], ALU.add))
            dve.sem_inc(x_ready, 1)
            normalise(X)
            to_features(w, vec[:, V_GFFN:V_GFFN + 8])
            dve.memset(Y, 0.0)
            link(dve.tensor_copy(gcur, ones2))
            w = groups(w, 2)
            add_layer(1, s=out_ready)


_INPUTS = ["x", "c", "ada_w", "ada_b", "norm1_w", "norm2_w", "final_norm_w", "m_w_in", "m_i_bias", "m_f_bias",
           "m_conv_w", "m_conv_b", "m_norm_w", "m_w_out", "h_w_in", "h_lb_logits", "h_norm_w", "h_w_out",
           "ffn_w_gate", "ffn_w_up", "ffn_w_down", "moe_router", "moe_w_gate", "moe_w_up", "moe_w_down", "mem_2",
           "g_mix_2", "w_in_2", "b_forget_2", "g_q_moba_2", "g_k_moba_2", "g_q_fox_2", "g_k_fox_2", "g_q_mem_2",
           "g_k_mem_2", "g_mem_2", "w_mem_kv_2", "w_br_moba_2", "w_br_fox_2", "w_br_mem_2", "w_out_2", "g_ffn_2",
           "w_gate_2", "w_up_2", "w_down_2"]


def kernel(**inputs):
    import concourse.bacc as bacc
    from concourse.bass_utils import run_bass_kernel_spmd

    nc = bacc.Bacc("TRN2", target_bir_lowering=False, num_devices=1)
    arrays = {f"in_{n}": np.ascontiguousarray(inputs[n]) for n in _INPUTS}
    arrays["in_shape_consts"] = shape_constants()
    t = {n[3:]: nc.dram_tensor(n, a.shape, mybir.dt.from_np(a.dtype), kind="ExternalInput").ap()
         for n, a in arrays.items()}
    out = nc.dram_tensor("out_x", (1, SEQ, D), mybir.dt.float32, kind="ExternalOutput").ap()
    build(nc, t, out)
    r = run_bass_kernel_spmd(nc, [arrays], core_ids=[0])
    return r.results[0]["out_x"]
```

```python
from contextlib import ExitStack

import numpy as np
import concourse.bass as bass
from concourse import mybir

SEQ, D = 256, 1024
KT = D // 128
TT = SEQ // 128
M_HEADS, M_DQK, M_DV = 8, 64, 128
M_QK, M_V = M_HEADS * M_DQK, M_HEADS * M_DV
H_HEADS, H_D = 8, 128
D_FF, N_EXPERTS = 2816, 8
D_GROUP = D_FF // 2
FT = D_GROUP // 128
CONV_K = 4
EPS = 1e-6
F_FLOOR = 1e-30
BIG = 1e30
A_HEADS, A_D, C_HEADS, C_D = 8, 64, 4, 128
N_RAW, N_HL = 3, 3
UNIT = 2048
LEVELS = 7
LN_SHIFT = 2.0 ** 50

V_NORM1, V_NORM2, V_C, V_CONVW, V_CONVB, V_MNORM, V_LB, V_HNORM, V_GMIX, V_GMEM, V_GFFN = \
    0, 16, 32, 40, 72, 80, 88, 96, 104, 112, 120
C_ID, C_CAUSAL, C_CAUSALT, C_COS, C_SIN, C_FOX, C_RANK, C_LEVEL = 0, 128, 256, 384, 400, 416, 434, 448
C_COLS = C_LEVEL + (LEVELS + 1) * 128

BRANCHES = ((0, A_HEADS, A_D, True, False), (A_HEADS, A_HEADS, A_D, True, True),
            (2 * A_HEADS, C_HEADS, C_D, False, False))
NORMED = ((0, 0, A_D), (1, A_D, A_D), (3, 2 * A_D, A_D), (4, 3 * A_D, A_D),
          (6, 4 * A_D, C_D), (None, 4 * A_D + C_D, C_D))

PAIR_HEADS = 2 + 2 + 2 + 4 + 1 + 1
PAIR_FFN = PAIR_HEADS + 2 * M_HEADS + 2 + 3 + 2 + 2
PAIR_LEVELS = PAIR_FFN + 16 + 4 + 2 + 4 + 4
PAIR_MOE = PAIR_LEVELS + 2 * LEVELS + 3 + 2 + 2 + 2 + 2 + 1 + 1 + 2
E_PAIRS = 16
PAIR_ATT = PAIR_MOE + E_PAIRS * N_EXPERTS + 2 + 2 + 2 + 7 + 1 + 6
PAIR_FFN2 = PAIR_ATT + 12 + 12 + 8 + 12 + 2 + 2 + 2


def m_bank_s(h):
    return 2 * ((PAIR_HEADS + (2 * h - 1 if h else 0)) % 4)


def t_bank_s(gh):
    b = 0 if gh < A_HEADS else 1 if gh < 2 * A_HEADS else 2
    i = gh - BRANCHES[b][0]
    before = max(0, i - 2) if b == 2 else max(0, (i - 1) // 2)
    return 2 * ((PAIR_ATT + 12 * b + i + before) % 4)


def shape_constants():
    c = np.zeros((128, C_COLS), np.float32)
    c[:, C_ID:C_ID + 128] = np.eye(128)
    row, col = np.arange(128)[:, None], np.arange(128)[None, :]
    c[:, C_CAUSAL:C_CAUSAL + 128] = np.where(col > row, -BIG, 0.0)
    c[:, C_CAUSALT:C_CAUSALT + 128] = np.where(row > col, BIG, 0.0)
    rot = A_D // 4
    half = rot // 2
    inv = (1.0 / (np.float32(500000.0) ** (np.arange(half, dtype=np.float32) * np.float32(2.0) / np.float32(rot))))
    ang = np.arange(SEQ, dtype=np.float32)[:, None] * inv.astype(np.float32)[None, :]
    for i in range(TT):
        c[:, C_COS + half * i:C_COS + half * (i + 1)] = np.cos(ang[128 * i:128 * (i + 1)])
        c[:, C_SIN + half * i:C_SIN + half * (i + 1)] = np.sin(ang[128 * i:128 * (i + 1)])
    for h in range(A_HEADS):
        c[h, C_FOX] = -8.0
        c[32 + h, C_FOX + 1] = 1.0
        c[32 + h, C_FOX + 2 + h] = 8.0
        c[h, C_FOX + 10 + h] = 1.0
    c[:, C_RANK:C_RANK + 8] = 8 - np.arange(8)
    for lev in range(LEVELS):
        b = 64 >> lev
        ok = (row // (2 * b) == col // (2 * b)) & (row % (2 * b) < b) & (col % (2 * b) >= b)
        c[:, C_LEVEL + 128 * lev:C_LEVEL + 128 * (lev + 1)] = ok
    c[:, C_LEVEL + 128 * LEVELS:] = row == col
    return c


def build(nc, t, out):
    fp, fr, bf, i32 = mybir.dt.float32, mybir.dt.float32r, mybir.dt.bfloat16, mybir.dt.int32
    ALU, ACT, AX = mybir.AluOpType, mybir.ActivationFunctionType, mybir.AxisListType

    ctx = ExitStack()
    with ctx:
        ctx.enter_context(nc.allow_non_contiguous_dma(reason="small parameters"))

        def sb(name, shape, dt=fp):
            return ctx.enter_context(nc.sbuf_tensor(name, shape, dt))

        def sem(name):
            return ctx.enter_context(nc.semaphore(name))

        raw = sb("raw", [128, N_RAW, UNIT])
        whi = sb("whi", [128, N_HL, UNIT], fr)
        wlo = sb("wlo", [128, N_HL, UNIT], fr)
        X = sb("X", [128, TT, D])
        AF = sb("AF", [128, KT, SEQ])
        AH = sb("AH", [128, KT, SEQ], fr)
        AL = sb("AL", [128, KT, SEQ], fr)
        HH = sb("HH", [128, 12, SEQ], fr)
        HL = sb("HL", [128, 12, SEQ], fr)
        acc = sb("acc", [128, 3, UNIT])
        TS = sb("TS", [128, TT, D])
        GB = sb("GB", [128, 2, D])
        Z = sb("Z", [128, 10240])
        cst = sb("cst", [128, C_COLS])
        ones = sb("ones", [128, SEQ])
        identb = sb("identb", [128, 128], bf)
        maskb = sb("maskb", [128, 2, 128], bf)
        vec = sb("vec", [128, 128])
        adab = sb("adab", [128, 96])
        mod = sb("mod", [128, 4, KT])
        cond = sb("cond", [128, KT])
        wsm = sb("wsm", [128, KT, 64])
        gains = sb("gains", [128, 4 * A_D + 2 * C_D])
        col = sb("col", [128, 292])
        crowded = sb("crowded", [128, 1], i32)
        ident = cst[:, C_ID:C_ID + 128]
        ps = ctx.enter_context(nc.psum_tensor("ps", [128, 8, 512], fp))

        ss, rs = col[:, 0:16], col[:, 16:32]
        nmx, rsum = col[:, 32:40], col[:, 40:48]
        gcol = col[:, 48:64].rearrange("p (i h) -> p i h", i=TT)
        ecol = col[:, 64:80].rearrange("p (i h) -> p i h", i=TT)
        dcol = col[:, 80:96]
        gates = col[:, 96:112].rearrange("p (i e) -> p i e", i=TT)
        gcur = col[:, 112:114]
        bias8 = col[:, 114:118]
        lbc = col[:, 120:136]
        lgt = col[:, 136:152].rearrange("p (i e) -> p i e", i=TT)
        oh = col[:, 152:184].rearrange("p (w i e) -> p w i e", w=2, i=TT)
        lg2 = col[:, 184:200].rearrange("p (i e) -> p i e", i=TT)
        io8 = col[:, 200:208]
        mm2 = col[:, 208:224].rearrange("p (w i) -> p w i", w=8)
        scl = col[:, 224:232]
        ones2 = col[:, 232:234]
        slot_of = col[:, 272:290].rearrange("p (i e) -> p i e", i=TT)
        slot_cur = col[:, 290:292]
        ms, nt = col[:, 240:256], col[:, 256:272]

        raw_full = [sem(f"raw_full{i}") for i in range(N_RAW)]
        w_hi, w_lo = sem("w_hi"), sem("w_lo")
        w_used = sem("w_used")
        ada_used = sem("ada_used")
        ada_init, ada_sum = sem("ada_init"), sem("ada_sum")
        ps_free = sem("ps_free")
        silu_done, hid_done = sem("silu_done"), sem("hid_done")
        rows_in, small_in, cst_in, x_in, late_in = (sem("rows_in"), sem("small_in"), sem("cst_in"), sem("x_in"),
                                                    sem("late_in"))
        vec_step, act_step = sem("vec_step"), sem("act_step")
        cleared, ones_set, consts_set = sem("cleared"), sem("ones_set"), sem("consts_set")
        rows_t, vec_set, cond_set = sem("rows_t"), sem("vec_set"), sem("cond_set")
        x_ready = sem("x_ready")
        sq_done = sem("sq_done")
        ts_ready, tp_done, a_ready = sem("ts_ready"), sem("tp_done"), sem("a_ready")
        small_mm = sem("small_mm")
        g_vec, g_act = sem("g_vec"), sem("g_act")
        conv_done, og_set, ogs_set, qk_silu = sem("conv_done"), sem("og_set"), sem("ogs_set"), sem("qk_silu")
        col_tp, cols_set = sem("col_tp"), sem("cols_set")
        m_sc, m_exp, m_pt, m_o, heads_done = (sem("m_sc"), sem("m_exp"), sem("m_pt"), sem("m_o"), sem("heads_done"))
        h_raw, h_act, h_vec = sem("h_raw"), sem("h_act"), sem("h_vec")
        l_sub, l_exp, l_kq, l_mm = sem("l_sub"), sem("l_exp"), sem("l_kq"), sem("l_mm")
        h_o = sem("h_o")
        tokens_set, crowd_set = sem("tokens_set"), sem("crowd_set")
        pick_set, place_tp, place_set = sem("pick_set"), sem("place_tp"), sem("place_set")
        e_gather, e_high, e_in = sem("e_gather"), sem("e_high"), sem("e_in")
        e_silu, e_prod, e_tp, e_hidden = sem("e_silu"), sem("e_prod"), sem("e_tp"), sem("e_hidden")
        e_set, e_back = sem("e_set"), sem("e_back")
        qk_raw, qk_ready, qk_set = sem("qk_raw"), sem("qk_ready"), sem("qk_set")
        fox_set = sem("fox_set")
        t_s, t_max, t_exp, t_p, t_tp, t_pt, t_o, t_y = (sem("t_s"), sem("t_max"), sem("t_exp"), sem("t_p"),
                                                        sem("t_tp"), sem("t_pt"), sem("t_o"), sem("t_y"))
        b_raw, b_sig = sem("b_raw"), sem("b_sig")
        root_in, root_out = sem("root_in"), sem("root_out")
        out_ready, out_done = sem("out_ready"), sem("out_done")

        def tok(ap):
            return ap.rearrange("p (i n) -> p i n", i=TT)

        qk = Z[:, 0:2048].rearrange("p (k t) -> p k t", k=KT)
        vx = Z[:, 2048:2048 + TT * M_HEADS * 129].rearrange("p (i h e) -> p i h e", i=TT, h=M_HEADS)
        og = tok(Z[:, 4352:6400])
        em = Z[:, 6400:7168].rearrange("p (b n) -> p b n", b=2)
        pt = Z[:, 7168:7936].rearrange("p (b n) -> p b n", b=2)
        rows = Z[0:8, 7936:7936 + 8 * SEQ].rearrange("p (r t) -> p r t", r=8)
        hv = tok(Z[:, 2048:4096])
        at = Z[:, 6400:8448].rearrange("p (g n) -> p g n", g=16)
        ax = Z[:, 8448:9472].rearrange("p (h n) -> p h n", h=H_HEADS)
        flatA = AF[:, :, :].rearrange("p k t -> p (k t)")
        flatT = TS[:, :, :].rearrange("p i n -> p (i n)")
        hq, hk, hb = acc[:, 0, :], acc[:, 1, :], acc[:, 2, :]
        level_buf = [flatA, flatT, Z[:, 0:2048]]
        Y = tok(Z[:, 0:2048])
        sil = Z[:, 2048:3072].rearrange("p (b n) -> p b n", b=2)
        hid = Z[:, 3072:4096].rearrange("p (b n) -> p b n", b=2)
        fwb = Z[:, 4096:5120]
        e_sil = Z[:, 2048:4096].rearrange("p (b j n) -> p b j n", b=2, j=TT)
        e_hid = acc[:, 1, :].rearrange("p (b j n) -> p b j n", b=2, j=TT)
        e_out = tok(Z[:, 5120:7168])
        chosen = tok(Z[:, 7168:7680])
        place = tok(Z[:, 7680:8192])
        numbers = Z[:, 8192:8448]
        upto = Z[:, 8448:8576]
        qkv = Z[:, 0:7168].rearrange("p (j i n) -> p j i n", j=7, i=TT)
        mkv = Z[:, 7168:9216].rearrange("p (j i n) -> p j i n", j=2, i=TT)
        prb = Z[:, 9216:10240].rearrange("p (b n) -> p b n", b=2)
        pts = GB[:, 0, :].rearrange("p (b n) -> p b n", b=2)
        memx = tok(acc[:, 0, :])
        sg = tok(Z[:, 0:2048])
        fox_l = AF[:, :, :]
        fox_r = GB[:, 1, 0:SEQ]
        fcum = TS[:, 1, 768:1024]
        frow = TS[0:40, 1, :].rearrange("p (r t) -> p r t", r=4)

        def wview(w):
            return w.rearrange("(k p) n -> p k n", p=128)

        ada_w = [t["ada_w"][l].rearrange("(k p) n -> k p n", p=128) for l in range(2)]
        m_in, m_out = wview(t["m_w_in"][0]), wview(t["m_w_out"][0])
        h_in, h_out = wview(t["h_w_in"][0]), wview(t["h_w_out"][0])
        w_in2, w_mkv, w_out2 = wview(t["w_in_2"][0]), wview(t["w_mem_kv_2"][0]), wview(t["w_out_2"][0])
        w_br = [wview(t[n][0]) for n in ("w_br_moba_2", "w_br_fox_2", "w_br_mem_2")]
        M_GATES = 2 * M_QK + 2 * M_V
        F_LOGIT = 6 * 512
        Q_MEM = F_LOGIT + A_HEADS
        A_COL = Q_MEM + 512

        class Walk:

            def __init__(self):
                self.slot, self.uses = 0, [0] * N_RAW
                self.unit, self.hl = 0, 0
                self.pair, self.pb = 0, 0
                self.ada = self.hidden = 0
                self.freed = []

            def next_raw(self):
                s = self.slot
                self.slot = (s + 1) % N_RAW
                self.uses[s] = self.uses[s] + 1
                return s, self.uses[s] * 16

            def next_unit(self):
                u, h = self.unit, self.hl
                self.unit, self.hl = u + 1, (h + 1) % N_HL
                return u, h

            def next_pair(self):
                p, b = self.pair, self.pb
                self.pair, self.pb = p + 1, (b + 1) % 4
                return p, 2 * b

            def after_groups(self, n, pairs=8):
                w = Walk()
                w.slot, w.hl, w.pb, w.ada = self.slot, self.hl, self.pb, self.ada
                w.uses = [c + n * (18 // N_RAW) for c in self.uses]
                w.unit, w.pair = self.unit + n * 18, self.pair + n * pairs
                w.hidden = self.hidden + (n * 6 if pairs == 8 else 0)
                w.freed = [(w_lo, w.unit - 2), (w_lo, w.unit - 1), (w_lo, w.unit)]
                return w

        COLS = [(256 * c, min(256, D_GROUP - 256 * c)) for c in range(6)]
        KS = [(4 * g, min(4, FT - 4 * g)) for g in range(3)]
        JOBS = [KT * COLS[j // 2][1] for j in range(12)] + [512 * KS[j % 3][1] for j in range(6)]

        E_COLS = [(512 * c, min(512, D_GROUP - 512 * c)) for c in range(3)]
        E_JOBS = [4 * E_COLS[j // 4][1] for j in range(12)] + JOBS[12:]
        LEAD = 2

        def at_least(eng, s, v):
            if not isinstance(v, int) or v > 0:
                eng.wait_ge(s, v)

        block = ctx.enter_context(nc.Block())

        @block.sync
        def _(sp):
            w = Walk()

            def load(w, src, n, view):
                if len(w.freed) >= N_RAW:
                    s, v = w.freed[-N_RAW]
                    sp.wait_ge(s, v)
                slot, _ = w.next_raw()
                sp.dma_start(view(raw[:, slot, 0:n]), src).then_inc(raw_full[slot], 16)

            def t_unit(w, wm, c0, n):
                load(w, wm[:, 0:KT, c0:c0 + n], KT * n, lambda r: r.rearrange("p (k n) -> p k n", k=KT))
                u, _ = w.next_unit()
                w.freed.append((w_lo, u + 1))

            def m_unit(w, wm, k0, nk, c0, n=512):
                load(w, wm[:, k0:k0 + nk, c0:c0 + n], nk * n, lambda r: r.rearrange("p (k n) -> p k n", k=nk))
                u, _ = w.next_unit()
                w.freed.append((w_lo, u + 1))

            def ada_unit(w, layer, chunk, k):
                load(w, ada_w[layer][k, :, chunk * UNIT:(chunk + 1) * UNIT], UNIT, lambda r: r)
                w.ada += 1
                w.freed.append((ada_used, w.ada))

            def m_matrix(w, wm, c0, chunks, kts=KT):
                for c in range(chunks):
                    for k0 in range(0, kts, 4):
                        m_unit(w, wm, k0, 4, c0 + 512 * c)

            def group(w, wg, wu, wd, side=lambda j: None):
                for c, (c0, n) in enumerate(COLS):
                    t_unit(w, wg, c0, n)
                    side(2 * c)
                    t_unit(w, wu, c0, n)
                    side(2 * c + 1)
                for c in range(2):
                    for k0, nk in KS:
                        m_unit(w, wd, k0, nk, 512 * c)

            def expert(w, wg, wu, wd):
                for c0, n in E_COLS:
                    for wm in (wg, wu):
                        for k0 in (0, 4):
                            m_unit(w, wm, k0, 4, c0, n)
                for c in range(2):
                    for k0, nk in KS:
                        m_unit(w, wd, k0, nk, 512 * c)

            def half(w, names, e, side=lambda j: None):
                g, u, d = (t[n][0] for n in names)
                cut = slice(e * D_GROUP, (e + 1) * D_GROUP) if isinstance(e, int) else bass.ds(e * D_GROUP, D_GROUP)
                group(w, wview(g[:, cut]), wview(u[:, cut]), wview(d[cut, :]), side)

            for k in range(KT):
                ada_unit(w, 0, 0, k)
            for c in range(4):
                t_unit(w, m_in, 256 * c, 256)
            m_matrix(w, m_in, 2 * M_QK, 4)
            for chunk in (1, 2):
                for k in range(KT):
                    ada_unit(w, 0, chunk, k)
            m_matrix(w, m_out, 0, 2)
            for e in range(2):
                half(w, ("ffn_w_gate", "ffn_w_up", "ffn_w_down"), e,
                     lambda j: ada_unit(w, 1, (12 * e + j) // 8, (12 * e + j) % 8))
            for c in range(8):
                t_unit(w, h_in, 256 * c, 256)
            m_matrix(w, h_in, 2 * D, 4)
            m_matrix(w, h_out, 0, 2)
            with sp.Fori(0, N_EXPERTS) as e:
                expert(w.after_groups(e), *(wview(t[n][0][bass.ds(e, 1)].rearrange("o k n -> (o k) n"))
                                            for n in ("moe_w_gate", "moe_w_up", "moe_w_down")))
            w = w.after_groups(N_EXPERTS)
            m_matrix(w, w_mkv, 0, 2)
            m_matrix(w, w_in2, 0, 6)
            m_matrix(w, w_in2, Q_MEM, 1)
            for b in range(3):
                m_matrix(w, w_in2, A_COL + D * b, 2)
                m_matrix(w, w_br[b], 0, 2, 4)
            m_matrix(w, w_out2, 0, 2)
            with sp.Fori(0, 2) as e:
                half(w.after_groups(e), ("w_gate_2", "w_up_2", "w_down_2"), e)
            sp.wait_ge(out_ready, 1)
            sp.dma_start(out[0].rearrange("(i p) n -> p i n", p=128), X[:, :, :]).then_inc(out_done, 16)
            sp.wait_ge(out_done, 16)

        @block.gpsimd
        def _(pool):
            pool.memset(ones[:, :], 1.0).then_inc(ones_set, 1)

        @block.scalar
        def _(act):
            steps = [0]

            def link(ins):
                steps[0] += 1
                ins.then_inc(act_step, 1)
                act.wait_ge(act_step, steps[0])

            act.dma_start(cst[:, :], t["shape_consts"]).then_inc(cst_in, 16)
            for name, r0, n in (("norm1_w", V_NORM1, 16), ("norm2_w", V_NORM2, 16), ("c", V_C, 8),
                                ("m_conv_w", V_CONVW, 32), ("m_conv_b", V_CONVB, 8), ("m_norm_w", V_MNORM, 8),
                                ("h_lb_logits", V_LB, 8), ("h_norm_w", V_HNORM, 8), ("g_mix_2", V_GMIX, 8),
                                ("g_mem_2", V_GMEM, 8), ("g_ffn_2", V_GFFN, 8)):
                flat = "a b c -> (a b c)" if len(t[name].shape) == 3 else "a b -> (a b)"
                act.dma_start(TS[r0:r0 + n, 1, 0:128],
                              t[name].rearrange(flat).rearrange("(r p) -> r p", p=128)).then_inc(rows_in, 16)
            act.dma_start(TS[0:96, 1, 128:256],
                          t["ada_b"].rearrange("l n -> (l n)").rearrange("(r p) -> r p", p=128)).then_inc(rows_in, 16)
            act.dma_start(X[:, :, :], t["x"][0].rearrange("(i p) n -> p i n", p=128)).then_inc(x_in, 16)
            act.wait_ge(cleared, 2)
            act.dma_start(bias8[0:8, 0:1], t["m_i_bias"].rearrange("o h -> h o")).then_inc(small_in, 16)
            act.dma_start(bias8[0:8, 1:2], t["m_f_bias"].rearrange("o h -> h o")).then_inc(small_in, 16)
            act.dma_start(bias8[0:8, 3:4], t["b_forget_2"].rearrange("o h -> h o")).then_inc(small_in, 16)
            act.dma_start(bias8[32:40, 3:4], t["b_forget_2"].rearrange("o h -> h o")).then_inc(small_in, 16)
            act.dma_start(wsm[:, :, 0:16], m_in[:, :, M_GATES:M_GATES + 16]).then_inc(small_in, 16)
            act.dma_start(wsm[:, :, 16:24], wview(t["moe_router"][0])).then_inc(small_in, 16)
            act.dma_start(wsm[:, :, 24:32], w_in2[:, :, F_LOGIT:F_LOGIT + 8]).then_inc(small_in, 16)
            act.dma_start(wsm[:, :, 56:64], w_in2[:, :, F_LOGIT:F_LOGIT + 8]).then_inc(small_in, 16)
            for j, name in enumerate(("g_q_moba_2", "g_k_moba_2", "g_q_fox_2", "g_k_fox_2")):
                act.dma_start(gains[:, A_D * j:A_D * (j + 1)], t[name].to_broadcast([128, A_D])).then_inc(small_in, 16)
            for j, name in enumerate(("g_q_mem_2", "g_k_mem_2")):
                act.dma_start(gains[:, 4 * A_D + C_D * j:4 * A_D + C_D * (j + 1)],
                              t[name].to_broadcast([128, C_D])).then_inc(small_in, 16)

            def hi(w, n=UNIT):
                s, full = w.next_raw()
                u, h = w.next_unit()
                act.wait_ge(raw_full[s], full)
                at_least(act, w_used, u - N_HL + 1)
                act.activation(whi[:, h, 0:n], raw[:, s, 0:n], ACT.Copy).then_inc(w_hi, 1)

            def his(w, k):
                for _ in range(k):
                    hi(w)

            def skip_raw(w, n):
                for _ in range(n):
                    w.next_raw()

            roots = [0]

            def root(n):
                roots[0] += 1
                act.wait_ge(root_in, roots[0])
                act.activation(rs[:, 0:n], rs[:, 0:n], ACT.Sqrt).then_inc(root_out, 1)

            def squares(src):
                for i in range(TT):
                    act.activation(AF[:, 4 * i:4 * i + 4, :].rearrange("p k t -> p (k t)"), src[:, i, :], ACT.Square,
                                   accum_out=ss[:, i:i + 1]).then_inc(sq_done, 1)
                root(2)

            def group(w, side=lambda j: None):
                first_unit, first_pb, done = w.unit, w.pb, w.hidden

                def silu(c):
                    act.wait_ge(w_used, first_unit + 2 * c + 2)
                    at_least(act, hid_done, done + c - 1)
                    n, bank = 2 * COLS[c][1], 2 * ((first_pb + c) % 4)
                    act.activation(sil[:, c % 2, 0:n], ps[:, bank, 0:n], ACT.Silu).then_inc(silu_done, 1)

                for j in range(18):
                    hi(w, JOBS[j])
                    if j < 12:
                        side(j)
                    if 3 <= j <= 13 and j % 2:
                        silu((j - 3) // 2)
                w.hidden = done + 6
                for _ in range(8):
                    w.next_pair()

            def expert_input(v, n, tiles):
                for q in range(2):
                    act.wait_ge(e_gather, n + q + 1)
                    _, bank = v.next_pair()
                    for k in range(4):
                        kk = 4 * q + k
                        c0 = SEQ * (k % 2)
                        ins = act.activation(AF[:, kk, 0:128 * tiles], ps[:, bank + k // 2, c0:c0 + 128 * tiles],
                                             ACT.Identity, bias=mod[:, 2, kk:kk + 1], scale=scl[:, kk:kk + 1])
                link(ins)
                act.activation(AH[:, :, 0:128 * tiles], AF[:, :, 0:128 * tiles], ACT.Copy).then_inc(e_high, 1)

            def expert(v, e, tiles):
                first = v.unit - LEAD
                banks = [2 * ((v.pb + i) % 4) for i in range(E_PAIRS)]

                def silu(c):
                    act.wait_ge(w_used, first + 4 * c + 2)
                    n = E_COLS[c][1]
                    act.activation(e_sil[:, c % 2, 0:tiles, 0:n], ps[:, banks[(1, 3, 6)[c]]:banks[(1, 3, 6)[c]] + tiles, 0:n],
                                   ACT.Silu).then_inc(e_silu, 1)

                def output(c):
                    act.wait_ge(w_used, first + 12 + 3 * (c + 1))
                    bank = banks[12 + c]
                    act.activation(e_out[:, 0:tiles, 512 * c:512 * c + 512], ps[:, bank:bank + tiles, :],
                                   ACT.Copy).then_inc(e_set, 1)

                for j in range(LEAD, 18 + LEAD):
                    hi(v, E_JOBS[j % 18])
                    if j in (4, 8, 12):
                        silu(j // 4 - 1)
                    if j == 14:
                        v.pb = (v.pb + 9) % 4
                        expert_input(v, 2 * e + 2, tiles)
                    if j == 17:
                        output(0)
                output(1)

            w = Walk()
            act.wait_ge(vec_set, 1)
            act.activation(cond[:, :], vec[:, V_C:V_C + 8], ACT.Silu).then_inc(cond_set, 1)
            act.wait_ge(x_in, 16)
            squares(X)
            skip_raw(w, 8)
            his(w, 12)
            act.wait_ge(conv_done, 1)
            act.activation(qk, qk, ACT.Silu).then_inc(qk_silu, 1)
            act.wait_ge(og_set, 1)
            act.activation(og, og, ACT.Sigmoid).then_inc(ogs_set, 1)
            act.wait_ge(g_vec, 1)
            act.activation(rows[:, 0, :], rows[:, 0, :], ACT.Tanh, bias=bias8[0:8, 2:3], scale=1.0 / 15.0)
            link(act.activation(rows[:, 3, :], rows[:, 2, :], ACT.Exp, scale=-1.0))
            act.activation(rows[:, 3, :], rows[:, 3, :], ACT.Ln, bias=1.0).then_inc(g_act, 1)
            act.wait_ge(g_vec, 2)
            act.activation(rows[:, 7, :], rows[:, 7, :], ACT.Exp, scale=-1.0).then_inc(g_act, 1)
            act.wait_ge(cols_set, 1)
            skip_raw(w, 16)
            for h in range(M_HEADS):
                act.wait_ge(m_sc, h + 1)
                at_least(act, m_pt, h - 1)
                bank = m_bank_s(h)
                act.activation(em[:, h % 2, 0:256], ps[:, bank, 0:256], ACT.Exp, bias=gcol[:, 0, h:h + 1], scale=-1.0)
                act.activation(em[:, h % 2, 256:384], ps[:, bank, 256:384], ACT.Exp, bias=gcol[:, 1, h:h + 1],
                               scale=-1.0).then_inc(m_exp, 1)
            act.wait_ge(heads_done, 1)
            act.activation(flatA, flatT, ACT.Square).then_inc(sq_done, 1)
            root(16)
            his(w, 4)
            act.wait_ge(x_ready, 1)
            squares(X)
            w.pair, w.pb = PAIR_FFN, PAIR_FFN % 4
            for e in range(2):
                group(w, lambda j: skip_raw(w, 1))
            act.wait_ge(x_ready, 2)
            squares(X)
            his(w, 6)
            act.wait_ge(h_raw, 1)
            act.activation(hq, hq, ACT.Silu)
            his(w, 4)
            act.wait_ge(h_raw, 2)
            act.activation(flatA, hk, ACT.Sigmoid).then_inc(h_act, 1)
            act.activation(hk, hk, ACT.Sigmoid, scale=-1.0).then_inc(h_act, 1)
            his(w, 6)
            act.wait_ge(h_vec, 1)
            act.activation(lbc[:, 0:8], lbc[:, 0:8], ACT.Exp).then_inc(h_act, 1)
            act.wait_ge(h_vec, 2)
            act.activation(flatT, flatA, ACT.Ln)
            act.activation(level_buf[2], flatA, ACT.Ln, scale=LN_SHIFT).then_inc(h_act, 1)
            act.wait_ge(og_set, 2)
            act.activation(og, og, ACT.Silu).then_inc(ogs_set, 1)
            for lev in range(LEVELS + 1):
                act.wait_ge(l_sub, lev + 1)
                act.activation(level_buf[lev % 3], level_buf[lev % 3], ACT.Exp).then_inc(l_exp, 1)
            act.wait_ge(heads_done, 2)
            act.activation(flatA, flatT, ACT.Square).then_inc(sq_done, 1)
            root(16)
            his(w, 4)
            act.wait_ge(x_ready, 3)
            squares(X)
            act.dma_start(memx, t["mem_2"][0].rearrange("(i p) n -> p i n", p=128)).then_inc(late_in, 16)
            act.dma_start(fwb, t["final_norm_w"].rearrange("(o n) -> o n", o=1).to_broadcast([128, D])).then_inc(late_in, 16)
            act.wait_ge(g_vec, 3)
            act.activation(mm2[:, 3, :], mm2[:, 2, :], ACT.Exp).then_inc(g_act, 1)
            act.wait_ge(crowd_set, 1)
            crowd = act.value_load(crowded[0:1, 0:1], min_val=0, max_val=1)
            w.pair, w.pb = PAIR_MOE - 2, (PAIR_MOE - 2) % 4
            expert_input(w, 0, TT)
            his(w, LEAD)
            w.pair = PAIR_MOE

            def experts(tiles):
                base = steps[0]
                with act.Fori(0, N_EXPERTS) as e:
                    steps[0] = base + e
                    expert(w.after_groups(e, E_PAIRS), e, tiles)
                steps[0] = base

            with act.If(crowd > 0):
                experts(TT)
            with act.Else():
                experts(1)
            steps[0] += N_EXPERTS
            w = w.after_groups(N_EXPERTS, E_PAIRS)
            act.wait_ge(x_ready, 4)
            squares(X)
            act.wait_ge(late_in, 32)
            act.wait_ge(ts_ready, 7)
            squares(memx)
            his(w, 4 - LEAD)
            act.wait_ge(x_ready, 5)
            act.wait_ge(a_ready, 2 * 7)
            squares(X)
            his(w, 14)
            act.wait_ge(g_vec, 4)
            link(act.activation(frow[:, 2, :], frow[:, 1, :], ACT.Exp, scale=-1.0))
            act.activation(frow[:, 2, :], frow[:, 2, :], ACT.Ln, bias=1.0).then_inc(g_act, 1)
            act.wait_ge(qk_raw, 1)
            for n in range(len(NORMED) + 1):
                if n < len(NORMED):
                    at_least(act, qk_ready, n - 1)
                    src = mkv[:, 0] if NORMED[n][0] is None else qkv[:, NORMED[n][0]]
                    act.activation(tok(flatA[:, 1024 * (n % 2):1024 * (n % 2) + 1024]), src, ACT.Square)\
                       .then_inc(sq_done, 1)
                if n:
                    root(2 * (512 // NORMED[n - 1][2]))
            for gh0, heads, dh, causal, fox in BRANCHES:
                for i in range(heads):
                    gh = gh0 + i
                    act.wait_ge(t_max, gh + 1)
                    at_least(act, t_tp, gh - 1)
                    bank = t_bank_s(gh)
                    n0 = 128 if causal else 256
                    for k, (c0, n) in enumerate(((0, n0), (n0, 256))):
                        ins = act.activation(prb[:, gh % 2, c0:c0 + n], ps[:, bank, c0:c0 + n], ACT.Exp,
                                             bias=nmx[:, 2 * (gh % 2) + k:2 * (gh % 2) + k + 1], scale=dh ** -0.5,
                                             accum_out=rsum[:, 2 * (gh % 2) + k:2 * (gh % 2) + k + 1])
                    ins.then_inc(t_exp, 1)
            for b in range(3):
                his(w, 4)
                act.wait_ge(b_raw, b + 1)
                act.activation(sg, sg, ACT.Sigmoid).then_inc(b_sig, 1)
                his(w, 2)
            his(w, 4)
            act.wait_ge(x_ready, 6)
            squares(X)
            w.pair, w.pb = PAIR_FFN2, PAIR_FFN2 % 4
            with act.Fori(0, 2) as e:
                group(w.after_groups(e))

        @block.tensor
        def _(pe):
            w = Walk()
            stage = [0]

            def pair(w):
                p, bank = w.next_pair()
                at_least(pe, ps_free, p - 3)
                return bank

            def three(o, sh, sl, mh, ml, first, last):
                pe.matmul(o, sh, mh, start=first, stop=False)
                pe.matmul(o, sh, ml, start=False, stop=False)
                return pe.matmul(o, sl, mh, start=False, stop=last)

            def t_unit(w, bank, n=256):
                u, h = w.next_unit()
                pe.wait_ge(w_lo, u + 1)
                wh = whi[:, h, 0:KT * n].rearrange("p (k n) -> p k n", k=KT)
                wl = wlo[:, h, 0:KT * n].rearrange("p (k n) -> p k n", k=KT)
                for f in range(n // 128):
                    for k in range(KT):
                        ins = three(ps[:, bank, SEQ * f:SEQ * (f + 1)], wh[:, k, 128 * f:128 * (f + 1)],
                                    wl[:, k, 128 * f:128 * (f + 1)], AH[:, k, :], AL[:, k, :], k == 0, k == KT - 1)
                ins.then_inc(w_used, 1)

            def m_unit(w, bank, k0, nk, kts, sh=AH, sl=AL, s0=0, n=512, tiles=TT):
                u, h = w.next_unit()
                pe.wait_ge(w_lo, u + 1)
                wh = whi[:, h, 0:nk * n].rearrange("p (k n) -> p k n", k=nk)
                wl = wlo[:, h, 0:nk * n].rearrange("p (k n) -> p k n", k=nk)
                for i in range(tiles):
                    for k in range(nk):
                        kk = k0 + k
                        ins = three(ps[:, bank + i, 0:n], sh[:, s0 + kk, 128 * i:128 * (i + 1)],
                                    sl[:, s0 + kk, 128 * i:128 * (i + 1)], wh[:, k, :], wl[:, k, :],
                                    kk == 0, kk == kts - 1)
                ins.then_inc(w_used, 1)

            def m_matrix(w, chunks, kts=KT, sh=AH, sl=AL, s0=0):
                for _ in range(chunks):
                    bank = pair(w)
                    for k0 in range(0, kts, 4):
                        m_unit(w, bank, k0, 4, kts, sh, sl, s0)

            def transposes(w):
                stage[0] += 1
                pe.wait_ge(ts_ready, stage[0])
                for q in range(2):
                    bank = pair(w)
                    for k in range(4):
                        for i in range(TT):
                            ins = pe.transpose(ps[:, bank + k // 2, SEQ * (k % 2) + 128 * i:SEQ * (k % 2) + 128 * (i + 1)],
                                               TS[:, i, 512 * q + 128 * k:512 * q + 128 * (k + 1)], ident)
                    ins.then_inc(tp_done, 1)

            def a_wait():
                pe.wait_ge(a_ready, 2 * stage[0])

            def ada_cols(bank, c0, chunk, n0, n):
                for f in range(n):
                    ins = pe.matmul(ps[:, bank, c0 + f:c0 + f + 1], acc[:, chunk, n0 + 128 * f:n0 + 128 * (f + 1)],
                                    ones[:, 0:1], start=True, stop=True)
                return ins

            def ada_rows(bank, chunk, n0):
                for c in range(2):
                    ins = pe.matmul(ps[:, bank + c, :], ones[:, 0:128], acc[:, chunk, n0 + 512 * c:n0 + 512 * (c + 1)],
                                    start=True, stop=True)
                return ins

            def ada_gates(w):
                bank = pair(w)
                ada_rows(bank, 1, 0).then_inc(ada_sum, 1)
                bank = pair(w)
                ada_cols(bank, 0, 1, 1024, 8)
                ada_cols(bank, 8, 2, 0, 8).then_inc(ada_sum, 1)
                bank = pair(w)
                ada_rows(bank, 2, 1024).then_inc(ada_sum, 1)

            def group(w):
                done = w.hidden
                for c, (_, n) in enumerate(COLS):
                    bank = pair(w)
                    t_unit(w, bank, n)
                    t_unit(w, bank + 1, n)
                for c in range(2):
                    bank = pair(w)
                    for k0, nk in KS:
                        if c == 0:
                            pe.wait_ge(hid_done, done + min(6, (k0 + nk + 1) // 2))
                        m_unit(w, bank, k0, nk, FT, HH, HL)
                w.hidden = done + 6

            def gather(w, tiles):
                for q in range(2):
                    bank = pair(w)
                    for k in range(4):
                        for i in range(TT):
                            ins = pe.matmul(ps[:, bank + k // 2, SEQ * (k % 2):SEQ * (k % 2) + 128 * tiles],
                                            TS[:, i, 512 * q + 128 * k:512 * q + 128 * (k + 1)],
                                            chosen[:, i, 0:128 * tiles], start=i == 0, stop=i == TT - 1)
                    ins.then_inc(e_gather, 1)

            def expert(w, e, tiles):
                def hidden_tp(bank, c):
                    pe.wait_ge(e_prod, 3 * e + c + 1)
                    for b in range(E_COLS[c][1] // 128):
                        for j in range(tiles):
                            c0 = SEQ * (b % 2) + 128 * j
                            ins = pe.transpose(ps[:, bank + b // 2, c0:c0 + 128],
                                               e_hid[:, c % 2, j, 128 * b:128 * (b + 1)], ident)
                    ins.then_inc(e_tp, 1)

                bank = pair(w)
                for i in range(TT):
                    for j in range(tiles):
                        ins = pe.transpose(ps[:, bank, SEQ * j + 128 * i:SEQ * j + 128 * (i + 1)],
                                           chosen[:, i, 128 * j:128 * (j + 1)], ident)
                ins.then_inc(place_tp, 1)
                pe.wait_ge(e_in, e + 1)
                for c, (_, n) in enumerate(E_COLS):
                    for _ in range(2):
                        bank = pair(w)
                        for k0 in (0, 4):
                            m_unit(w, bank, k0, 4, KT, n=n, tiles=tiles)
                    if c:
                        hidden_tp(pair(w), c - 1)
                pe.wait_ge(pick_set, e + 2)
                gather(w, tiles)
                tp_bank, bank = pair(w), pair(w)
                for c in range(2):
                    if c:
                        bank = pair(w)
                    for k0, nk in KS:
                        if c == 0:
                            pe.wait_ge(e_hidden, 3 * e + 1 + k0 // 4)
                        m_unit(w, bank, k0, nk, FT, HH, HL, tiles=tiles)
                        if c == 0 and k0 == 0:
                            hidden_tp(tp_bank, 2)
                pe.wait_ge(place_set, e + 1)
                for c in range(2):
                    bank = pair(w)
                    pe.wait_ge(e_set, 2 * e + c + 1)
                    for i in range(TT):
                        for j in range(tiles):
                            ins = pe.matmul(ps[:, bank + i, :], place[:, j, 128 * i:128 * (i + 1)],
                                            e_out[:, j, 512 * c:512 * c + 512], start=j == 0, stop=j == tiles - 1)
                    ins.then_inc(e_back, 1)

            pe.wait_ge(cst_in, 16)
            pe.wait_ge(rows_in, 12 * 16)
            bank = pair(w)
            pe.transpose(ps[:, bank, 0:128], TS[:, 1, 0:128], ident)
            pe.transpose(ps[:, bank + 1, 0:96], TS[0:96, 1, 128:256], cst[0:96, C_ID:C_ID + 96]).then_inc(rows_t, 1)
            pe.wait_ge(ones_set, 1)
            pe.wait_ge(ada_used, 8)
            bank = pair(w)
            ada_cols(bank, 0, 0, 0, 16).then_inc(ada_sum, 1)
            transposes(w)
            a_wait()
            for _ in range(2):
                bank = pair(w)
                t_unit(w, bank)
                t_unit(w, bank + 1)
            m_matrix(w, 4)
            pe.wait_ge(small_in, 14 * 16)
            bank = pair(w)
            for g in range(2):
                for k in range(KT):
                    ins = pe.matmul(ps[0:8, bank + g, 0:SEQ], wsm[:, k, 8 * g:8 * g + 8], AF[:, k, :],
                                    start=k == 0, stop=k == KT - 1)
            ins.then_inc(small_mm, 1)
            pe.wait_ge(g_act, 2)
            bank = pair(w)
            for r, row in ((0, 5), (1, 7)):
                for i in range(TT):
                    ins = pe.transpose(ps[:, bank, 16 * r + 8 * i:16 * r + 8 * i + 8], rows[:, row, 128 * i:128 * (i + 1)],
                                       cst[0:8, C_ID:C_ID + 8])
            ins.then_inc(col_tp, 1)
            pe.wait_ge(consts_set, 1)
            pe.wait_ge(qk_silu, 1)
            pe.wait_ge(ps_free, w.pair)
            for step in range(M_HEADS + 1):
                if step < M_HEADS:
                    h = step
                    bank = pair(w)
                    assert bank == m_bank_s(h)
                    ro, kt = 64 * (h % 2), h // 2
                    pick = cst[0:8, C_ID + h:C_ID + h + 1].to_broadcast([8, 128])
                    M = rows[:, 6, :]
                    pe.matmul(ps[:, bank, 0:256], pick, M, start=True, stop=False)
                    pe.matmul(ps[:, bank, 0:128], identb[:, :], maskb[:, 1, :], start=False, stop=True)
                    pe.matmul(ps[:, bank, 256:384], pick, M[:, 128:256], start=True, stop=False)
                    pe.matmul(ps[:, bank, 256:384], identb[:, :], maskb[:, 1, :], start=False, stop=True)
                    q, k = qk[ro:ro + 64, kt, :], qk[ro:ro + 64, 4 + kt, :]
                    pe.matmul(ps[:, bank + 1, 0:256], k[:, 0:128], q, start=True, stop=True)
                    pe.matmul(ps[:, bank + 1, 256:384], k[:, 128:256], q[:, 128:256], start=True, stop=True)\
                      .then_inc(m_sc, 1)
                if step >= 1:
                    h = step - 1
                    bank = pair(w)
                    pe.wait_ge(m_pt, h + 1)
                    p = pt[:, h % 2, :]
                    pe.matmul(ps[:, bank, 0:129], p[:, 0:128], vx[:, 0, h, :], start=True, stop=True)
                    pe.matmul(ps[:, bank, 256:385], p[:, 128:256], vx[:, 0, h, :], start=True, stop=False)
                    pe.matmul(ps[:, bank, 256:385], p[:, 256:384], vx[:, 1, h, :], start=False, stop=True)\
                      .then_inc(m_o, 1)
            transposes(w)
            pe.wait_ge(ada_used, 24)
            ada_gates(w)
            a_wait()
            m_matrix(w, 2)
            transposes(w)
            a_wait()
            assert w.pair == PAIR_FFN
            for e in range(2):
                group(w)
            pe.wait_ge(ada_used, 48)
            bank = pair(w)
            ada_cols(bank, 0, 0, 0, 16).then_inc(ada_sum, 1)
            ada_gates(w)
            transposes(w)
            a_wait()
            for _ in range(4):
                bank = pair(w)
                t_unit(w, bank)
                t_unit(w, bank + 1)
            m_matrix(w, 4)
            for lev in range(-1, LEVELS + 1):
                n = lev + 1
                if lev < LEVELS:
                    pe.wait_ge(l_kq, n + 1)
                    lhs = rhs = level_buf[n % 3].rearrange("p (g t) -> p g t", g=16)
                else:
                    lhs, rhs = (a.rearrange("p (g t) -> p g t", g=16) for a in (hk, hq))
                for half_ in range(1 if lev < 0 else 2):
                    bank = pair(w)
                    for g in range(8):
                        if lev < 0:
                            l_ap, r_ap = lhs[:, 2 * g, :], rhs[:, 2 * g + 1, :]
                        else:
                            l_ap, r_ap = lhs[:, 8 * half_ + g, :], rhs[:, 8 * half_ + g, :]
                        ins = pe.matmul(ps[:, bank + g // 4, 128 * (g % 4):128 * (g % 4) + 128], l_ap, r_ap,
                                        start=True, stop=True)
                    ins.then_inc(l_mm, 1)
            for i in range(TT):
                bank = pair(w)
                if i == 0:
                    pe.wait_ge(ps_free, w.pair - 1)
                for h in range(H_HEADS):
                    o = ps[:, bank + h // 4, 128 * (h % 4):128 * (h % 4) + 128]
                    ins = pe.matmul(o, at[:, 2 * h + i, :], hv[:, i, 128 * h:128 * h + 128], start=True, stop=i == 0)
                    if i:
                        ins = pe.matmul(o, ax[:, h, :], hv[:, 0, 128 * h:128 * h + 128], start=False, stop=True)
                ins.then_inc(h_o, 1)
            transposes(w)
            a_wait()
            m_matrix(w, 2)
            transposes(w)
            a_wait()
            bank = pair(w)
            for i in range(TT):
                for k in range(KT):
                    ins = pe.matmul(ps[:, bank, 8 * i:8 * i + 8], AF[:, k, 128 * i:128 * (i + 1)], wsm[:, k, 16:24],
                                    start=k == 0, stop=k == KT - 1)
            ins.then_inc(small_mm, 1)
            pe.wait_ge(tokens_set, 1)
            bank = pair(w)
            for i in range(TT):
                if i:
                    pe.matmul(ps[:, bank, 8:16], ones[:, 0:128], oh[:, 0, 0, :], start=True, stop=False)
                pe.matmul(ps[:, bank, 8 * i:8 * i + 8], upto, oh[:, 0, i, :], start=i == 0, stop=True)
            for i in range(TT):
                ins = pe.matmul(ps[:, bank, 16:24], ones[:, 0:128], oh[:, 0, i, :], start=i == 0, stop=i == TT - 1)
            ins.then_inc(small_mm, 1)
            pe.wait_ge(crowd_set, 1)
            crowd = pe.value_load(crowded[0:1, 0:1], min_val=0, max_val=1)
            pe.wait_ge(pick_set, 1)
            gather(w, TT)
            assert w.pair == PAIR_MOE

            def experts(tiles):
                with pe.Fori(0, N_EXPERTS) as e:
                    expert(w.after_groups(e, E_PAIRS), e, tiles)

            with pe.If(crowd > 0):
                experts(TT)
            with pe.Else():
                experts(1)
            w = w.after_groups(N_EXPERTS, E_PAIRS)
            stage[0] += 1
            transposes(w)
            a_wait_n = 2 * 7
            pe.wait_ge(a_ready, a_wait_n)
            m_matrix(w, 2)
            transposes(w)
            pe.wait_ge(a_ready, a_wait_n + 2)
            m_matrix(w, 7)
            bank = pair(w)
            for k in range(KT):
                ins = pe.matmul(ps[0:40, bank, 0:SEQ], wsm[:, k, 24:64], AF[:, k, :], start=k == 0, stop=k == KT - 1)
            ins.then_inc(small_mm, 1)
            for b in range(3):
                for which in range(2):
                    src = mkv[:, 0] if (b, which) == (2, 1) else qkv[:, (0, 3, 6)[b] + which]
                    pe.wait_ge(qk_ready, 2 * b + which + 1)
                    bank = pair(w)
                    for k in range(4):
                        for i in range(TT):
                            ins = pe.transpose(ps[:, bank + k // 2, SEQ * (k % 2) + 128 * i:SEQ * (k % 2) + 128 * (i + 1)],
                                               src[:, i, 128 * k:128 * (k + 1)], ident)
                    ins.then_inc(tp_done, 1)
            pe.wait_ge(qk_set, 6)
            pe.wait_ge(fox_set, 1)
            for b, (gh0, heads, dh, causal, fox) in enumerate(BRANCHES):
                per = 128 // dh
                qT = acc[:, b, 0:1024].rearrange("p (k t) -> p k t", k=4)
                kT = acc[:, b, 1024:2048].rearrange("p (k t) -> p k t", k=4)
                s_bank = {}
                o_bank = {}
                n0 = 128 if causal else 256
                for step in range(heads + 2):
                    if step < heads:
                        h = step
                        s_bank[h] = bank = pair(w)
                        assert bank == t_bank_s(gh0 + h)
                        ro, kt = dh * (h % per), h // per
                        q, k = qT[ro:ro + dh, kt, :], kT[ro:ro + dh, kt, :]
                        for i, (c0, n) in enumerate(((0, n0), (n0, 256))):
                            o = ps[:, bank, c0:c0 + n]
                            ins = pe.matmul(o, q[:, 128 * i:128 * (i + 1)], k[:, 0:n], start=True, stop=not causal)
                            if fox:
                                pe.matmul(o, fox_l[:, h, 128 * i:128 * (i + 1)], fox_r[:, 0:n], start=False, stop=False)
                            if causal:
                                ins = pe.matmul(ps[:, bank, c0 + n - 128:c0 + n], identb[:, :], maskb[:, 0, :],
                                                start=False, stop=True)
                        ins.then_inc(t_s, 1)
                    if 1 <= step <= heads:
                        h = step - 1
                        bank = s_bank[h] + 1
                        pe.wait_ge(t_p, gh0 + h + 1)
                        p = prb[:, (gh0 + h) % 2, :]
                        cuts = ((0, 0), (128, 128), (256, 256)) if causal else ((0, 0), (256, 128), (128, 256), (384, 384))
                        for c_in, c_out in cuts:
                            ins = pe.transpose(ps[:, bank, c_out:c_out + 128], p[:, c_in:c_in + 128], ident)
                        ins.then_inc(t_tp, 1)
                    if step >= 2:
                        h = step - 2
                        ro, kt = dh * (h % per), h // per
                        if kt not in o_bank:
                            o_bank[kt] = pair(w)
                        bank = o_bank[kt]
                        pe.wait_ge(t_pt, gh0 + h + 1)
                        p = pts[:, (gh0 + h) % 2, :]
                        v = mkv[:, 1] if b == 2 else qkv[:, 3 * b + 2]
                        q0 = 128 if causal else 0
                        pe.matmul(ps[ro:ro + dh, bank, 0:256], v[:, 0, dh * h:dh * (h + 1)], p[:, 0:256],
                                  start=True, stop=False)
                        pe.matmul(ps[ro:ro + dh, bank, q0:256], v[:, 1, dh * h:dh * (h + 1)], p[:, 256:512 - q0],
                                  start=False, stop=True).then_inc(t_o, 1)
            pe.wait_ge(t_y, 12)
            for b in range(3):
                m_matrix(w, 2)
                m_matrix(w, 2, 4, HH, HL, 4 * b)
            pe.wait_ge(ts_ready, 10)
            for q in range(2):
                bank = pair(w)
                for k in range(4):
                    for i in range(TT):
                        ins = pe.transpose(ps[:, bank + k // 2, SEQ * (k % 2) + 128 * i:SEQ * (k % 2) + 128 * (i + 1)],
                                           TS[:, i, 512 * q + 128 * k:512 * q + 128 * (k + 1)], ident)
                ins.then_inc(tp_done, 1)
            pe.wait_ge(a_ready, 18)
            m_matrix(w, 2)
            stage[0] = 10
            transposes(w)
            pe.wait_ge(a_ready, 20)
            assert w.pair == PAIR_FFN2 and w.pb == PAIR_FFN2 % 4
            with pe.Fori(0, 2) as e:
                group(w.after_groups(e))

        @block.vector
        def _(dve):
            steps = [0]

            def link(ins):
                steps[0] = steps[0] + 1
                ins.then_inc(vec_step, 1)
                dve.wait_ge(vec_step, steps[0])

            def both(ins, s, n):
                ins.then_inc(s, 1)
                dve.wait_ge(s, n)

            def free(w, ins):
                w.next_pair()
                ins.then_inc(ps_free, 1)
                dve.wait_ge(ps_free, w.pair)

            def bank_of(w):
                return 2 * w.pb

            def lo(w, n=UNIT):
                s, _ = w.next_raw()
                u, h = w.next_unit()
                dve.wait_ge(w_hi, u + 1)
                dve.tensor_tensor(wlo[:, h, 0:n], raw[:, s, 0:n], whi[:, h, 0:n].bitcast(fp), ALU.subtract)\
                   .then_inc(w_lo, 1)

            def los(w, k):
                for _ in range(k):
                    lo(w)

            def ada_unit(w, layer, chunk, k):
                if k == 0:
                    dve.tensor_tensor(acc[:, chunk, :].rearrange("p (f n) -> p f n", f=16),
                                      ident.rearrange("p (o n) -> p o n", o=1).to_broadcast([128, 16, 128]),
                                      adab[:, 48 * layer + 16 * chunk:48 * layer + 16 * chunk + 16]
                                      .rearrange("p (f o) -> p f o", o=1).to_broadcast([128, 16, 128]),
                                      ALU.mult).then_inc(ada_init, 1)
                    dve.wait_ge(ada_init, 3 * layer + chunk + 1)
                s, full = w.next_raw()
                at_least(dve, ada_used, w.ada)
                dve.wait_ge(raw_full[s], full)
                dve.scalar_tensor_tensor(acc[:, chunk, :], raw[:, s, :], cond[:, k:k + 1], acc[:, chunk, :],
                                         ALU.mult, ALU.add).then_inc(ada_used, 1)
                w.ada += 1

            def root(n, width):
                m, y, s = ms[:, 0:n], rs[:, 0:n], nt[:, 0:n]
                link(dve.tensor_scalar(m, ss[:, 0:n], 1.0 / width, EPS, ALU.mult, ALU.add))
                dve.reciprocal(y, m).then_inc(root_in, 1)
                counts["root"] += 1
                dve.wait_ge(root_out, counts["root"])
                link(dve.tensor_tensor(s, y, y, ALU.mult))
                link(dve.tensor_tensor(s, s, m, ALU.mult))
                link(dve.tensor_scalar(s, s, -0.5, 1.5, ALU.mult, ALU.add))
                link(dve.tensor_tensor(y, y, s, ALU.mult))

            counts = dict(root=0, sq=0, ts=0, tp=0, a=0)

            def normalise(src):
                counts["sq"] += 2
                dve.wait_ge(sq_done, counts["sq"])
                root(2, D)
                for i in range(TT):
                    ins = dve.tensor_scalar(TS[:, i, :], src[:, i, :], rs[:, i:i + 1], None, ALU.mult)
                counts["ts"] += 1
                ins.then_inc(ts_ready, 1)

            def to_features(w, scale=None, shift=None):
                for q in range(2):
                    counts["tp"] += 1
                    dve.wait_ge(tp_done, counts["tp"])
                    bank = bank_of(w)
                    for k in range(4):
                        kk = 4 * q + k
                        src = ps[:, bank + k // 2, SEQ * (k % 2):SEQ * (k % 2) + SEQ]
                        if scale is None:
                            ins = dve.tensor_copy(AF[:, kk, :], src)
                        elif shift is None:
                            ins = dve.tensor_scalar(AF[:, kk, :], src, scale[:, kk:kk + 1], None, ALU.mult)
                        else:
                            ins = dve.tensor_scalar(AF[:, kk, :], src, scale[:, kk:kk + 1], shift[:, kk:kk + 1],
                                                    ALU.mult, ALU.add)
                    free(w, ins)
                    half_ = slice(4 * q, 4 * q + 4)
                    link(dve.tensor_copy(AH[:, half_, :], AF[:, half_, :]))
                    dve.tensor_tensor(AL[:, half_, :], AF[:, half_, :], AH[:, half_, :].bitcast(fp), ALU.subtract)\
                       .then_inc(a_ready, 1)
                    counts["a"] += 1
                dve.wait_ge(a_ready, counts["a"])

            def norm_scale(scale_cols, norm_cols):
                link(dve.scalar_tensor_tensor(scl, scale_cols, 1.0, norm_cols, ALU.add, ALU.mult))

            def head_norm(w, norm_cols):
                counts["sq"] += 1
                dve.wait_ge(sq_done, counts["sq"])
                link(dve.tensor_reduce(ss, flatA.rearrange("p (g n) -> p g n", g=16), AX.X, ALU.add))
                root(16, M_DV)
                dve.wait_ge(ogs_set, 1 if norm_cols == V_MNORM else 2)
                link(dve.tensor_tensor(flatT.rearrange("p (g n) -> p g n", g=16),
                                       flatT.rearrange("p (g n) -> p g n", g=16),
                                       rs.rearrange("p (g o) -> p g o", o=1).to_broadcast([128, 16, 128]), ALU.mult))
                counts["ts"] += 1
                dve.tensor_tensor(TS[:, :, :], TS[:, :, :], og, ALU.mult).then_inc(ts_ready, 1)

            def out_matrix(w, n_ready):
                for c in range(2):
                    los(w, 2)
                    dve.wait_ge(w_used, w.unit)
                    bank = bank_of(w)
                    cut = slice(512 * c, 512 * c + 512)
                    tmp = tok(flatA[:, 1024 * c:1024 * c + 1024])
                    for i in range(TT):
                        ins = dve.tensor_tensor(tmp[:, i, :], ps[:, bank + i, :], GB[:, 0, cut], ALU.mult)
                    free(w, ins)
                    ins = dve.tensor_tensor(X[:, :, cut], X[:, :, cut], tmp, ALU.add)
                both(ins, x_ready, n_ready)

            def ada_gates(w, n):
                for g in range(3):
                    dve.wait_ge(ada_sum, n + g)
                    bank = bank_of(w)
                    if g == 1:
                        ins = dve.tensor_copy(mod[:, 2:4, :], ps[:, bank, 0:16].rearrange("p (a k) -> p a k", a=2))
                    else:
                        ins = dve.tensor_copy(GB[:, g // 2, :].rearrange("p (b n) -> p b n", b=2), ps[:, bank:bank + 2, :])
                    free(w, ins)

            def evac_t(w, c, done):
                dve.wait_ge(silu_done, done + c + 1)
                bank = bank_of(w)
                n = 2 * COLS[c][1]
                free(w, dve.tensor_tensor(hid[:, c % 2, 0:n], sil[:, c % 2, 0:n], ps[:, bank + 1, 0:n], ALU.mult))
                hh = HH[:, 2 * c:2 * c + n // SEQ, :].rearrange("p k t -> p (k t)")
                hl = HL[:, 2 * c:2 * c + n // SEQ, :].rearrange("p k t -> p (k t)")
                link(dve.tensor_copy(hh, hid[:, c % 2, 0:n]))
                dve.tensor_tensor(hl, hid[:, c % 2, 0:n], hh.bitcast(fp), ALU.subtract).then_inc(hid_done, 1)

            def evac_d(w, first_unit, c):
                dve.wait_ge(w_used, first_unit + 12 + 3 * (c + 1))
                bank = bank_of(w)
                cut = slice(512 * c, 512 * c + 512)
                for i in range(TT):
                    ins = dve.scalar_tensor_tensor(Y[:, i, cut], ps[:, bank + i, :], gcur[:, i:i + 1], Y[:, i, cut],
                                                   ALU.mult, ALU.add)
                free(w, ins)

            def group_from(w, first, first_unit, done, side):
                for j in range(first, 18):
                    lo(w, JOBS[j])
                    if j < 12:
                        side(j)
                    if 3 <= j <= 13 and j % 2:
                        evac_t(w, (j - 3) // 2, done)
                evac_d(w, first_unit, 0)

            def groups(w, n, gate=None, side=lambda e, j: None, loop=False):
                LINKS = 6 + (gate is not None)
                first_unit, done = w.unit, w.hidden
                for j in range(2):
                    lo(w, JOBS[j])
                    side(0, j)

                def rest(w, e, first_unit, done):
                    if gate is not None:
                        gate(e)
                    group_from(w, 2, first_unit, done, lambda j: side(e, j))

                def next_start(w, e):
                    for j in range(2):
                        lo(w, JOBS[j])
                        side(e, j)

                if loop:
                    base = steps[0]
                    with dve.Fori(0, n - 1) as e:
                        v = w.after_groups(e)
                        steps[0] = base + e * LINKS
                        rest(v, e, first_unit + e * 18, done + e * 6)
                        next_start(v, e)
                        evac_d(v, first_unit + e * 18, 1)
                    steps[0] = base + (n - 1) * LINKS
                    w = w.after_groups(n - 1)
                else:
                    for e in range(n - 1):
                        rest(w, e, first_unit + e * 18, done + e * 6)
                        next_start(w, e + 1)
                        evac_d(w, first_unit + e * 18, 1)
                e = n - 1
                rest(w, e, first_unit + e * 18, done + e * 6)
                evac_d(w, first_unit + e * 18, 1)
                w.hidden = done + 6 * n
                return w

            w = Walk()
            dve.memset(wsm[:, :, :], 0.0).then_inc(cleared, 1)
            dve.memset(col[:, :], 0.0).then_inc(cleared, 1)
            dve.memset(vx[:, :, :, 128:129].rearrange("p i h o -> p (i h) o"), 1.0)
            dve.wait_ge(cleared, 2)
            dve.memset(ones2, 1.0)
            dve.wait_ge(cst_in, 16)
            dve.tensor_copy(identb[:, :], ident)
            dve.tensor_copy(maskb[:, :, :], cst[:, C_CAUSAL:C_CAUSAL + 256].rearrange("p (a n) -> p a n", a=2))\
               .then_inc(consts_set, 1)
            dve.wait_ge(rows_t, 1)
            dve.tensor_copy(vec[:, :], ps[:, 0, 0:128]).then_inc(vec_set, 1)
            free(w, dve.tensor_copy(adab[:, :], ps[:, 1, 0:96]))
            dve.wait_ge(cond_set, 1)
            for k in range(KT):
                ada_unit(w, 0, 0, k)
            dve.wait_ge(ada_sum, 1)
            free(w, dve.tensor_copy(mod[:, 0:2, :], ps[:, 2, 0:16].rearrange("p (a k) -> p a k", a=2)))
            norm_scale(mod[:, 1, :], vec[:, V_NORM1:V_NORM1 + 8])
            normalise(X)
            to_features(w, scl, mod[:, 0, :])
            dve.wait_ge(small_in, 14 * 16)
            link(dve.tensor_scalar(bias8[0:8, 2:3], bias8[0:8, 0:1], 1.0 / 15.0, None, ALU.mult))
            los(w, 2)
            for q in range(2):
                los(w, 2)
                dve.wait_ge(w_used, 2 * q + 2)
                bank = bank_of(w)
                for tap in range(CONV_K):
                    for k in range(4):
                        kk = 4 * q + k
                        x_ = ps[:, bank + k // 2, SEQ * (k % 2):SEQ * (k % 2) + SEQ - tap]
                        wc = vec[:, V_CONVW + 8 * (CONV_K - 1 - tap) + kk:V_CONVW + 8 * (CONV_K - 1 - tap) + kk + 1]
                        if tap == 0:
                            ins = dve.tensor_scalar(qk[:, kk, :], x_, wc, vec[:, V_CONVB + kk:V_CONVB + kk + 1],
                                                    ALU.mult, ALU.add)
                        else:
                            ins = dve.scalar_tensor_tensor(qk[:, kk, tap:], x_, wc, qk[:, kk, tap:], ALU.mult, ALU.add)
                    if tap < CONV_K - 1:
                        link(ins)
                free(w, ins)
            dve.sem_inc(conv_done, 1)
            for c in range(4):
                if c < 3:
                    los(w, 2)
                dve.wait_ge(w_used, 4 + 2 * c + 2)
                bank = bank_of(w)
                cc = c % 2
                for i in range(TT):
                    if c < 2:
                        ins = dve.tensor_copy(vx[:, i, 4 * cc:4 * cc + 4, 0:128],
                                              ps[:, bank + i, :].rearrange("p (h n) -> p h n", h=4))
                    else:
                        ins = dve.tensor_copy(og[:, i, 512 * cc:512 * cc + 512], ps[:, bank + i, :])
                free(w, ins)
            dve.sem_inc(og_set, 1)
            dve.wait_ge(small_mm, 1)
            bank = bank_of(w)
            dve.tensor_copy(rows[:, 0, :], ps[0:8, bank, 0:SEQ])
            free(w, dve.tensor_scalar(rows[:, 1, :], ps[0:8, bank + 1, 0:SEQ], bias8[0:8, 1:2], None, ALU.add))
            dve.scalar_tensor_tensor(rows[:, 2, :], rows[:, 1, :], -1.0, rows[:, 1, :], ALU.mult, ALU.max).then_inc(g_vec, 1)
            dve.wait_ge(g_act, 1)
            link(dve.scalar_tensor_tensor(rows[:, 4, :], rows[:, 1, :], 0.0, rows[:, 3, :], ALU.min, ALU.subtract))
            link(dve.tensor_tensor_scan(rows[:, 2, :], ones[0:8, :], rows[:, 4, :], 0.0, ALU.mult, ALU.add))
            link(dve.scalar_tensor_tensor(rows[:, 5, :], rows[:, 0, :], 15.0, rows[:, 2, :], ALU.mult, ALU.subtract))
            link(dve.tensor_tensor_scan(rows[:, 6, :], ones[0:8, :], rows[:, 5, :], 0.0, ALU.mult, ALU.max))
            dve.tensor_tensor(rows[:, 7, :], rows[:, 2, :], rows[:, 6, :], ALU.add).then_inc(g_vec, 1)
            dve.wait_ge(col_tp, 1)
            bank = bank_of(w)
            free(w, dve.tensor_copy(col[:, 48:80], ps[:, bank, 0:32]))
            dve.sem_inc(cols_set, 1)
            for step in range(M_HEADS + 1):
                if step < M_HEADS:
                    h = step
                    dve.wait_ge(m_exp, h + 1)
                    at_least(dve, m_o, h - 1)
                    bank = bank_of(w)
                    w.next_pair()
                    dve.scalar_tensor_tensor(pt[:, h % 2, :], ps[:, bank + 1, 0:384], M_DQK ** -0.5, em[:, h % 2, :],
                                             ALU.mult, ALU.mult).then_inc(m_pt, 1)
                    dve.wait_ge(m_pt, h + 1)
                    dve.sem_inc(ps_free, 1)
                if step >= 1:
                    h = step - 1
                    dve.wait_ge(m_o, h + 1)
                    bank = bank_of(w)
                    d = dcol[:, 8 + 2 * (h % 2):10 + 2 * (h % 2)]
                    link(dve.scalar_tensor_tensor(d, ps[:, bank, 128:512:256], -1.0, ecol[:, :, h], ALU.mult, ALU.max))
                    link(dve.tensor_tensor(d, ps[:, bank, 128:512:256], d, ALU.max))
                    link(dve.reciprocal(d, d))
                    for i in range(TT):
                        ins = dve.tensor_scalar(TS[:, i, 128 * h:128 * h + 128], ps[:, bank, 256 * i:256 * i + 128],
                                                d[:, i:i + 1], None, ALU.mult)
                    free(w, ins)
                    for k in range(2 * h, 2 * h + 2):
                        ada_unit(w, 0, 1 + k // 8, k % 8)
            dve.sem_inc(heads_done, 1)
            head_norm(w, V_MNORM)
            to_features(w, vec[:, V_MNORM:V_MNORM + 8])
            ada_gates(w, 2)
            out_matrix(w, 1)
            norm_scale(mod[:, 3, :], vec[:, V_NORM2:V_NORM2 + 8])
            normalise(X)
            to_features(w, scl, mod[:, 2, :])
            dve.memset(Y, 0.0)
            link(dve.tensor_copy(gcur, ones2))
            w = groups(w, 2, side=lambda e, j: ada_unit(w, 1, (12 * e + j) // 8, (12 * e + j) % 8))

            def add_layer(n_ready, gate_row=None, s=x_ready):
                if gate_row is not None:
                    for i in range(TT):
                        ins = dve.tensor_tensor(Y[:, i, :], Y[:, i, :], gate_row, ALU.mult)
                    link(ins)
                both(dve.tensor_tensor(X[:, :, :], X[:, :, :], Y, ALU.add), s, n_ready)

            add_layer(2, GB[:, 1, :])
            dve.wait_ge(ada_sum, 5)
            bank = bank_of(w)
            free(w, dve.tensor_copy(mod[:, 0:2, :], ps[:, bank, 0:16].rearrange("p (a k) -> p a k", a=2)))
            ada_gates(w, 6)
            norm_scale(mod[:, 1, :], vec[:, V_NORM1 + 8:V_NORM1 + 16])
            normalise(X)
            to_features(w, scl, mod[:, 0, :])
            first_unit = w.unit
            los(w, 2)
            for q in range(4):
                los(w, 2)
                dve.wait_ge(w_used, first_unit + 2 * q + 2)
                bank = bank_of(w)
                dst = (hq if q < 2 else hk)[:, 1024 * (q % 2):1024 * (q % 2) + 1024]
                free(w, dve.tensor_copy(dst.rearrange("p (b n) -> p b n", b=2), ps[:, bank:bank + 2, :]))
                if q % 2:
                    dve.sem_inc(h_raw, 1)
            for c in range(4):
                if c < 3:
                    los(w, 2)
                dve.wait_ge(w_used, first_unit + 8 + 2 * c + 2)
                bank = bank_of(w)
                dst = (hv if c < 2 else og)[:, :, 512 * (c % 2):512 * (c % 2) + 512]
                free(w, dve.tensor_copy(dst, ps[:, bank:bank + 2, :]))
            dve.sem_inc(og_set, 1)
            dve.tensor_tensor(lbc[:, 0:8], vec[:, V_LB:V_LB + 8], vec[:, V_LB:V_LB + 8], ALU.subtract)\
               .then_inc(h_vec, 1)
            dve.wait_ge(h_act, 3)
            link(dve.reciprocal(lbc[:, 8:16], lbc[:, 0:8]))
            link(dve.tensor_tensor(lbc[:, 0:8], lbc[:, 0:8], lbc[:, 8:16], ALU.mult))
            link(dve.tensor_tensor(lbc[:, 0:8], lbc[:, 0:8], lbc[:, 0:8], ALU.subtract))
            link(dve.tensor_scalar(lbc[:, 8:16], lbc[:, 0:8], -1.0, 1.0, ALU.mult, ALU.add))
            for k in range(KT):
                cut = slice(SEQ * k, SEQ * (k + 1))
                dve.tensor_scalar(hk[:, cut], hk[:, cut], lbc[:, 8 + k:9 + k], None, ALU.mult)
                ins = dve.tensor_scalar(flatA[:, cut], flatA[:, cut], lbc[:, 8 + k:9 + k], lbc[:, k:k + 1],
                                        ALU.mult, ALU.add)
            link(ins)
            both(dve.tensor_scalar(flatA, flatA, F_FLOOR, None, ALU.max), h_vec, 2)
            dve.wait_ge(h_act, 4)
            kq = level_buf[2]
            dve.tensor_scalar(flatA, flatA, 2.0 ** -40, None, ALU.is_lt)
            link(dve.tensor_scalar(kq, kq, float(np.log(LN_SHIFT)), None, ALU.subtract))
            link(dve.copy_predicated(flatT, flatA.bitcast(i32), kq))
            dve.memset(at, 0.0)
            link(dve.memset(kq, 1.0))
            link(dve.memset(kq.rearrange("p (g n) -> p g n", g=16)[:, :, 0:1], 0.0))
            link(dve.tensor_tensor_scan(hb, kq, flatT, 0.0, ALU.mult, ALU.add))

            def halves(a, blk):
                v = a.rearrange("p (n two b) -> p n two b", two=2, b=blk)
                return v[:, :, 0, :], v[:, :, 1, :]

            def sub(n):
                blk = 128 >> n
                left, right = halves(level_buf[n % 3], blk)
                bl, br = halves(hb, blk)
                ref = bl[:, :, blk - 1:blk].to_broadcast([128, 1024 // blk, blk])
                dve.tensor_tensor(left, ref, bl, ALU.subtract)
                if n == 0:
                    dve.tensor_copy(right, br).then_inc(l_sub, 1)
                else:
                    dve.tensor_tensor(right, br, ref, ALU.subtract).then_inc(l_sub, 1)

            mm_count = 0
            sub(0)
            for n in range(LEVELS + 2):
                if n < LEVELS:
                    sub(n + 1)
                if n <= LEVELS:
                    dve.wait_ge(l_exp, n + 1)
                    blk = 128 >> n
                    left, right = halves(level_buf[n % 3], blk)
                    dve.tensor_tensor(left, left, halves(hk, blk)[0], ALU.mult)
                    dve.tensor_tensor(right, right, halves(hq, blk)[1], ALU.mult).then_inc(l_kq, 1)
                for m in ([n - 1] if n <= LEVELS else [n - 1, n]):
                    if m < 0:
                        continue
                    for half_ in range(1 if m == 0 else 2):
                        mm_count += 1
                        dve.wait_ge(l_mm, mm_count)
                        bank = bank_of(w)
                        src = ps[:, bank:bank + 2, :]
                        if m == 0:
                            ins = dve.tensor_copy(ax.rearrange("p (b h) n -> p b (h n)", b=2), src)
                        else:
                            c0 = C_LEVEL + 128 * (m - 1)
                            mask = cst[:, c0:c0 + 128].bitcast(i32).rearrange("p (o n) -> p o n", o=1)\
                                .to_broadcast([128, 8, 128])
                            ins = dve.copy_predicated(at[:, 8 * half_:8 * half_ + 8, :], mask,
                                                      src.rearrange("p b (g n) -> p (b g) n", g=4))
                        free(w, ins)
            for i in range(TT):
                dve.wait_ge(h_o, i + 1)
                bank = bank_of(w)
                free(w, dve.tensor_copy(TS[:, i, :].rearrange("p (b n) -> p b n", b=2), ps[:, bank:bank + 2, :]))
            dve.sem_inc(heads_done, 1)
            head_norm(w, V_HNORM)
            to_features(w, vec[:, V_HNORM:V_HNORM + 8])
            out_matrix(w, 3)
            norm_scale(mod[:, 3, :], vec[:, V_NORM2 + 8:V_NORM2 + 16])
            normalise(X)
            to_features(w, scl, mod[:, 2, :])
            dve.wait_ge(small_mm, 2)
            bank = bank_of(w)
            free(w, dve.tensor_copy(lgt, ps[:, bank, 0:16].rearrange("p (i e) -> p i e", i=TT)))

            def over(a):
                return a.rearrange("p (i o) -> p i o", o=1).to_broadcast([128, TT, N_EXPERTS])

            rank = cst[:, C_RANK:C_RANK + 8].rearrange("p (o e) -> p o e", o=1).to_broadcast([128, TT, N_EXPERTS])
            for which, src in ((0, lgt), (1, lg2)):
                link(dve.tensor_reduce(mm2[:, which, :], src, AX.X, ALU.max))
                link(dve.tensor_tensor(oh[:, which], src, over(mm2[:, which, :]), ALU.is_equal))
                link(dve.tensor_tensor(oh[:, which], oh[:, which], rank, ALU.mult))
                link(dve.tensor_reduce(mm2[:, 7, :], oh[:, which], AX.X, ALU.max))
                link(dve.tensor_tensor(oh[:, which], rank, over(mm2[:, 7, :]), ALU.is_equal))
                if which == 0:
                    link(dve.scalar_tensor_tensor(lg2, oh[:, 0], -BIG, lgt, ALU.mult, ALU.add))
            dve.tensor_tensor(mm2[:, 2, :], mm2[:, 1, :], mm2[:, 0, :], ALU.subtract).then_inc(g_vec, 1)
            dve.wait_ge(g_act, 3)
            link(dve.tensor_scalar(mm2[:, 4, :], mm2[:, 3, :], 1.0, None, ALU.add))
            link(dve.reciprocal(mm2[:, 5, :], mm2[:, 4, :]))
            link(dve.tensor_tensor(mm2[:, 6, :], mm2[:, 5, :], mm2[:, 3, :], ALU.mult))
            link(dve.tensor_tensor(lgt, oh[:, 0], over(mm2[:, 5, :]), ALU.mult))
            link(dve.tensor_tensor(lg2, oh[:, 1], over(mm2[:, 6, :]), ALU.mult))
            dve.tensor_tensor(gates[:, :, 0:8], lgt, lg2, ALU.add)
            dve.tensor_scalar(upto, cst[:, C_CAUSALT:C_CAUSALT + 128], 0.0, None, ALU.is_equal)
            dve.tensor_tensor_scan(numbers, ones[:, :], ones[:, :], 0.0, ALU.mult, ALU.add)
            dve.memset(slot_of, 0.0)
            both(dve.tensor_tensor(oh[:, 0], oh[:, 0], oh[:, 1], ALU.add), tokens_set, 1)
            dve.wait_ge(small_mm, 3)
            bank = bank_of(w)
            dve.tensor_tensor(slot_of[:, :, 0:8], ps[:, bank, 0:16].rearrange("p (i e) -> p i e", i=TT), oh[:, 0], ALU.mult)
            free(w, dve.tensor_reduce(mm2[:, 0, 0:1], ps[:, bank, 16:24], AX.X, ALU.max))
            both(dve.tensor_scalar(crowded[:, :], mm2[:, 0, 0:1], 128.0, None, ALU.is_gt), crowd_set, 1)

            def choose(e, tiles):
                cut = slice(e, e + 1) if isinstance(e, int) else bass.ds(e, 1)
                link(dve.tensor_copy(slot_cur, slot_of[:, :, cut].rearrange("p i o -> p (i o)")))
                for i in range(TT):
                    ins = dve.tensor_scalar(chosen[:, i, 0:128 * tiles], numbers[:, 0:128 * tiles], slot_cur[:, i:i + 1],
                                            None, ALU.is_equal)
                ins.then_inc(pick_set, 1)

            def expert_low(v, n, tiles):
                dve.wait_ge(e_high, n)
                dve.sem_inc(ps_free, 2)
                v.next_pair(), v.next_pair()
                dve.tensor_tensor(AL[:, :, 0:128 * tiles], AF[:, :, 0:128 * tiles], AH[:, :, 0:128 * tiles].bitcast(fp),
                                  ALU.subtract).then_inc(e_in, 1)

            def expert(v, e, tiles):
                first = v.unit - LEAD

                def product(c):
                    dve.wait_ge(e_silu, 3 * e + c + 1)
                    dve.wait_ge(w_used, first + 4 * c + 4)
                    _, _ = v.next_pair()
                    bank = bank_of(v)
                    v.next_pair()
                    n = E_COLS[c][1]
                    dve.tensor_tensor(e_hid[:, c % 2, 0:tiles, 0:n], e_sil[:, c % 2, 0:tiles, 0:n],
                                      ps[:, bank:bank + tiles, 0:n], ALU.mult).then_inc(e_prod, 1)
                    dve.wait_ge(e_prod, 3 * e + c + 1)
                    dve.sem_inc(ps_free, 2)

                def split(c):
                    dve.wait_ge(e_tp, 3 * e + c + 1)
                    bank = bank_of(v)
                    nb = E_COLS[c][1] // 128
                    src = ps[:, bank:bank + 2, :].rearrange("p b (k t) -> p (b k) t", k=2)[:, 0:nb, 0:128 * tiles]
                    hh, hl = (a[:, 4 * c:4 * c + nb, 0:128 * tiles] for a in (HH, HL))
                    link(dve.tensor_copy(hh, src))
                    dve.tensor_tensor(hl, src, hh.bitcast(fp), ALU.subtract).then_inc(e_hidden, 1)
                    dve.wait_ge(e_hidden, 3 * e + c + 1)
                    v.next_pair()
                    dve.sem_inc(ps_free, 1)

                for j in range(LEAD, 18 + LEAD):
                    lo(v, E_JOBS[j % 18])
                    if j == 3:
                        dve.wait_ge(place_tp, e + 1)
                        bank = bank_of(v)
                        free(v, dve.tensor_copy(place[:, 0:tiles, :].rearrange("p j t -> p (j t)"),
                                                ps[:, bank, 0:SEQ * tiles]))
                        dve.sem_inc(place_set, 1)
                        choose(e + 1, tiles)
                        link(dve.tensor_copy(gcur, gates[:, :, bass.ds(e, 1)].rearrange("p i o -> p (i o)")))
                    if j == 6:
                        product(0)
                    if j == 10:
                        product(1)
                        split(0)
                    if j == 13:
                        product(2)
                    if j == 14:
                        split(1)
                    if j == 15:
                        expert_low(v, e + 2, tiles)
                        split(2)
                    if j == 17:
                        dve.wait_ge(e_set, 2 * e + 1)
                        dve.sem_inc(ps_free, 1)
                        v.next_pair()
                dve.wait_ge(e_set, 2 * e + 2)
                dve.sem_inc(ps_free, 1)
                v.next_pair()
                for c in range(2):
                    dve.wait_ge(e_back, 2 * e + c + 1)
                    bank = bank_of(v)
                    cut = slice(512 * c, 512 * c + 512)
                    for i in range(TT):
                        ins = dve.scalar_tensor_tensor(Y[:, i, cut], ps[:, bank + i, :], gcur[:, i:i + 1], Y[:, i, cut],
                                                       ALU.mult, ALU.add)
                    if c == 0:
                        free(v, ins)
                    else:
                        ins.then_inc(ps_free, 1)

            choose(0, TT)
            link(dve.memset(Y, 0.0))
            dve.wait_ge(crowd_set, 1)
            crowd = dve.value_load(crowded[0:1, 0:1], min_val=0, max_val=1)
            expert_low(w, 1, TT)
            assert w.pair == PAIR_MOE
            los(w, LEAD)
            LINKS = 5

            def experts(tiles):
                base = steps[0]
                with dve.Fori(0, N_EXPERTS) as e:
                    steps[0] = base + e * LINKS
                    dve.wait_ge(ps_free, w.pair + e * E_PAIRS)
                    expert(w.after_groups(e, E_PAIRS), e, tiles)
                steps[0] = base

            with dve.If(crowd > 0):
                experts(TT)
            with dve.Else():
                experts(1)
            steps[0] += LINKS * N_EXPERTS
            w = w.after_groups(N_EXPERTS, E_PAIRS)
            dve.wait_ge(ps_free, w.pair)
            add_layer(4, GB[:, 1, :])
            normalise(X)
            dve.wait_ge(ts_ready, counts["ts"])
            dve.wait_ge(late_in, 32)
            for i in range(TT):
                ins = dve.tensor_tensor(X[:, i, :], TS[:, i, :], fwb, ALU.mult)
            both(ins, x_ready, 5)
            normalise(memx)
            to_features(w, vec[:, V_GMEM:V_GMEM + 8])
            first_unit = w.unit - LEAD
            for c in range(2):
                if c == 0:
                    los(w, 2)
                dve.wait_ge(w_used, first_unit + 2 * c + 2)
                bank = bank_of(w)
                free(w, dve.tensor_copy(mkv[:, c], ps[:, bank:bank + 2, :]))
            normalise(X)
            to_features(w, vec[:, V_GMIX:V_GMIX + 8])
            first_unit = w.unit
            los(w, 2)
            for j in range(7):
                if j < 6:
                    los(w, 2)
                dve.wait_ge(w_used, first_unit + 2 * j + 2)
                bank = bank_of(w)
                free(w, dve.tensor_copy(qkv[:, j], ps[:, bank:bank + 2, :]))
            dve.wait_ge(small_mm, 4)
            bank = bank_of(w)
            free(w, dve.tensor_scalar(frow[:, 0, :], ps[0:40, bank, 0:SEQ], bias8[0:40, 3:4], None, ALU.add))
            both(dve.scalar_tensor_tensor(frow[:, 1, :], frow[:, 0, :], -1.0, frow[:, 0, :], ALU.mult, ALU.max), g_vec, 4)
            dve.sem_inc(qk_raw, 1)
            dve.wait_ge(g_act, 4)
            link(dve.scalar_tensor_tensor(frow[:, 1, :], frow[:, 0, :], 0.0, frow[:, 2, :], ALU.min, ALU.subtract))
            link(dve.memset(fcum, 0.0))
            link(dve.tensor_tensor_scan(frow[:, 3, :], ones[0:40, :], frow[:, 1, :], 0.0, ALU.mult, ALU.add))
            dve.tensor_scalar(fox_r, fcum, cst[:, C_FOX:C_FOX + 1], cst[:, C_FOX + 1:C_FOX + 2],
                              ALU.mult, ALU.add)
            for n, (blk, g0, dh) in enumerate(NORMED):
                counts["sq"] += 1
                dve.wait_ge(sq_done, counts["sq"])
                nh = 512 // dh
                a = (mkv[:, 0] if blk is None else qkv[:, blk]).rearrange("p i (h d) -> p i h d", d=dh)
                sq = flatA[:, 1024 * (n % 2):1024 * (n % 2) + 1024].rearrange("p (g d) -> p g d", d=dh)
                link(dve.tensor_reduce(ss[:, 0:2 * nh], sq, AX.X, ALU.add))
                root(2 * nh, dh)
                fa = a.rearrange("p i h d -> p (i h) d")
                link(dve.tensor_tensor(fa, fa, rs[:, 0:2 * nh].rearrange("p (g o) -> p g o", o=1)
                                       .to_broadcast([128, 2 * nh, dh]), ALU.mult))
                ins = dve.tensor_tensor(fa, fa, gains[:, g0:g0 + dh].rearrange("p (o d) -> p o d", o=1)
                                        .to_broadcast([128, 2 * nh, dh]), ALU.mult)
                if blk in (0, 1):
                    link(ins)
                    x1, x2 = a[:, :, :, 0:8], a[:, :, :, 8:16]
                    tr = TS[:, 0, 0:512].rearrange("p (r i h d) -> p r i h d", r=4, i=TT, h=A_HEADS)

                    def table(c0):
                        return cst[:, c0:c0 + 16].rearrange("p (i o d) -> p i o d", i=TT, o=1)\
                            .to_broadcast([128, TT, A_HEADS, 8])
                    for r, (x_, c0) in enumerate(((x1, C_COS), (x2, C_SIN), (x2, C_COS), (x1, C_SIN))):
                        ins = dve.tensor_tensor(tr[:, r], x_, table(c0), ALU.mult)
                    link(ins)
                    dve.tensor_tensor(x1, tr[:, 0], tr[:, 1], ALU.subtract)
                    ins = dve.tensor_tensor(x2, tr[:, 2], tr[:, 3], ALU.add)
                both(ins, qk_ready, n + 1)
            for h in range(A_HEADS):
                ins = dve.tensor_scalar(fox_l[:, h, :], fcum, cst[:, C_FOX + 2 + h:C_FOX + 3 + h],
                                        cst[:, C_FOX + 10 + h:C_FOX + 11 + h], ALU.mult, ALU.add)
            ins.then_inc(fox_set, 1)
            for b in range(3):
                for which in range(2):
                    counts["tp"] += 1
                    dve.wait_ge(tp_done, counts["tp"])
                    bank = bank_of(w)
                    free(w, dve.tensor_copy(acc[:, b, 1024 * which:1024 * which + 1024]
                                            .rearrange("p (b n) -> p b n", b=2), ps[:, bank:bank + 2, :]))
                    dve.sem_inc(qk_set, 1)
            outs = 0
            for b, (gh0, heads, dh, causal, fox) in enumerate(BRANCHES):
                n0 = 128 if causal else 256
                per = 128 // dh
                for step in range(heads + 4):
                    if step < heads:
                        gh = gh0 + step
                        dve.wait_ge(t_s, gh + 1)
                        at_least(dve, t_exp, gh - 1)
                        bank = t_bank_s(gh)
                        m0 = 2 * (gh % 2)
                        dve.tensor_reduce(nmx[:, 4 + m0:5 + m0], ps[:, bank, 0:n0], AX.X, ALU.max)
                        link(dve.tensor_reduce(nmx[:, 5 + m0:6 + m0], ps[:, bank, n0:n0 + 256], AX.X, ALU.max))
                        dve.tensor_scalar(nmx[:, m0:m0 + 2], nmx[:, 4 + m0:6 + m0], -(dh ** -0.5), None, ALU.mult)\
                           .then_inc(t_max, 1)
                    if 1 <= step <= heads:
                        gh = gh0 + step - 1
                        m0 = 2 * (gh % 2)
                        dve.wait_ge(t_exp, gh + 1)
                        link(dve.reciprocal(rsum[:, 4 + m0:6 + m0], rsum[:, m0:m0 + 2]))
                        dve.tensor_scalar(prb[:, gh % 2, 0:n0], prb[:, gh % 2, 0:n0], rsum[:, 4 + m0:5 + m0], None, ALU.mult)
                        dve.tensor_scalar(prb[:, gh % 2, n0:n0 + 256], prb[:, gh % 2, n0:n0 + 256],
                                          rsum[:, 5 + m0:6 + m0], None, ALU.mult).then_inc(t_p, 1)
                    if 2 <= step <= heads + 1:
                        gh = gh0 + step - 2
                        dve.wait_ge(t_tp, gh + 1)
                        at_least(dve, t_o, gh - 1)
                        bank = t_bank_s(gh) + 1
                        assert bank == bank_of(w) + 1
                        w.next_pair()
                        n = 384 if causal else 512
                        dve.tensor_copy(pts[:, gh % 2, 0:n], ps[:, bank, 0:n]).then_inc(t_pt, 1)
                        dve.wait_ge(t_pt, gh + 1)
                        dve.sem_inc(ps_free, 1)
                    h = step - 4
                    if 0 <= h and h % per == 0:
                        kt = h // per
                        dve.wait_ge(t_o, gh0 + h + per)
                        bank = bank_of(w)
                        outs += 1
                        hh, hl = HH[:, 4 * b + kt, :], HL[:, 4 * b + kt, :]
                        link(dve.tensor_copy(hh, ps[:, bank, 0:SEQ]))
                        both(dve.tensor_tensor(hl, ps[:, bank, 0:SEQ], hh.bitcast(fp), ALU.subtract), t_y, outs)
                        w.next_pair()
                        dve.sem_inc(ps_free, 1)
            first_unit = w.unit
            for b in range(3):
                for c in range(2):
                    los(w, 2)
                    dve.wait_ge(w_used, w.unit)
                    bank = bank_of(w)
                    free(w, dve.tensor_copy(sg[:, :, 512 * c:512 * c + 512], ps[:, bank:bank + 2, :]))
                dve.sem_inc(b_raw, 1)
                los(w, 1)
                dve.wait_ge(b_sig, b + 1)
                for c in range(2):
                    if c == 0:
                        los(w, 1)
                    dve.wait_ge(w_used, first_unit + 6 * b + 4 + c + 1)
                    bank = bank_of(w)
                    cut = slice(512 * c, 512 * c + 512)
                    dst = TS[:, :, cut] if b == 0 else tok(flatA[:, 0:1024])
                    free(w, dve.tensor_tensor(dst, ps[:, bank:bank + 2, :], sg[:, :, cut], ALU.mult))
                    if b:
                        link(dve.tensor_tensor(TS[:, :, cut], TS[:, :, cut], dst, ALU.add))
            counts["ts"] += 1
            dve.sem_inc(ts_ready, 1)
            to_features(w)
            for c in range(2):
                los(w, 2)
                dve.wait_ge(w_used, w.unit)
                bank = bank_of(w)
                cut = slice(512 * c, 512 * c + 512)
                free(w, dve.tensor_tensor(X[:, :, cut], X[:, :, cut], ps[:, bank:bank + 2, :], ALU.add))
            dve.sem_inc(x_ready, 1)
            normalise(X)
            to_features(w, vec[:, V_GFFN:V_GFFN + 8])
            dve.memset(Y, 0.0)
            link(dve.tensor_copy(gcur, ones2))
            w = groups(w, 2)
            add_layer(1, s=out_ready)


_INPUTS = ["x", "c", "ada_w", "ada_b", "norm1_w", "norm2_w", "final_norm_w", "m_w_in", "m_i_bias", "m_f_bias",
           "m_conv_w", "m_conv_b", "m_norm_w", "m_w_out", "h_w_in", "h_lb_logits", "h_norm_w", "h_w_out",
           "ffn_w_gate", "ffn_w_up", "ffn_w_down", "moe_router", "moe_w_gate", "moe_w_up", "moe_w_down", "mem_2",
           "g_mix_2", "w_in_2", "b_forget_2", "g_q_moba_2", "g_k_moba_2", "g_q_fox_2", "g_k_fox_2", "g_q_mem_2",
           "g_k_mem_2", "g_mem_2", "w_mem_kv_2", "w_br_moba_2", "w_br_fox_2", "w_br_mem_2", "w_out_2", "g_ffn_2",
           "w_gate_2", "w_up_2", "w_down_2"]


def kernel(**inputs):
    import concourse.bacc as bacc
    from concourse.bass_utils import run_bass_kernel_spmd

    nc = bacc.Bacc("TRN2", target_bir_lowering=False, num_devices=1, dynamic_dma_scratch_size=256)
    arrays = {f"in_{n}": np.ascontiguousarray(inputs[n]) for n in _INPUTS}
    arrays["in_shape_consts"] = shape_constants()
    t = {n[3:]: nc.dram_tensor(n, a.shape, mybir.dt.from_np(a.dtype), kind="ExternalInput").ap()
         for n, a in arrays.items()}
    out = nc.dram_tensor("out_x", (1, SEQ, D), mybir.dt.float32, kind="ExternalOutput").ap()
    build(nc, t, out)
    r = run_bass_kernel_spmd(nc, [arrays], core_ids=[0])
    return r.results[0]["out_x"]
```

```python
from contextlib import ExitStack

import numpy as np
import concourse.bass as bass
from concourse import mybir

SEQ, D = 256, 1024
KT = D // 128
TT = SEQ // 128
M_HEADS, M_DQK, M_DV = 8, 64, 128
M_QK, M_V = M_HEADS * M_DQK, M_HEADS * M_DV
H_HEADS, H_D = 8, 128
D_FF, N_EXPERTS = 2816, 8
D_GROUP = D_FF // 2
FT = D_GROUP // 128
CONV_K = 4
EPS = 1e-6
F_FLOOR = 1e-30
BIG = 1e30
A_HEADS, A_D, C_HEADS, C_D = 8, 64, 4, 128
N_RAW, N_HL = 3, 3
N_RAW_E = 6
UNIT = 2048
LEVELS = 7
LN_SHIFT = 2.0 ** 50

V_NORM1, V_NORM2, V_C, V_CONVW, V_CONVB, V_MNORM, V_LB, V_HNORM, V_GMIX, V_GMEM, V_GFFN = \
    0, 16, 32, 40, 72, 80, 88, 96, 104, 112, 120
C_ID, C_CAUSAL, C_CAUSALT, C_COS, C_SIN, C_FOX, C_RANK, C_LEVEL = 0, 128, 256, 384, 400, 416, 434, 448
C_COLS = C_LEVEL + (LEVELS + 1) * 128

BRANCHES = ((0, A_HEADS, A_D, True, False), (A_HEADS, A_HEADS, A_D, True, True),
            (2 * A_HEADS, C_HEADS, C_D, False, False))
NORMED = ((0, 0, A_D, 0, 0, 0), (1, A_D, A_D, 0, 1, 1), (None, 4 * A_D + C_D, C_D, 2, 1, 2),
          (3, 2 * A_D, A_D, 1, 0, 3), (4, 3 * A_D, A_D, 1, 1, 4), (6, 4 * A_D, C_D, 2, 0, 6))
NORM_BEHIND = {entry[5]: n for n, entry in enumerate(NORMED)}

PAIR_HEADS = 2 + 2 + 2 + 4 + 1 + 1
PAIR_FFN = PAIR_HEADS + 2 * M_HEADS + 2 + 3 + 2 + 2
PAIR_LEVELS = PAIR_FFN + 16 + 4 + 2 + 4 + 4
PAIR_MOE = PAIR_LEVELS + 2 * LEVELS + 3 + 2 + 2 + 2 + 2 + 1 + 1 + 2
E_PAIRS = 16
PAIR_ATT = PAIR_MOE + E_PAIRS * N_EXPERTS + 2 + 2 + 2 + 7 + 1 + 6
PAIR_FFN2 = PAIR_ATT + 12 + 12 + 8 + 12 + 2 + 2 + 2


FEATURE_TPS = (4, 6, 8, 10, 12, 14, 16, 24, 26)
FEATURE_PAIRS = (PAIR_HEADS + 2 * M_HEADS + 1, PAIR_FFN - 1, PAIR_FFN + 16 + 4 + 1, PAIR_LEVELS + 2 * LEVELS + 3 + 2 + 1,
                 PAIR_MOE - 5, PAIR_MOE + E_PAIRS * N_EXPERTS + 1, PAIR_MOE + E_PAIRS * N_EXPERTS + 2 + 2 + 1,
                 PAIR_FFN2 - 5, PAIR_FFN2 - 1)


def m_bank_s(h):
    return 2 * ((PAIR_HEADS + (2 * h - 1 if h else 0)) % 4)


def t_bank_s(gh):
    b = 0 if gh < A_HEADS else 1 if gh < 2 * A_HEADS else 2
    i = gh - BRANCHES[b][0]
    before = max(0, i - 2) if b == 2 else max(0, (i - 1) // 2)
    return 2 * ((PAIR_ATT + 12 * b + i + before) % 4)


def shape_constants():
    c = np.zeros((128, C_COLS), np.float32)
    c[:, C_ID:C_ID + 128] = np.eye(128)
    row, col = np.arange(128)[:, None], np.arange(128)[None, :]
    c[:, C_CAUSAL:C_CAUSAL + 128] = np.where(col > row, -BIG, 0.0)
    c[:, C_CAUSALT:C_CAUSALT + 128] = np.where(row > col, BIG, 0.0)
    rot = A_D // 4
    half = rot // 2
    inv = (1.0 / (np.float32(500000.0) ** (np.arange(half, dtype=np.float32) * np.float32(2.0) / np.float32(rot))))
    ang = np.arange(SEQ, dtype=np.float32)[:, None] * inv.astype(np.float32)[None, :]
    for i in range(TT):
        c[:, C_COS + half * i:C_COS + half * (i + 1)] = np.cos(ang[128 * i:128 * (i + 1)])
        c[:, C_SIN + half * i:C_SIN + half * (i + 1)] = np.sin(ang[128 * i:128 * (i + 1)])
    for h in range(A_HEADS):
        c[h, C_FOX] = -8.0
        c[32 + h, C_FOX + 1] = 1.0
        c[32 + h, C_FOX + 2 + h] = 8.0
        c[h, C_FOX + 10 + h] = 1.0
    c[:, C_RANK:C_RANK + 8] = 8 - np.arange(8)
    for lev in range(LEVELS):
        b = 64 >> lev
        ok = (row // (2 * b) == col // (2 * b)) & (row % (2 * b) < b) & (col % (2 * b) >= b)
        c[:, C_LEVEL + 128 * lev:C_LEVEL + 128 * (lev + 1)] = ok
    c[:, C_LEVEL + 128 * LEVELS:] = row == col
    return c


def build(nc, t, out):
    fp, fr, bf, i32 = mybir.dt.float32, mybir.dt.float32r, mybir.dt.bfloat16, mybir.dt.int32
    ALU, ACT, AX = mybir.AluOpType, mybir.ActivationFunctionType, mybir.AxisListType

    ctx = ExitStack()
    with ctx:
        ctx.enter_context(nc.allow_non_contiguous_dma(reason="small parameters"))

        def sb(name, shape, dt=fp):
            return ctx.enter_context(nc.sbuf_tensor(name, shape, dt))

        def sem(name):
            return ctx.enter_context(nc.semaphore(name))

        raw = sb("raw", [128, N_RAW, UNIT])
        whi = sb("whi", [128, N_HL, UNIT], fr)
        wlo = sb("wlo", [128, N_HL, UNIT], fr)
        X = sb("X", [128, TT, D])
        AF = sb("AF", [128, KT, SEQ])
        AH = sb("AH", [128, KT, SEQ], fr)
        AL = sb("AL", [128, KT, SEQ], fr)
        HH = sb("HH", [128, 12, SEQ], fr)
        HL = sb("HL", [128, 12, SEQ], fr)
        acc = sb("acc", [128, 3, UNIT])
        TS = sb("TS", [128, TT, D])
        GB = sb("GB", [128, 2, D])
        Z = sb("Z", [128, 10240])
        cst = sb("cst", [128, C_COLS])
        ones = sb("ones", [128, SEQ])
        identb = sb("identb", [128, 128], bf)
        maskb = sb("maskb", [128, 2, 128], bf)
        vec = sb("vec", [128, 128])
        adab = sb("adab", [128, 96])
        mod = sb("mod", [128, 4, KT])
        cond = sb("cond", [128, KT])
        wsm = sb("wsm", [128, KT, 64])
        gains = sb("gains", [128, 4 * A_D + 2 * C_D])
        col = sb("col", [128, 292])
        crowded = sb("crowded", [128, 1], i32)
        ident = cst[:, C_ID:C_ID + 128]
        ps = ctx.enter_context(nc.psum_tensor("ps", [128, 8, 512], fp))

        ss, rs = col[:, 0:16], col[:, 16:32]
        nmx, rsum = col[:, 32:40], col[:, 40:48]
        gcol = col[:, 48:64].rearrange("p (i h) -> p i h", i=TT)
        ecol = col[:, 64:80].rearrange("p (i h) -> p i h", i=TT)
        dcol = col[:, 80:96]
        gates = col[:, 96:112].rearrange("p (i e) -> p i e", i=TT)
        gcur = col[:, 112:114]
        bias8 = col[:, 114:118]
        lbc = col[:, 120:136]
        lgt = col[:, 136:152].rearrange("p (i e) -> p i e", i=TT)
        oh = col[:, 152:184].rearrange("p (w i e) -> p w i e", w=2, i=TT)
        lg2 = col[:, 184:200].rearrange("p (i e) -> p i e", i=TT)
        io8 = col[:, 200:208]
        mm2 = col[:, 208:224].rearrange("p (w i) -> p w i", w=8)
        scl = col[:, 224:232]
        ones2 = col[:, 232:234]
        slot_of = col[:, 272:290].rearrange("p (i e) -> p i e", i=TT)
        slot_cur = col[:, 290:292]
        ms, nt = col[:, 240:256], col[:, 256:272]

        raw_full = [sem(f"raw_full{i}") for i in range(N_RAW_E)]
        w_hi, w_lo = sem("w_hi"), sem("w_lo")
        w_used = sem("w_used")
        ada_used = sem("ada_used")
        ada_init, ada_sum = sem("ada_init"), sem("ada_sum")
        ps_free = sem("ps_free")
        silu_done, hid_done = sem("silu_done"), sem("hid_done")
        rows_in, small_in, cst_in, x_in, late_in = (sem("rows_in"), sem("small_in"), sem("cst_in"), sem("x_in"),
                                                    sem("late_in"))
        vec_step, act_step = sem("vec_step"), sem("act_step")
        cleared, ones_set, consts_set = sem("cleared"), sem("ones_set"), sem("consts_set")
        rows_t, vec_set, cond_set = sem("rows_t"), sem("vec_set"), sem("cond_set")
        x_ready = sem("x_ready")
        sq_done = sem("sq_done")
        ts_ready, tp_done, a_ready = sem("ts_ready"), sem("tp_done"), sem("a_ready")
        small_mm = sem("small_mm")
        g_vec, g_act = sem("g_vec"), sem("g_act")
        conv_done, og_set, ogs_set, qk_silu = sem("conv_done"), sem("og_set"), sem("ogs_set"), sem("qk_silu")
        col_tp, cols_set = sem("col_tp"), sem("cols_set")
        m_sc, m_exp, m_pt, m_o, heads_done = (sem("m_sc"), sem("m_exp"), sem("m_pt"), sem("m_o"), sem("heads_done"))
        h_raw, h_act, h_vec = sem("h_raw"), sem("h_act"), sem("h_vec")
        l_sub, l_exp, l_kq, l_mm = sem("l_sub"), sem("l_exp"), sem("l_kq"), sem("l_mm")
        h_o = sem("h_o")
        mem_in, sum_clear = sem("mem_in"), sem("sum_clear")
        half_set = sem("half_set")
        head_out = sem("head_out")
        starts_set, sums_set, at_clear = sem("starts_set"), sem("sums_set"), sem("at_clear")
        tokens_set, crowd_set = sem("tokens_set"), sem("crowd_set")
        pick_set, place_tp, place_set = sem("pick_set"), sem("place_tp"), sem("place_set")
        e_gather, e_high, e_in = sem("e_gather"), sem("e_high"), sem("e_in")
        e_silu, e_prod, e_tp, e_hidden = sem("e_silu"), sem("e_prod"), sem("e_tp"), sem("e_hidden")
        e_set, e_back = sem("e_set"), sem("e_back")
        qk_raw, qk_ready, qk_set = sem("qk_raw"), sem("qk_ready"), sem("qk_set")
        fox_set = sem("fox_set")
        t_s, t_max, t_exp, t_p, t_tp, t_pt, t_o, t_y = (sem("t_s"), sem("t_max"), sem("t_exp"), sem("t_p"),
                                                        sem("t_tp"), sem("t_pt"), sem("t_o"), sem("t_y"))
        b_raw, b_sig = sem("b_raw"), sem("b_sig")
        root_in, root_out = sem("root_in"), sem("root_out")
        out_ready, out_done = sem("out_ready"), sem("out_done")

        def tok(ap):
            return ap.rearrange("p (i n) -> p i n", i=TT)

        qk = Z[:, 0:2048].rearrange("p (k t) -> p k t", k=KT)
        vx = Z[:, 2048:2048 + TT * M_HEADS * 129].rearrange("p (i h e) -> p i h e", i=TT, h=M_HEADS)
        og = tok(Z[:, 4352:6400])
        em = Z[:, 6400:7168].rearrange("p (b n) -> p b n", b=2)
        pt = Z[:, 7168:7936].rearrange("p (b n) -> p b n", b=2)
        rows = Z[0:8, 7936:7936 + 8 * SEQ].rearrange("p (r t) -> p r t", r=8)
        hv = tok(Z[:, 2048:4096])
        at = Z[:, 6400:8448].rearrange("p (g n) -> p g n", g=16)
        ax = Z[:, 8448:9472].rearrange("p (h n) -> p h n", h=H_HEADS)
        flatA = AF[:, :, :].rearrange("p k t -> p (k t)")
        flatT = TS[:, :, :].rearrange("p i n -> p (i n)")
        hq, hk, hb = acc[:, 0, :], acc[:, 1, :], acc[:, 2, :]
        level_buf = [flatA, flatT, Z[:, 0:2048]]
        Y = tok(Z[:, 0:2048])
        sil = Z[:, 2048:3072].rearrange("p (b n) -> p b n", b=2)
        hid = Z[:, 3072:4096].rearrange("p (b n) -> p b n", b=2)
        fwb = Z[:, 4096:5120]
        e_hid = acc[:, 1, :].rearrange("p (b j n) -> p b j n", b=2, j=TT)
        e_out = tok(Z[:, 5120:7168])
        chosen = tok(Z[:, 7168:7680])
        place = tok(Z[:, 7680:8192])
        numbers = Z[:, 8192:8448]
        upto = Z[:, 8448:8576]
        raw_at = [raw[:, i, :] for i in range(N_RAW)] + [acc[:, 0, :], acc[:, 2, :], Z[:, 2048:4096]]
        qkv = Z[:, 0:7168].rearrange("p (j i n) -> p j i n", j=7, i=TT)
        mkv = Z[:, 7168:9216].rearrange("p (j i n) -> p j i n", j=2, i=TT)
        prb = Z[:, 9216:10240].rearrange("p (b n) -> p b n", b=2)
        pts = GB[:, 0, :].rearrange("p (b n) -> p b n", b=2)
        memx = tok(acc[:, 0, :])
        sg = tok(Z[:, 0:2048])
        fox_l = AF[:, :, :]
        fox_r = GB[:, 1, 0:SEQ]
        fcum = TS[:, 1, 768:1024]
        frow = TS[0:40, 1, :].rearrange("p (r t) -> p r t", r=4)

        def wview(w):
            return w.rearrange("(k p) n -> p k n", p=128)

        ada_w = [t["ada_w"][l].rearrange("(k p) n -> k p n", p=128) for l in range(2)]
        m_in, m_out = wview(t["m_w_in"][0]), wview(t["m_w_out"][0])
        h_in, h_out = wview(t["h_w_in"][0]), wview(t["h_w_out"][0])
        w_in2, w_mkv, w_out2 = wview(t["w_in_2"][0]), wview(t["w_mem_kv_2"][0]), wview(t["w_out_2"][0])
        w_br = [wview(t[n][0]) for n in ("w_br_moba_2", "w_br_fox_2", "w_br_mem_2")]
        M_GATES = 2 * M_QK + 2 * M_V
        F_LOGIT = 6 * 512
        Q_MEM = F_LOGIT + A_HEADS
        A_COL = Q_MEM + 512

        class Walk:

            def __init__(self):
                self.slot, self.depth, self.uses = 0, N_RAW, [0] * N_RAW_E
                self.unit, self.hl = 0, 0
                self.pair, self.pb = 0, 0
                self.ada = self.hidden = 0
                self.free_at = {}

            def next_raw(self):
                s = self.slot
                self.slot = (s + 1) % self.depth
                self.uses[s] = self.uses[s] + 1
                return s, self.uses[s] * 16

            def next_unit(self):
                u, h = self.unit, self.hl
                self.unit, self.hl = u + 1, (h + 1) % N_HL
                return u, h

            def next_pair(self):
                p, b = self.pair, self.pb
                self.pair, self.pb = p + 1, (b + 1) % 4
                return p, 2 * b

            def after_groups(self, n, pairs=8):
                w = Walk()
                w.slot, w.hl, w.pb, w.ada, w.depth = self.slot, self.hl, self.pb, self.ada, self.depth
                w.uses = [c + n * (18 // self.depth) for c in self.uses]
                w.unit, w.pair = self.unit + n * 18, self.pair + n * pairs
                w.hidden = self.hidden + (n * 6 if pairs == 8 else 0)
                w.free_at = {(w.slot + k) % w.depth: (w_lo, w.unit - w.depth + k + 1) for k in range(w.depth)}
                return w

        COLS = [(256 * c, min(256, D_GROUP - 256 * c)) for c in range(6)]
        KS = [(4 * g, min(4, FT - 4 * g)) for g in range(3)]
        JOBS = [KT * COLS[j // 2][1] for j in range(12)] + [512 * KS[j % 3][1] for j in range(6)]

        E_COLS = [(512 * c, min(512, D_GROUP - 512 * c)) for c in range(3)]
        E_JOBS = [4 * E_COLS[j // 4][1] for j in range(12)] + JOBS[12:]
        LEAD = 2

        def at_least(eng, s, v):
            if not isinstance(v, int) or v > 0:
                eng.wait_ge(s, v)

        block = ctx.enter_context(nc.Block())

        @block.sync
        def _(sp):
            w = Walk()

            def load(w, src, n, view):
                slot, _ = w.next_raw()
                if slot in w.free_at:
                    s, v = w.free_at[slot]
                    sp.wait_ge(s, v)
                sp.dma_start(view(raw_at[slot][:, 0:n]), src).then_inc(raw_full[slot], 16)
                return slot

            def t_unit(w, wm, c0, n):
                slot = load(w, wm[:, 0:KT, c0:c0 + n], KT * n, lambda r: r.rearrange("p (k n) -> p k n", k=KT))
                u, _ = w.next_unit()
                w.free_at[slot] = (w_lo, u + 1)

            def m_unit(w, wm, k0, nk, c0, n=512):
                slot = load(w, wm[:, k0:k0 + nk, c0:c0 + n], nk * n, lambda r: r.rearrange("p (k n) -> p k n", k=nk))
                u, _ = w.next_unit()
                w.free_at[slot] = (w_lo, u + 1)

            def ada_unit(w, layer, chunk, k):
                slot = load(w, ada_w[layer][k, :, chunk * UNIT:(chunk + 1) * UNIT], UNIT, lambda r: r)
                w.ada += 1
                w.free_at[slot] = (ada_used, w.ada)

            def m_matrix(w, wm, c0, chunks, kts=KT):
                for c in range(chunks):
                    for k0 in range(0, kts, 4):
                        m_unit(w, wm, k0, 4, c0 + 512 * c)

            def group(w, wg, wu, wd, side=lambda j: None):
                for c, (c0, n) in enumerate(COLS):
                    t_unit(w, wg, c0, n)
                    side(2 * c)
                    t_unit(w, wu, c0, n)
                    side(2 * c + 1)
                for c in range(2):
                    for k0, nk in KS:
                        m_unit(w, wd, k0, nk, 512 * c)

            def expert(w, e, j0, j1, later=0):
                cut = slice(e, e + 1) if isinstance(e, int) else bass.ds(e, 1)
                wg, wu, wd = (wview(t[n][0][later:][cut].rearrange("o k n -> (o k) n"))
                              for n in ("moe_w_gate", "moe_w_up", "moe_w_down"))
                units = [(wm, k0, 4, c0, n) for c0, n in E_COLS for wm in (wg, wu) for k0 in (0, 4)]
                units += [(wd, k0, nk, 512 * c, 512) for c in range(2) for k0, nk in KS]
                for wm, k0, nk, c0, n in units[j0:j1]:
                    m_unit(w, wm, k0, nk, c0, n)

            def half(w, names, e, side=lambda j: None):
                g, u, d = (t[n][0] for n in names)
                cut = slice(e * D_GROUP, (e + 1) * D_GROUP) if isinstance(e, int) else bass.ds(e * D_GROUP, D_GROUP)
                group(w, wview(g[:, cut]), wview(u[:, cut]), wview(d[cut, :]), side)

            for k in range(KT):
                ada_unit(w, 0, 0, k)
            for c in range(4):
                t_unit(w, m_in, 256 * c, 256)
                ada_unit(w, 0, 1, c)
            for m in range(8):
                m_unit(w, m_in, 4 * (m % 2), 4, 2 * M_QK + 512 * (m // 2))
                if m < 4:
                    ada_unit(w, 0, 1, 4 + m)
            for k in range(KT):
                ada_unit(w, 0, 2, k)
            m_matrix(w, m_out, 0, 2)
            for e in range(2):
                half(w, ("ffn_w_gate", "ffn_w_up", "ffn_w_down"), e,
                     lambda j: ada_unit(w, 1, (12 * e + j) // 8, (12 * e + j) % 8))
            for c in range(8):
                t_unit(w, h_in, 256 * c, 256)
            m_matrix(w, h_in, 2 * D, 4)
            m_matrix(w, h_out, 0, 2)
            w.depth = N_RAW_E
            assert w.slot == 0
            expert(w, 0, 0, N_RAW)
            sp.wait_ge(heads_done, 2)
            expert(w, 0, N_RAW, N_RAW_E)
            with sp.Fori(0, N_EXPERTS - 1) as e:
                v = w.after_groups(e)
                sp.compute_val(e * (D * D_GROUP) * 4)
                expert(v, e, N_RAW_E, 18)
                expert(v, e, 0, N_RAW_E, 1)
            w = w.after_groups(N_EXPERTS - 1)
            expert(w, N_EXPERTS - 1, N_RAW_E, 18)
            w.depth = N_RAW
            for k0 in (0, 4):
                m_unit(w, w_mkv, k0, 4, 0)
            sp.wait_ge(*w.free_at[N_RAW])
            sp.dma_start(memx, t["mem_2"][0].rearrange("(i p) n -> p i n", p=128)).then_inc(mem_in, 16)
            for k0 in (0, 4):
                m_unit(w, w_mkv, k0, 4, 512)
            m_matrix(w, w_in2, 0, 6)
            m_matrix(w, w_in2, Q_MEM, 1)
            for b in range(3):
                m_matrix(w, w_in2, A_COL + D * b, 2)
                m_matrix(w, w_br[b], 0, 2, 4)
            m_matrix(w, w_out2, 0, 2)
            with sp.Fori(0, 2) as e:
                half(w.after_groups(e), ("w_gate_2", "w_up_2", "w_down_2"), e)
            sp.wait_ge(out_ready, 1)
            sp.dma_start(out[0].rearrange("(i p) n -> p i n", p=128), X[:, :, :]).then_inc(out_done, 16)
            sp.wait_ge(out_done, 16)

        @block.gpsimd
        def _(pool):
            pool.memset(ones[:, :], 1.0).then_inc(ones_set, 1)
            pool.wait_ge(heads_done, 1)
            pool.memset(at, 1.0).then_inc(starts_set, 1)
            pool.wait_ge(starts_set, 1)
            pool.memset(at[:, :, 0:1], 0.0).then_inc(starts_set, 1)
            pool.memset(Y, 0.0).then_inc(sum_clear, 1)
            pool.wait_ge(sums_set, 1)
            pool.memset(at, 0.0).then_inc(at_clear, 1)
            pool.wait_ge(heads_done, 2)
            pool.memset(Y, 0.0).then_inc(sum_clear, 1)
            pool.wait_ge(x_ready, 6)
            pool.memset(Y, 0.0).then_inc(sum_clear, 1)

        @block.scalar
        def _(act):
            steps = [0]

            def link(ins):
                steps[0] += 1
                ins.then_inc(act_step, 1)
                act.wait_ge(act_step, steps[0])

            act.dma_start(cst[:, C_ID:C_ID + 128], t["shape_consts"][:, C_ID:C_ID + 128]).then_inc(cst_in, 16)
            for name, r0, n in (("norm1_w", V_NORM1, 16), ("norm2_w", V_NORM2, 16), ("c", V_C, 8),
                                ("m_conv_w", V_CONVW, 32), ("m_conv_b", V_CONVB, 8), ("m_norm_w", V_MNORM, 8),
                                ("h_lb_logits", V_LB, 8), ("h_norm_w", V_HNORM, 8), ("g_mix_2", V_GMIX, 8),
                                ("g_mem_2", V_GMEM, 8), ("g_ffn_2", V_GFFN, 8)):
                flat = "a b c -> (a b c)" if len(t[name].shape) == 3 else "a b -> (a b)"
                act.dma_start(TS[r0:r0 + n, 1, 0:128],
                              t[name].rearrange(flat).rearrange("(r p) -> r p", p=128)).then_inc(rows_in, 16)
            act.dma_start(TS[0:96, 1, 128:256],
                          t["ada_b"].rearrange("l n -> (l n)").rearrange("(r p) -> r p", p=128)).then_inc(rows_in, 16)
            act.dma_start(X[:, :, :], t["x"][0].rearrange("(i p) n -> p i n", p=128)).then_inc(x_in, 16)
            act.wait_ge(vec_set, 1)
            act.activation(cond[:, :], vec[:, V_C:V_C + 8], ACT.Silu).then_inc(cond_set, 1)
            act.dma_start(cst[:, C_ID + 128:], t["shape_consts"][:, C_ID + 128:]).then_inc(cst_in, 16)
            act.wait_ge(cleared, 2)
            act.dma_start(bias8[0:8, 0:1], t["m_i_bias"].rearrange("o h -> h o")).then_inc(small_in, 16)
            act.dma_start(bias8[0:8, 1:2], t["m_f_bias"].rearrange("o h -> h o")).then_inc(small_in, 16)
            act.dma_start(bias8[0:8, 3:4], t["b_forget_2"].rearrange("o h -> h o")).then_inc(small_in, 16)
            act.dma_start(bias8[32:40, 3:4], t["b_forget_2"].rearrange("o h -> h o")).then_inc(small_in, 16)
            act.dma_start(wsm[:, :, 0:16], m_in[:, :, M_GATES:M_GATES + 16]).then_inc(small_in, 16)
            act.dma_start(wsm[:, :, 16:24], wview(t["moe_router"][0])).then_inc(small_in, 16)
            act.dma_start(wsm[:, :, 24:32], w_in2[:, :, F_LOGIT:F_LOGIT + 8]).then_inc(small_in, 16)
            act.dma_start(wsm[:, :, 56:64], w_in2[:, :, F_LOGIT:F_LOGIT + 8]).then_inc(small_in, 16)
            for j, name in enumerate(("g_q_moba_2", "g_k_moba_2", "g_q_fox_2", "g_k_fox_2")):
                act.dma_start(gains[:, A_D * j:A_D * (j + 1)], t[name].to_broadcast([128, A_D])).then_inc(small_in, 16)
            for j, name in enumerate(("g_q_mem_2", "g_k_mem_2")):
                act.dma_start(gains[:, 4 * A_D + C_D * j:4 * A_D + C_D * (j + 1)],
                              t[name].to_broadcast([128, C_D])).then_inc(small_in, 16)

            def hi(w, n=UNIT):
                s, full = w.next_raw()
                u, h = w.next_unit()
                act.wait_ge(raw_full[s], full)
                at_least(act, w_used, u - N_HL + 1)
                act.activation(whi[:, h, 0:n], raw_at[s][:, 0:n], ACT.Copy).then_inc(w_hi, 1)

            def his(w, k):
                for _ in range(k):
                    hi(w)

            def skip_raw(w, n):
                for _ in range(n):
                    w.next_raw()

            roots = [0]

            def root(n):
                roots[0] += 1
                act.wait_ge(root_in, roots[0])
                act.activation(rs[:, 0:n], rs[:, 0:n], ACT.Sqrt).then_inc(root_out, 1)

            halves_set = [0]

            def second_half(scale=None, shift=None, split=True):
                n = halves_set[0]
                halves_set[0] += 1
                act.wait_ge(tp_done, FEATURE_TPS[n])
                bank = 2 * (FEATURE_PAIRS[n] % 4)
                for k in range(4):
                    src = ps[:, bank + k // 2, SEQ * (k % 2):SEQ * (k % 2) + SEQ]
                    if scale is None:
                        ins = act.activation(AF[:, 4 + k, :], src, ACT.Copy)
                    elif shift is None:
                        ins = act.activation(AF[:, 4 + k, :], src, ACT.Identity, scale=scale[:, 4 + k:5 + k])
                    else:
                        ins = act.activation(AF[:, 4 + k, :], src, ACT.Identity, bias=shift[:, 4 + k:5 + k],
                                             scale=scale[:, 4 + k:5 + k])
                if split:
                    link(ins)
                    ins = act.activation(AH[:, 4:8, :], AF[:, 4:8, :], ACT.Copy)
                ins.then_inc(half_set, 1)

            def head_squares(i, h):
                return act.activation(flatA[:, 0:128], TS[:, i, 128 * h:128 * h + 128], ACT.Square,
                                      accum_out=ss[:, 8 * i + h:8 * i + h + 1])

            def squares(src):
                for i in range(TT):
                    act.activation(AF[:, 4 * i:4 * i + 4, :].rearrange("p k t -> p (k t)"), src[:, i, :], ACT.Square,
                                   accum_out=ss[:, i:i + 1]).then_inc(sq_done, 1)
                root(2)

            def group(w, side=lambda j: None, begin=0):
                first_unit, first_pb, done = w.unit - begin, w.pb, w.hidden

                def silu(c):
                    act.wait_ge(w_used, first_unit + 2 * c + 2)
                    at_least(act, hid_done, done + c - 1)
                    n, bank = 2 * COLS[c][1], 2 * ((first_pb + c) % 4)
                    act.activation(sil[:, c % 2, 0:n], ps[:, bank, 0:n], ACT.Silu).then_inc(silu_done, 1)

                for j in range(begin, 18):
                    hi(w, JOBS[j])
                    if j < 12:
                        side(j)
                    if 3 <= j <= 13 and j % 2:
                        silu((j - 3) // 2)
                w.hidden = done + 6
                for _ in range(8):
                    w.next_pair()

            def expert_input(v, n, tiles):
                for q in range(2):
                    act.wait_ge(e_gather, n + q + 1)
                    _, bank = v.next_pair()
                    for k in range(4):
                        kk = 4 * q + k
                        c0 = SEQ * (k % 2)
                        ins = act.activation(AF[:, kk, 0:128 * tiles], ps[:, bank + k // 2, c0:c0 + 128 * tiles],
                                             ACT.Identity, bias=mod[:, 2, kk:kk + 1], scale=scl[:, kk:kk + 1])
                link(ins)
                act.activation(AH[:, :, 0:128 * tiles], AF[:, :, 0:128 * tiles], ACT.Copy).then_inc(e_high, 1)

            def expert(v, e, tiles):
                first = v.unit - LEAD
                banks = [2 * ((v.pb + i) % 4) for i in range(E_PAIRS)]

                def silu(c):
                    act.wait_ge(w_used, first + 4 * c + 2)
                    n = E_COLS[c][1]
                    act.activation(e_hid[:, c % 2, 0:tiles, 0:n], ps[:, banks[(1, 3, 6)[c]]:banks[(1, 3, 6)[c]] + tiles, 0:n],
                                   ACT.Silu).then_inc(e_silu, 1)

                def output(c):
                    act.wait_ge(w_used, first + 12 + 3 * (c + 1))
                    bank = banks[12 + c]
                    act.activation(e_out[:, 0:tiles, 512 * c:512 * c + 512], ps[:, bank:bank + tiles, :],
                                   ACT.Copy).then_inc(e_set, 1)

                for j in range(LEAD, 18 + LEAD):
                    hi(v, E_JOBS[j % 18])
                    if j in (4, 8, 12):
                        silu(j // 4 - 1)
                    if j == 14:
                        v.pb = (v.pb + 9) % 4
                        expert_input(v, 2 * e + 2, tiles)
                    if j == 17:
                        output(0)
                output(1)

            w = Walk()
            act.wait_ge(x_in, 16)
            squares(X)
            skip_raw(w, 8)
            for u in range(12):
                hi(w)
                if u < 8:
                    skip_raw(w, 1)
            act.wait_ge(conv_done, 1)
            act.activation(qk, qk, ACT.Silu).then_inc(qk_silu, 1)
            act.wait_ge(og_set, 1)
            act.activation(og, og, ACT.Sigmoid).then_inc(ogs_set, 1)
            act.wait_ge(g_vec, 1)
            act.activation(rows[:, 0, :], rows[:, 0, :], ACT.Tanh, bias=bias8[0:8, 2:3], scale=1.0 / 15.0)
            link(act.activation(rows[:, 3, :], rows[:, 2, :], ACT.Exp, scale=-1.0))
            act.activation(rows[:, 3, :], rows[:, 3, :], ACT.Ln, bias=1.0).then_inc(g_act, 1)
            act.wait_ge(g_vec, 2)
            act.activation(rows[:, 7, :], rows[:, 7, :], ACT.Exp, scale=-1.0).then_inc(g_act, 1)
            act.wait_ge(cols_set, 1)
            skip_raw(w, 8)
            for h in range(M_HEADS):
                act.wait_ge(m_sc, h + 1)
                at_least(act, m_pt, h - 1)
                bank = m_bank_s(h)
                act.activation(em[:, h % 2, 0:256], ps[:, bank, 0:256], ACT.Exp, bias=gcol[:, 0, h:h + 1], scale=-1.0)
                act.activation(em[:, h % 2, 256:384], ps[:, bank, 256:384], ACT.Exp, bias=gcol[:, 1, h:h + 1],
                               scale=-1.0).then_inc(m_exp, 1)
                if h >= 2:
                    act.wait_ge(head_out, h - 1)
                    for i in range(TT):
                        link(head_squares(i, h - 2))
            for h in (M_HEADS - 2, M_HEADS - 1):
                act.wait_ge(head_out, h + 1)
                link(head_squares(0, h))
                ins = head_squares(1, h)
                if h < M_HEADS - 1:
                    link(ins)
            ins.then_inc(sq_done, 1)
            root(16)
            hi(w)
            second_half(vec[:, V_MNORM:V_MNORM + 8])
            his(w, 3)
            for _ in range(LEAD):
                hi(w)
                skip_raw(w, 1)
            act.wait_ge(x_ready, 1)
            squares(X)
            second_half(scl, mod[:, 2, :])
            w.pair, w.pb = PAIR_FFN, PAIR_FFN % 4
            group(w, lambda j: skip_raw(w, 1), LEAD)
            for _ in range(LEAD):
                hi(w)
                skip_raw(w, 1)
            group(w, lambda j: skip_raw(w, 1), LEAD)
            his(w, LEAD)
            act.wait_ge(x_ready, 2)
            squares(X)
            second_half(scl, mod[:, 0, :])
            his(w, 6 - LEAD)
            act.wait_ge(h_raw, 1)
            act.activation(hq, hq, ACT.Silu)
            his(w, 4)
            act.wait_ge(h_raw, 2)
            act.activation(flatA, hk, ACT.Sigmoid).then_inc(h_act, 1)
            act.activation(hk, hk, ACT.Sigmoid, scale=-1.0).then_inc(h_act, 1)
            act.wait_ge(h_vec, 1)
            act.activation(lbc[:, 0:8], lbc[:, 0:8], ACT.Exp).then_inc(h_act, 1)
            his(w, 2)
            act.wait_ge(h_vec, 2)
            act.activation(flatT, flatA, ACT.Ln)
            act.activation(level_buf[2], flatA, ACT.Ln, scale=LN_SHIFT).then_inc(h_act, 1)
            his(w, 4 + LEAD)
            act.wait_ge(og_set, 2)
            act.activation(og, og, ACT.Silu).then_inc(ogs_set, 1)
            for lev in range(LEVELS + 1):
                act.wait_ge(l_sub, lev + 1)
                act.activation(level_buf[lev % 3], level_buf[lev % 3], ACT.Exp).then_inc(l_exp, 1)
            for i in range(TT):
                act.wait_ge(head_out, M_HEADS + i + 1)
                for h in range(H_HEADS):
                    ins = head_squares(i, h)
                    if (i, h) < (TT - 1, H_HEADS - 1):
                        link(ins)
            ins.then_inc(sq_done, 1)
            root(16)
            second_half(vec[:, V_HNORM:V_HNORM + 8])
            his(w, 4 - LEAD)
            w.depth = N_RAW_E
            his(w, LEAD)
            act.wait_ge(x_ready, 3)
            squares(X)
            second_half(scl, mod[:, 2, :], split=False)
            act.dma_start(fwb, t["final_norm_w"].rearrange("(o n) -> o n", o=1).to_broadcast([128, D])).then_inc(late_in, 16)
            act.wait_ge(g_vec, 3)
            act.activation(mm2[:, 3, :], mm2[:, 2, :], ACT.Exp).then_inc(g_act, 1)
            act.wait_ge(crowd_set, 1)
            crowd = act.value_load(crowded[0:1, 0:1], min_val=0, max_val=1)
            w.pair, w.pb = PAIR_MOE - 2, (PAIR_MOE - 2) % 4
            expert_input(w, 0, TT)
            w.pair = PAIR_MOE

            def experts(tiles):
                base = steps[0]
                with act.Fori(0, N_EXPERTS) as e:
                    steps[0] = base + e
                    expert(w.after_groups(e, E_PAIRS), e, tiles)
                steps[0] = base

            with act.If(crowd > 0):
                experts(TT)
            with act.Else():
                experts(1)
            steps[0] += N_EXPERTS
            w = w.after_groups(N_EXPERTS, E_PAIRS)
            w.depth = N_RAW
            act.wait_ge(mem_in, 16)
            squares(memx)
            second_half(vec[:, V_GMEM:V_GMEM + 8])
            his(w, 2)
            act.wait_ge(a_ready, 2 * 7)
            act.wait_ge(x_ready, 4)
            squares(X)
            act.wait_ge(x_ready, 5)
            squares(X)
            his(w, 2)
            second_half(vec[:, V_GMIX:V_GMIX + 8])
            for j in range(7):
                his(w, 2)
                if j == 0:
                    act.wait_ge(g_vec, 4)
                    link(act.activation(frow[:, 2, :], frow[:, 1, :], ACT.Exp, scale=-1.0))
                    act.activation(frow[:, 2, :], frow[:, 2, :], ACT.Ln, bias=1.0).then_inc(g_act, 1)
                if j in NORM_BEHIND:
                    n = NORM_BEHIND[j]
                    act.wait_ge(qk_raw, n + 1)
                    at_least(act, qk_ready, n)
                    src = mkv[:, 0] if NORMED[n][0] is None else qkv[:, NORMED[n][0]]
                    act.activation(tok(GB[:, 0, :]), src, ACT.Square).then_inc(sq_done, 1)
                    root(2 * (512 // NORMED[n][2]))
            for gh0, heads, dh, causal, fox in BRANCHES:
                for i in range(heads):
                    gh = gh0 + i
                    act.wait_ge(t_max, gh + 1)
                    at_least(act, t_tp, gh - 1)
                    bank = t_bank_s(gh)
                    n0 = 128 if causal else 256
                    for k, (c0, n) in enumerate(((0, n0), (n0, 256))):
                        ins = act.activation(prb[:, gh % 2, c0:c0 + n], ps[:, bank, c0:c0 + n], ACT.Exp,
                                             bias=nmx[:, 2 * (gh % 2) + k:2 * (gh % 2) + k + 1], scale=dh ** -0.5,
                                             accum_out=rsum[:, 2 * (gh % 2) + k:2 * (gh % 2) + k + 1])
                    ins.then_inc(t_exp, 1)
            for b in range(3):
                his(w, 4)
                act.wait_ge(b_raw, b + 1)
                act.activation(sg, sg, ACT.Sigmoid).then_inc(b_sig, 1)
                his(w, 2)
            second_half()
            his(w, 4)
            act.wait_ge(x_ready, 6)
            squares(X)
            second_half(vec[:, V_GFFN:V_GFFN + 8])
            w.pair, w.pb = PAIR_FFN2, PAIR_FFN2 % 4
            group(w, begin=LEAD)
            his(w, LEAD)
            group(w, begin=LEAD)

        @block.tensor
        def _(pe):
            w = Walk()
            stage = [0]

            def pair(w):
                p, bank = w.next_pair()
                at_least(pe, ps_free, p - 3)
                return bank

            def three(o, sh, sl, mh, ml, first, last):
                pe.matmul(o, sh, mh, start=first, stop=False)
                pe.matmul(o, sh, ml, start=False, stop=False)
                return pe.matmul(o, sl, mh, start=False, stop=last)

            inputs, halves_in = [0], [0]

            def input_half(q):
                if halves_in[0] < 2 * inputs[0] and q == halves_in[0] % 2:
                    halves_in[0] += 1
                    pe.wait_ge(a_ready, halves_in[0])

            def t_unit(w, bank, n=256):
                u, h = w.next_unit()
                pe.wait_ge(w_lo, u + 1)
                wh = whi[:, h, 0:KT * n].rearrange("p (k n) -> p k n", k=KT)
                wl = wlo[:, h, 0:KT * n].rearrange("p (k n) -> p k n", k=KT)
                for f in range(n // 128):
                    for k in range(KT):
                        if k % 4 == 0:
                            input_half(k // 4)
                        ins = three(ps[:, bank, SEQ * f:SEQ * (f + 1)], wh[:, k, 128 * f:128 * (f + 1)],
                                    wl[:, k, 128 * f:128 * (f + 1)], AH[:, k, :], AL[:, k, :], k == 0, k == KT - 1)
                ins.then_inc(w_used, 1)

            def m_unit(w, bank, k0, nk, kts, sh=AH, sl=AL, s0=0, n=512, tiles=TT):
                u, h = w.next_unit()
                if sh is AH:
                    input_half(k0 // 4)
                pe.wait_ge(w_lo, u + 1)
                wh = whi[:, h, 0:nk * n].rearrange("p (k n) -> p k n", k=nk)
                wl = wlo[:, h, 0:nk * n].rearrange("p (k n) -> p k n", k=nk)
                for i in range(tiles):
                    for k in range(nk):
                        kk = k0 + k
                        ins = three(ps[:, bank + i, 0:n], sh[:, s0 + kk, 128 * i:128 * (i + 1)],
                                    sl[:, s0 + kk, 128 * i:128 * (i + 1)], wh[:, k, :], wl[:, k, :],
                                    kk == 0, kk == kts - 1)
                ins.then_inc(w_used, 1)

            def m_matrix(w, chunks, kts=KT, sh=AH, sl=AL, s0=0):
                for _ in range(chunks):
                    bank = pair(w)
                    for k0 in range(0, kts, 4):
                        m_unit(w, bank, k0, 4, kts, sh, sl, s0)

            def transposes(w):
                stage[0] += 1
                pe.wait_ge(ts_ready, stage[0])
                for q in range(2):
                    bank = pair(w)
                    for k in range(4):
                        for i in range(TT):
                            ins = pe.transpose(ps[:, bank + k // 2, SEQ * (k % 2) + 128 * i:SEQ * (k % 2) + 128 * (i + 1)],
                                               TS[:, i, 512 * q + 128 * k:512 * q + 128 * (k + 1)], ident)
                    ins.then_inc(tp_done, 1)

            def new_input(whole=False):
                inputs[0] += 1
                if whole:
                    halves_in[0] = 2 * inputs[0]
                    pe.wait_ge(a_ready, halves_in[0])

            def ada_cols(bank, c0, chunk, n0, n):
                for f in range(n):
                    ins = pe.matmul(ps[:, bank, c0 + f:c0 + f + 1], acc[:, chunk, n0 + 128 * f:n0 + 128 * (f + 1)],
                                    ones[:, 0:1], start=True, stop=True)
                return ins

            def ada_rows(bank, chunk, n0):
                for c in range(2):
                    ins = pe.matmul(ps[:, bank + c, :], ones[:, 0:128], acc[:, chunk, n0 + 512 * c:n0 + 512 * (c + 1)],
                                    start=True, stop=True)
                return ins

            def ada_gates(w):
                bank = pair(w)
                ada_rows(bank, 1, 0).then_inc(ada_sum, 1)
                bank = pair(w)
                ada_cols(bank, 0, 1, 1024, 8)
                ada_cols(bank, 8, 2, 0, 8).then_inc(ada_sum, 1)
                bank = pair(w)
                ada_rows(bank, 2, 1024).then_inc(ada_sum, 1)

            def group(w):
                done = w.hidden
                for c, (_, n) in enumerate(COLS):
                    bank = pair(w)
                    t_unit(w, bank, n)
                    t_unit(w, bank + 1, n)
                for c in range(2):
                    bank = pair(w)
                    for k0, nk in KS:
                        if c == 0:
                            pe.wait_ge(hid_done, done + min(6, (k0 + nk + 1) // 2))
                        m_unit(w, bank, k0, nk, FT, HH, HL)
                w.hidden = done + 6

            def gather(w, tiles):
                for q in range(2):
                    bank = pair(w)
                    for k in range(4):
                        for i in range(TT):
                            ins = pe.matmul(ps[:, bank + k // 2, SEQ * (k % 2):SEQ * (k % 2) + 128 * tiles],
                                            TS[:, i, 512 * q + 128 * k:512 * q + 128 * (k + 1)],
                                            chosen[:, i, 0:128 * tiles], start=i == 0, stop=i == TT - 1)
                    ins.then_inc(e_gather, 1)

            def expert(w, e, tiles):
                def hidden_tp(bank, c):
                    pe.wait_ge(e_prod, 3 * e + c + 1)
                    for b in range(E_COLS[c][1] // 128):
                        for j in range(tiles):
                            c0 = SEQ * (b % 2) + 128 * j
                            ins = pe.transpose(ps[:, bank + b // 2, c0:c0 + 128],
                                               e_hid[:, c % 2, j, 128 * b:128 * (b + 1)], ident)
                    ins.then_inc(e_tp, 1)

                bank = pair(w)
                for i in range(TT):
                    for j in range(tiles):
                        ins = pe.transpose(ps[:, bank, SEQ * j + 128 * i:SEQ * j + 128 * (i + 1)],
                                           chosen[:, i, 128 * j:128 * (j + 1)], ident)
                ins.then_inc(place_tp, 1)
                pe.wait_ge(e_in, e + 1)
                for c, (_, n) in enumerate(E_COLS):
                    for _ in range(2):
                        bank = pair(w)
                        for k0 in (0, 4):
                            m_unit(w, bank, k0, 4, KT, n=n, tiles=tiles)
                    if c:
                        hidden_tp(pair(w), c - 1)
                pe.wait_ge(pick_set, e + 2)
                gather(w, tiles)
                tp_bank, bank = pair(w), pair(w)
                for c in range(2):
                    if c:
                        bank = pair(w)
                    for k0, nk in KS:
                        if c == 0:
                            pe.wait_ge(e_hidden, 3 * e + 1 + k0 // 4)
                        m_unit(w, bank, k0, nk, FT, HH, HL, tiles=tiles)
                        if c == 0 and k0 == 0:
                            hidden_tp(tp_bank, 2)
                pe.wait_ge(place_set, e + 1)
                for c in range(2):
                    bank = pair(w)
                    pe.wait_ge(e_set, 2 * e + c + 1)
                    for i in range(TT):
                        for j in range(tiles):
                            ins = pe.matmul(ps[:, bank + i, :], place[:, j, 128 * i:128 * (i + 1)],
                                            e_out[:, j, 512 * c:512 * c + 512], start=j == 0, stop=j == tiles - 1)
                    ins.then_inc(e_back, 1)

            pe.wait_ge(cst_in, 16)
            pe.wait_ge(rows_in, 12 * 16)
            bank = pair(w)
            pe.transpose(ps[:, bank, 0:128], TS[:, 1, 0:128], ident)
            pe.transpose(ps[:, bank + 1, 0:96], TS[0:96, 1, 128:256], cst[0:96, C_ID:C_ID + 96]).then_inc(rows_t, 1)
            pe.wait_ge(ones_set, 1)
            pe.wait_ge(ada_used, 8)
            bank = pair(w)
            ada_cols(bank, 0, 0, 0, 16).then_inc(ada_sum, 1)
            transposes(w)
            new_input()
            for _ in range(2):
                bank = pair(w)
                t_unit(w, bank)
                t_unit(w, bank + 1)
            m_matrix(w, 4)
            pe.wait_ge(small_in, 14 * 16)
            bank = pair(w)
            for g in range(2):
                for k in range(KT):
                    ins = pe.matmul(ps[0:8, bank + g, 0:SEQ], wsm[:, k, 8 * g:8 * g + 8], AF[:, k, :],
                                    start=k == 0, stop=k == KT - 1)
            ins.then_inc(small_mm, 1)
            pe.wait_ge(g_act, 2)
            bank = pair(w)
            for r, row in ((0, 5), (1, 7)):
                for i in range(TT):
                    ins = pe.transpose(ps[:, bank, 16 * r + 8 * i:16 * r + 8 * i + 8], rows[:, row, 128 * i:128 * (i + 1)],
                                       cst[0:8, C_ID:C_ID + 8])
            ins.then_inc(col_tp, 1)
            pe.wait_ge(consts_set, 1)
            pe.wait_ge(qk_silu, 1)
            pe.wait_ge(ps_free, w.pair)
            for step in range(M_HEADS + 1):
                if step < M_HEADS:
                    h = step
                    bank = pair(w)
                    assert bank == m_bank_s(h)
                    ro, kt = 64 * (h % 2), h // 2
                    pick = cst[0:8, C_ID + h:C_ID + h + 1].to_broadcast([8, 128])
                    M = rows[:, 6, :]
                    pe.matmul(ps[:, bank, 0:256], pick, M, start=True, stop=False)
                    pe.matmul(ps[:, bank, 0:128], identb[:, :], maskb[:, 1, :], start=False, stop=True)
                    pe.matmul(ps[:, bank, 256:384], pick, M[:, 128:256], start=True, stop=False)
                    pe.matmul(ps[:, bank, 256:384], identb[:, :], maskb[:, 1, :], start=False, stop=True)
                    q, k = qk[ro:ro + 64, kt, :], qk[ro:ro + 64, 4 + kt, :]
                    pe.matmul(ps[:, bank + 1, 0:256], k[:, 0:128], q, start=True, stop=True)
                    pe.matmul(ps[:, bank + 1, 256:384], k[:, 128:256], q[:, 128:256], start=True, stop=True)\
                      .then_inc(m_sc, 1)
                if step >= 1:
                    h = step - 1
                    bank = pair(w)
                    pe.wait_ge(m_pt, h + 1)
                    p = pt[:, h % 2, :]
                    pe.matmul(ps[:, bank, 0:129], p[:, 0:128], vx[:, 0, h, :], start=True, stop=True)
                    pe.matmul(ps[:, bank, 256:385], p[:, 128:256], vx[:, 0, h, :], start=True, stop=False)
                    pe.matmul(ps[:, bank, 256:385], p[:, 256:384], vx[:, 1, h, :], start=False, stop=True)\
                      .then_inc(m_o, 1)
            transposes(w)
            pe.wait_ge(ada_used, 24)
            ada_gates(w)
            new_input()
            m_matrix(w, 2)
            transposes(w)
            new_input()
            assert w.pair == PAIR_FFN
            for e in range(2):
                group(w)
            pe.wait_ge(ada_used, 48)
            bank = pair(w)
            ada_cols(bank, 0, 0, 0, 16).then_inc(ada_sum, 1)
            ada_gates(w)
            transposes(w)
            new_input()
            for _ in range(4):
                bank = pair(w)
                t_unit(w, bank)
                t_unit(w, bank + 1)
            m_matrix(w, 4)
            for lev in range(-1, LEVELS + 1):
                n = lev + 1
                if lev < LEVELS:
                    pe.wait_ge(l_kq, n + 1)
                    lhs = rhs = level_buf[n % 3].rearrange("p (g t) -> p g t", g=16)
                else:
                    lhs, rhs = (a.rearrange("p (g t) -> p g t", g=16) for a in (hk, hq))
                for half_ in range(1 if lev < 0 else 2):
                    bank = pair(w)
                    for g in range(8):
                        if lev < 0:
                            l_ap, r_ap = lhs[:, 2 * g, :], rhs[:, 2 * g + 1, :]
                        else:
                            l_ap, r_ap = lhs[:, 8 * half_ + g, :], rhs[:, 8 * half_ + g, :]
                        ins = pe.matmul(ps[:, bank + g // 4, 128 * (g % 4):128 * (g % 4) + 128], l_ap, r_ap,
                                        start=True, stop=True)
                    ins.then_inc(l_mm, 1)
            for i in range(TT):
                bank = pair(w)
                if i == 0:
                    pe.wait_ge(ps_free, w.pair - 1)
                for h in range(H_HEADS):
                    o = ps[:, bank + h // 4, 128 * (h % 4):128 * (h % 4) + 128]
                    ins = pe.matmul(o, at[:, 2 * h + i, :], hv[:, i, 128 * h:128 * h + 128], start=True, stop=i == 0)
                    if i:
                        ins = pe.matmul(o, ax[:, h, :], hv[:, 0, 128 * h:128 * h + 128], start=False, stop=True)
                ins.then_inc(h_o, 1)
            transposes(w)
            new_input()
            m_matrix(w, 2)
            transposes(w)
            new_input(whole=True)
            bank = pair(w)
            for i in range(TT):
                for k in range(KT):
                    ins = pe.matmul(ps[:, bank, 8 * i:8 * i + 8], AF[:, k, 128 * i:128 * (i + 1)], wsm[:, k, 16:24],
                                    start=k == 0, stop=k == KT - 1)
            ins.then_inc(small_mm, 1)
            pe.wait_ge(tokens_set, 1)
            bank = pair(w)
            for i in range(TT):
                if i:
                    pe.matmul(ps[:, bank, 8:16], ones[:, 0:128], oh[:, 0, 0, :], start=True, stop=False)
                pe.matmul(ps[:, bank, 8 * i:8 * i + 8], upto, oh[:, 0, i, :], start=i == 0, stop=True)
            for i in range(TT):
                ins = pe.matmul(ps[:, bank, 16:24], ones[:, 0:128], oh[:, 0, i, :], start=i == 0, stop=i == TT - 1)
            ins.then_inc(small_mm, 1)
            pe.wait_ge(crowd_set, 1)
            crowd = pe.value_load(crowded[0:1, 0:1], min_val=0, max_val=1)
            pe.wait_ge(pick_set, 1)
            gather(w, TT)
            assert w.pair == PAIR_MOE

            def experts(tiles):
                with pe.Fori(0, N_EXPERTS) as e:
                    expert(w.after_groups(e, E_PAIRS), e, tiles)

            with pe.If(crowd > 0):
                experts(TT)
            with pe.Else():
                experts(1)
            w = w.after_groups(N_EXPERTS, E_PAIRS)
            transposes(w)
            new_input()
            m_matrix(w, 2)
            stage[0] += 1
            transposes(w)
            new_input()

            def qk_transposes(n):
                src = mkv[:, 0] if NORMED[n][0] is None else qkv[:, NORMED[n][0]]
                pe.wait_ge(qk_ready, n + 1)
                bank = pair(w)
                for k in range(4):
                    for i in range(TT):
                        ins = pe.transpose(ps[:, bank + k // 2, SEQ * (k % 2) + 128 * i:SEQ * (k % 2) + 128 * (i + 1)],
                                           src[:, i, 128 * k:128 * (k + 1)], ident)
                ins.then_inc(tp_done, 1)

            for j in range(7):
                m_matrix(w, 1)
                if j == 0:
                    bank = pair(w)
                    for k in range(KT):
                        ins = pe.matmul(ps[0:40, bank, 0:SEQ], wsm[:, k, 24:64], AF[:, k, :], start=k == 0, stop=k == KT - 1)
                    ins.then_inc(small_mm, 1)
                if j - 1 in NORM_BEHIND:
                    qk_transposes(NORM_BEHIND[j - 1])
            qk_transposes(len(NORMED) - 1)
            pe.wait_ge(qk_set, 6)
            pe.wait_ge(fox_set, 1)
            for b, (gh0, heads, dh, causal, fox) in enumerate(BRANCHES):
                per = 128 // dh
                qT = acc[:, b, 0:1024].rearrange("p (k t) -> p k t", k=4)
                kT = acc[:, b, 1024:2048].rearrange("p (k t) -> p k t", k=4)
                s_bank = {}
                o_bank = {}
                n0 = 128 if causal else 256
                for step in range(heads + 2):
                    if step < heads:
                        h = step
                        s_bank[h] = bank = pair(w)
                        assert bank == t_bank_s(gh0 + h)
                        ro, kt = dh * (h % per), h // per
                        q, k = qT[ro:ro + dh, kt, :], kT[ro:ro + dh, kt, :]
                        for i, (c0, n) in enumerate(((0, n0), (n0, 256))):
                            o = ps[:, bank, c0:c0 + n]
                            ins = pe.matmul(o, q[:, 128 * i:128 * (i + 1)], k[:, 0:n], start=True, stop=not causal)
                            if fox:
                                pe.matmul(o, fox_l[:, h, 128 * i:128 * (i + 1)], fox_r[:, 0:n], start=False, stop=False)
                            if causal:
                                ins = pe.matmul(ps[:, bank, c0 + n - 128:c0 + n], identb[:, :], maskb[:, 0, :],
                                                start=False, stop=True)
                        ins.then_inc(t_s, 1)
                    if 1 <= step <= heads:
                        h = step - 1
                        bank = s_bank[h] + 1
                        pe.wait_ge(t_p, gh0 + h + 1)
                        p = prb[:, (gh0 + h) % 2, :]
                        cuts = ((0, 0), (128, 128), (256, 256)) if causal else ((0, 0), (256, 128), (128, 256), (384, 384))
                        for c_in, c_out in cuts:
                            ins = pe.transpose(ps[:, bank, c_out:c_out + 128], p[:, c_in:c_in + 128], ident)
                        ins.then_inc(t_tp, 1)
                    if step >= 2:
                        h = step - 2
                        ro, kt = dh * (h % per), h // per
                        if kt not in o_bank:
                            o_bank[kt] = pair(w)
                        bank = o_bank[kt]
                        pe.wait_ge(t_pt, gh0 + h + 1)
                        p = pts[:, (gh0 + h) % 2, :]
                        v = mkv[:, 1] if b == 2 else qkv[:, 3 * b + 2]
                        q0 = 128 if causal else 0
                        pe.matmul(ps[ro:ro + dh, bank, 0:256], v[:, 0, dh * h:dh * (h + 1)], p[:, 0:256],
                                  start=True, stop=False)
                        pe.matmul(ps[ro:ro + dh, bank, q0:256], v[:, 1, dh * h:dh * (h + 1)], p[:, 256:512 - q0],
                                  start=False, stop=True).then_inc(t_o, 1)
            pe.wait_ge(t_y, 12)
            for b in range(3):
                m_matrix(w, 2)
                m_matrix(w, 2, 4, HH, HL, 4 * b)
            pe.wait_ge(ts_ready, 10)
            for q in range(2):
                bank = pair(w)
                for k in range(4):
                    for i in range(TT):
                        ins = pe.transpose(ps[:, bank + k // 2, SEQ * (k % 2) + 128 * i:SEQ * (k % 2) + 128 * (i + 1)],
                                           TS[:, i, 512 * q + 128 * k:512 * q + 128 * (k + 1)], ident)
                ins.then_inc(tp_done, 1)
            new_input()
            m_matrix(w, 2)
            stage[0] = 10
            transposes(w)
            new_input(whole=True)
            assert w.pair == PAIR_FFN2 and w.pb == PAIR_FFN2 % 4
            with pe.Fori(0, 2) as e:
                group(w.after_groups(e))

        @block.vector
        def _(dve):
            steps = [0]

            def link(ins):
                steps[0] = steps[0] + 1
                ins.then_inc(vec_step, 1)
                dve.wait_ge(vec_step, steps[0])

            def both(ins, s, n):
                ins.then_inc(s, 1)
                dve.wait_ge(s, n)

            def free(w, ins):
                w.next_pair()
                ins.then_inc(ps_free, 1)
                dve.wait_ge(ps_free, w.pair)

            def bank_of(w):
                return 2 * w.pb

            def lo(w, n=UNIT):
                s, _ = w.next_raw()
                u, h = w.next_unit()
                dve.wait_ge(w_hi, u + 1)
                dve.tensor_tensor(wlo[:, h, 0:n], raw_at[s][:, 0:n], whi[:, h, 0:n].bitcast(fp), ALU.subtract)\
                   .then_inc(w_lo, 1)

            def los(w, k):
                for _ in range(k):
                    lo(w)

            def ada_begin(layer, chunk):
                dve.tensor_tensor(acc[:, chunk, :].rearrange("p (f n) -> p f n", f=16),
                                  ident.rearrange("p (o n) -> p o n", o=1).to_broadcast([128, 16, 128]),
                                  adab[:, 48 * layer + 16 * chunk:48 * layer + 16 * chunk + 16]
                                  .rearrange("p (f o) -> p f o", o=1).to_broadcast([128, 16, 128]),
                                  ALU.mult).then_inc(ada_init, 1)
                dve.wait_ge(ada_init, 3 * layer + chunk + 1)

            def ada_unit(w, layer, chunk, k):
                if k == 0 and (layer, chunk) != (0, 0):
                    ada_begin(layer, chunk)
                s, full = w.next_raw()
                at_least(dve, ada_used, w.ada)
                dve.wait_ge(raw_full[s], full)
                dve.scalar_tensor_tensor(acc[:, chunk, :], raw_at[s], cond[:, k:k + 1], acc[:, chunk, :],
                                         ALU.mult, ALU.add).then_inc(ada_used, 1)
                w.ada += 1

            def root(n, width):
                m, y, s = ms[:, 0:n], rs[:, 0:n], nt[:, 0:n]
                link(dve.tensor_scalar(m, ss[:, 0:n], 1.0 / width, EPS, ALU.mult, ALU.add))
                dve.reciprocal(y, m).then_inc(root_in, 1)
                counts["root"] += 1
                dve.wait_ge(root_out, counts["root"])
                link(dve.tensor_tensor(s, y, y, ALU.mult))
                link(dve.tensor_tensor(s, s, m, ALU.mult))
                link(dve.tensor_scalar(s, s, -0.5, 1.5, ALU.mult, ALU.add))
                link(dve.tensor_tensor(y, y, s, ALU.mult))

            counts = dict(half=0, root=0, sq=0, ts=0, tp=0, a=0)

            def normalise(src):
                counts["sq"] += 2
                dve.wait_ge(sq_done, counts["sq"])
                root(2, D)
                for i in range(TT):
                    ins = dve.tensor_scalar(TS[:, i, :], src[:, i, :], rs[:, i:i + 1], None, ALU.mult)
                counts["ts"] += 1
                ins.then_inc(ts_ready, 1)

            def to_features(w, scale=None, shift=None, split=True):
                for q in range(2):
                    counts["tp"] += 1
                    if q and counts["tp"] > 2:
                        counts["half"] += 1
                        dve.wait_ge(half_set, counts["half"])
                        assert w.pair == FEATURE_PAIRS[counts["half"] - 1]
                        w.next_pair()
                        dve.sem_inc(ps_free, 1)
                        if split:
                            dve.tensor_tensor(AL[:, 4:8, :], AF[:, 4:8, :], AH[:, 4:8, :].bitcast(fp), ALU.subtract)\
                               .then_inc(a_ready, 1)
                            counts["a"] += 1
                        continue
                    dve.wait_ge(tp_done, counts["tp"])
                    bank = bank_of(w)
                    for k in range(4):
                        kk = 4 * q + k
                        src = ps[:, bank + k // 2, SEQ * (k % 2):SEQ * (k % 2) + SEQ]
                        if scale is None:
                            ins = dve.tensor_copy(AF[:, kk, :], src)
                        elif shift is None:
                            ins = dve.tensor_scalar(AF[:, kk, :], src, scale[:, kk:kk + 1], None, ALU.mult)
                        else:
                            ins = dve.tensor_scalar(AF[:, kk, :], src, scale[:, kk:kk + 1], shift[:, kk:kk + 1],
                                                    ALU.mult, ALU.add)
                    free(w, ins)
                    if not split:
                        continue
                    half_ = slice(4 * q, 4 * q + 4)
                    link(dve.tensor_copy(AH[:, half_, :], AF[:, half_, :]))
                    dve.tensor_tensor(AL[:, half_, :], AF[:, half_, :], AH[:, half_, :].bitcast(fp), ALU.subtract)\
                       .then_inc(a_ready, 1)
                    counts["a"] += 1
                if not split:
                    dve.sem_inc(a_ready, 2)
                    counts["a"] += 2
                dve.wait_ge(a_ready, counts["a"])

            def norm_scale(scale_cols, norm_cols):
                link(dve.scalar_tensor_tensor(scl, scale_cols, 1.0, norm_cols, ALU.add, ALU.mult))

            def head_norm(w, norm_cols):
                dve.wait_ge(ogs_set, 1 if norm_cols == V_MNORM else 2)
                link(dve.tensor_tensor(og, TS[:, :, :], og, ALU.mult))
                counts["sq"] += 1
                dve.wait_ge(sq_done, counts["sq"])
                root(16, M_DV)
                counts["ts"] += 1
                dve.tensor_tensor(flatT.rearrange("p (g n) -> p g n", g=16),
                                  Z[:, 4352:6400].rearrange("p (g n) -> p g n", g=16),
                                  rs.rearrange("p (g o) -> p g o", o=1).to_broadcast([128, 16, 128]), ALU.mult)\
                   .then_inc(ts_ready, 1)

            def out_matrix(w, n_ready, ahead):
                first = w.unit - LEAD
                for c in range(2):
                    if c == 0:
                        los(w, 2)
                    else:
                        ahead()
                    dve.wait_ge(w_used, first + 2 * c + 2)
                    bank = bank_of(w)
                    cut = slice(512 * c, 512 * c + 512)
                    tmp = tok(flatA[:, 1024 * c:1024 * c + 1024])
                    for i in range(TT):
                        ins = dve.tensor_tensor(tmp[:, i, :], ps[:, bank + i, :], GB[:, 0, cut], ALU.mult)
                    free(w, ins)
                    ins = dve.tensor_tensor(X[:, :, cut], X[:, :, cut], tmp, ALU.add)
                both(ins, x_ready, n_ready)

            def ada_gates(w, n):
                for g in range(3):
                    dve.wait_ge(ada_sum, n + g)
                    bank = bank_of(w)
                    if g == 1:
                        ins = dve.tensor_copy(mod[:, 2:4, :], ps[:, bank, 0:16].rearrange("p (a k) -> p a k", a=2))
                    else:
                        ins = dve.tensor_copy(GB[:, g // 2, :].rearrange("p (b n) -> p b n", b=2), ps[:, bank:bank + 2, :])
                    free(w, ins)

            def evac_t(w, c, done):
                dve.wait_ge(silu_done, done + c + 1)
                bank = bank_of(w)
                n = 2 * COLS[c][1]
                free(w, dve.tensor_tensor(hid[:, c % 2, 0:n], sil[:, c % 2, 0:n], ps[:, bank + 1, 0:n], ALU.mult))
                hh = HH[:, 2 * c:2 * c + n // SEQ, :].rearrange("p k t -> p (k t)")
                hl = HL[:, 2 * c:2 * c + n // SEQ, :].rearrange("p k t -> p (k t)")
                link(dve.tensor_copy(hh, hid[:, c % 2, 0:n]))
                dve.tensor_tensor(hl, hid[:, c % 2, 0:n], hh.bitcast(fp), ALU.subtract).then_inc(hid_done, 1)

            def evac_d(w, first_unit, c):
                dve.wait_ge(w_used, first_unit + 12 + 3 * (c + 1))
                bank = bank_of(w)
                cut = slice(512 * c, 512 * c + 512)
                for i in range(TT):
                    ins = dve.scalar_tensor_tensor(Y[:, i, cut], ps[:, bank + i, :], gcur[:, i:i + 1], Y[:, i, cut],
                                                   ALU.mult, ALU.add)
                free(w, ins)

            def group_from(w, first, first_unit, done, side):
                for j in range(first, 18):
                    lo(w, JOBS[j])
                    if j < 12:
                        side(j)
                    if 3 <= j <= 13 and j % 2:
                        evac_t(w, (j - 3) // 2, done)
                evac_d(w, first_unit, 0)

            def groups(w, n, side=lambda e, j: None, last=False):
                first_unit, done = w.unit - LEAD, w.hidden

                def rest(w, e, first_unit, done):
                    group_from(w, 2, first_unit, done, lambda j: side(e, j))

                def next_start(w, e):
                    for j in range(2):
                        lo(w, JOBS[j])
                        side(e, j)

                for e in range(n - 1):
                    rest(w, e, first_unit + e * 18, done + e * 6)
                    next_start(w, e + 1)
                    evac_d(w, first_unit + e * 18, 1)
                e = n - 1
                rest(w, e, first_unit + e * 18, done + e * 6)
                if not last:
                    los(w, LEAD)
                evac_d(w, first_unit + e * 18, 1)
                w.hidden = done + 6 * n
                return w

            w = Walk()
            dve.memset(wsm[:, :, :], 0.0).then_inc(cleared, 1)
            dve.memset(col[:, :], 0.0).then_inc(cleared, 1)
            dve.memset(vx[:, :, :, 128:129].rearrange("p i h o -> p (i h) o"), 1.0)
            dve.wait_ge(cleared, 2)
            dve.memset(ones2, 1.0)
            dve.wait_ge(rows_t, 1)
            dve.tensor_copy(vec[:, :], ps[:, 0, 0:128]).then_inc(vec_set, 1)
            free(w, dve.tensor_copy(adab[:, :], ps[:, 1, 0:96]))
            ada_begin(0, 0)
            dve.wait_ge(cond_set, 1)
            for k in range(KT):
                ada_unit(w, 0, 0, k)
            dve.wait_ge(cst_in, 32)
            dve.tensor_copy(identb[:, :], ident)
            dve.tensor_copy(maskb[:, :, :], cst[:, C_CAUSAL:C_CAUSAL + 256].rearrange("p (a n) -> p a n", a=2))\
               .then_inc(consts_set, 1)

            def in_units(k):
                for _ in range(k):
                    lo(w)
                    if w.unit <= 8:
                        ada_unit(w, 0, 1, w.unit - 1)

            normalise(X)
            in_units(1)
            dve.wait_ge(ada_sum, 1)
            free(w, dve.tensor_copy(mod[:, 0:2, :], ps[:, 2, 0:16].rearrange("p (a k) -> p a k", a=2)))
            norm_scale(mod[:, 1, :], vec[:, V_NORM1:V_NORM1 + 8])
            to_features(w, scl, mod[:, 0, :])
            in_units(1)
            dve.wait_ge(small_in, 14 * 16)
            link(dve.tensor_scalar(bias8[0:8, 2:3], bias8[0:8, 0:1], 1.0 / 15.0, None, ALU.mult))
            for q in range(2):
                in_units(2)
                dve.wait_ge(w_used, 2 * q + 2)
                bank = bank_of(w)
                for tap in range(CONV_K):
                    for k in range(4):
                        kk = 4 * q + k
                        x_ = ps[:, bank + k // 2, SEQ * (k % 2):SEQ * (k % 2) + SEQ - tap]
                        wc = vec[:, V_CONVW + 8 * (CONV_K - 1 - tap) + kk:V_CONVW + 8 * (CONV_K - 1 - tap) + kk + 1]
                        if tap == 0:
                            ins = dve.tensor_scalar(qk[:, kk, :], x_, wc, vec[:, V_CONVB + kk:V_CONVB + kk + 1],
                                                    ALU.mult, ALU.add)
                        else:
                            ins = dve.scalar_tensor_tensor(qk[:, kk, tap:], x_, wc, qk[:, kk, tap:], ALU.mult, ALU.add)
                    if tap < CONV_K - 1:
                        link(ins)
                free(w, ins)
            dve.sem_inc(conv_done, 1)
            for c in range(4):
                if c < 3:
                    in_units(2)
                dve.wait_ge(w_used, 4 + 2 * c + 2)
                bank = bank_of(w)
                cc = c % 2
                for i in range(TT):
                    if c < 2:
                        ins = dve.tensor_copy(vx[:, i, 4 * cc:4 * cc + 4, 0:128],
                                              ps[:, bank + i, :].rearrange("p (h n) -> p h n", h=4))
                    else:
                        ins = dve.tensor_copy(og[:, i, 512 * cc:512 * cc + 512], ps[:, bank + i, :])
                free(w, ins)
            dve.sem_inc(og_set, 1)
            dve.wait_ge(small_mm, 1)
            bank = bank_of(w)
            dve.tensor_copy(rows[:, 0, :], ps[0:8, bank, 0:SEQ])
            free(w, dve.tensor_scalar(rows[:, 1, :], ps[0:8, bank + 1, 0:SEQ], bias8[0:8, 1:2], None, ALU.add))
            dve.scalar_tensor_tensor(rows[:, 2, :], rows[:, 1, :], -1.0, rows[:, 1, :], ALU.mult, ALU.max).then_inc(g_vec, 1)
            dve.wait_ge(g_act, 1)
            link(dve.scalar_tensor_tensor(rows[:, 4, :], rows[:, 1, :], 0.0, rows[:, 3, :], ALU.min, ALU.subtract))
            link(dve.tensor_tensor_scan(rows[:, 2, :], ones[0:8, :], rows[:, 4, :], 0.0, ALU.mult, ALU.add))
            link(dve.scalar_tensor_tensor(rows[:, 5, :], rows[:, 0, :], 15.0, rows[:, 2, :], ALU.mult, ALU.subtract))
            link(dve.tensor_tensor_scan(rows[:, 6, :], ones[0:8, :], rows[:, 5, :], 0.0, ALU.mult, ALU.max))
            dve.tensor_tensor(rows[:, 7, :], rows[:, 2, :], rows[:, 6, :], ALU.add).then_inc(g_vec, 1)
            dve.wait_ge(col_tp, 1)
            bank = bank_of(w)
            free(w, dve.tensor_copy(col[:, 48:80], ps[:, bank, 0:32]))
            dve.sem_inc(cols_set, 1)
            for step in range(M_HEADS + 1):
                if step < M_HEADS:
                    h = step
                    dve.wait_ge(m_exp, h + 1)
                    at_least(dve, m_o, h - 1)
                    bank = bank_of(w)
                    w.next_pair()
                    dve.scalar_tensor_tensor(pt[:, h % 2, :], ps[:, bank + 1, 0:384], M_DQK ** -0.5, em[:, h % 2, :],
                                             ALU.mult, ALU.mult).then_inc(m_pt, 1)
                    dve.wait_ge(m_pt, h + 1)
                    dve.sem_inc(ps_free, 1)
                if step >= 1:
                    h = step - 1
                    dve.wait_ge(m_o, h + 1)
                    bank = bank_of(w)
                    d = dcol[:, 8 + 2 * (h % 2):10 + 2 * (h % 2)]
                    link(dve.scalar_tensor_tensor(d, ps[:, bank, 128:512:256], -1.0, ecol[:, :, h], ALU.mult, ALU.max))
                    link(dve.tensor_tensor(d, ps[:, bank, 128:512:256], d, ALU.max))
                    link(dve.reciprocal(d, d))
                    for i in range(TT):
                        ins = dve.tensor_scalar(TS[:, i, 128 * h:128 * h + 128], ps[:, bank, 256 * i:256 * i + 128],
                                                d[:, i:i + 1], None, ALU.mult)
                    free(w, ins)
                    dve.sem_inc(head_out, 1)
                    ada_unit(w, 0, 2, h)
            dve.sem_inc(heads_done, 1)
            head_norm(w, V_MNORM)
            lo(w)
            to_features(w, vec[:, V_MNORM:V_MNORM + 8])
            lo(w)
            ada_gates(w, 2)

            def ffn_ada(e, j):
                ada_unit(w, 1, (12 * e + j) // 8, (12 * e + j) % 8)

            def ffn_start():
                lo(w)
                ffn_ada(0, 0)
                lo(w)

            out_matrix(w, 1, ffn_start)
            norm_scale(mod[:, 3, :], vec[:, V_NORM2:V_NORM2 + 8])
            normalise(X)
            ffn_ada(0, 1)
            to_features(w, scl, mod[:, 2, :])
            link(dve.tensor_copy(gcur, ones2))
            dve.wait_ge(sum_clear, 1)
            w = groups(w, 2, side=ffn_ada)

            def add_layer(n_ready, gate_row=None, s=x_ready):
                if gate_row is not None:
                    for i in range(TT):
                        ins = dve.tensor_tensor(Y[:, i, :], Y[:, i, :], gate_row, ALU.mult)
                    link(ins)
                both(dve.tensor_tensor(X[:, :, :], X[:, :, :], Y, ALU.add), s, n_ready)

            add_layer(2, GB[:, 1, :])
            dve.wait_ge(ada_sum, 5)
            bank = bank_of(w)
            free(w, dve.tensor_copy(mod[:, 0:2, :], ps[:, bank, 0:16].rearrange("p (a k) -> p a k", a=2)))
            ada_gates(w, 6)
            norm_scale(mod[:, 1, :], vec[:, V_NORM1 + 8:V_NORM1 + 16])
            normalise(X)
            to_features(w, scl, mod[:, 0, :])
            dve.tensor_tensor(lbc[:, 0:8], vec[:, V_LB:V_LB + 8], vec[:, V_LB:V_LB + 8], ALU.subtract)\
               .then_inc(h_vec, 1)
            first_unit = w.unit - LEAD
            for q in range(4):
                los(w, 2)
                dve.wait_ge(w_used, first_unit + 2 * q + 2)
                bank = bank_of(w)
                dst = (hq if q < 2 else hk)[:, 1024 * (q % 2):1024 * (q % 2) + 1024]
                free(w, dve.tensor_copy(dst.rearrange("p (b n) -> p b n", b=2), ps[:, bank:bank + 2, :]))
                if q % 2:
                    dve.sem_inc(h_raw, 1)
            for c in range(4):
                los(w, 2)
                dve.wait_ge(w_used, first_unit + 8 + 2 * c + 2)
                bank = bank_of(w)
                dst = (hv if c < 2 else og)[:, :, 512 * (c % 2):512 * (c % 2) + 512]
                free(w, dve.tensor_copy(dst, ps[:, bank:bank + 2, :]))
                if c == 0:
                    dve.wait_ge(h_act, 3)
                    link(dve.reciprocal(lbc[:, 8:16], lbc[:, 0:8]))
                    link(dve.tensor_tensor(lbc[:, 0:8], lbc[:, 0:8], lbc[:, 8:16], ALU.mult))
                    link(dve.tensor_tensor(lbc[:, 0:8], lbc[:, 0:8], lbc[:, 0:8], ALU.subtract))
                    link(dve.tensor_scalar(lbc[:, 8:16], lbc[:, 0:8], -1.0, 1.0, ALU.mult, ALU.add))
                    for k in range(KT):
                        cut = slice(SEQ * k, SEQ * (k + 1))
                        dve.tensor_scalar(hk[:, cut], hk[:, cut], lbc[:, 8 + k:9 + k], None, ALU.mult)
                        ins = dve.tensor_scalar(flatA[:, cut], flatA[:, cut], lbc[:, 8 + k:9 + k], lbc[:, k:k + 1],
                                                ALU.mult, ALU.add)
                    link(ins)
                    both(dve.tensor_scalar(flatA, flatA, F_FLOOR, None, ALU.max), h_vec, 2)
                if c == 1:
                    dve.wait_ge(h_act, 4)
                    kq = level_buf[2]
                    dve.tensor_scalar(flatA, flatA, 2.0 ** -40, None, ALU.is_lt)
                    link(dve.tensor_scalar(kq, kq, float(np.log(LN_SHIFT)), None, ALU.subtract))
                    link(dve.copy_predicated(flatT, flatA.bitcast(i32), kq))
                    dve.wait_ge(starts_set, 2)
                    both(dve.tensor_tensor_scan(hb, at.rearrange("p g n -> p (g n)"), flatT, 0.0, ALU.mult, ALU.add),
                         sums_set, 1)
            dve.sem_inc(og_set, 1)
            def halves(a, blk):
                v = a.rearrange("p (n two b) -> p n two b", two=2, b=blk)
                return v[:, :, 0, :], v[:, :, 1, :]

            def sub(n):
                blk = 128 >> n
                left, right = halves(level_buf[n % 3], blk)
                bl, br = halves(hb, blk)
                ref = bl[:, :, blk - 1:blk].to_broadcast([128, 1024 // blk, blk])
                dve.tensor_tensor(left, ref, bl, ALU.subtract)
                if n == 0:
                    dve.tensor_copy(right, br).then_inc(l_sub, 1)
                else:
                    dve.tensor_tensor(right, br, ref, ALU.subtract).then_inc(l_sub, 1)

            mm_count = 0
            sub(0)
            for n in range(LEVELS + 2):
                if n < LEVELS:
                    sub(n + 1)
                if n <= LEVELS:
                    dve.wait_ge(l_exp, n + 1)
                    blk = 128 >> n
                    left, right = halves(level_buf[n % 3], blk)
                    dve.tensor_tensor(left, left, halves(hk, blk)[0], ALU.mult)
                    dve.tensor_tensor(right, right, halves(hq, blk)[1], ALU.mult).then_inc(l_kq, 1)
                for m in ([n - 1] if n <= LEVELS else [n - 1, n]):
                    if m < 0:
                        continue
                    for half_ in range(1 if m == 0 else 2):
                        mm_count += 1
                        dve.wait_ge(l_mm, mm_count)
                        bank = bank_of(w)
                        src = ps[:, bank:bank + 2, :]
                        if m == 0:
                            ins = dve.tensor_copy(ax.rearrange("p (b h) n -> p b (h n)", b=2), src)
                        else:
                            c0 = C_LEVEL + 128 * (m - 1)
                            dve.wait_ge(at_clear, 1)
                            mask = cst[:, c0:c0 + 128].bitcast(i32).rearrange("p (o n) -> p o n", o=1)\
                                .to_broadcast([128, 8, 128])
                            ins = dve.copy_predicated(at[:, 8 * half_:8 * half_ + 8, :], mask,
                                                      src.rearrange("p b (g n) -> p (b g) n", g=4))
                        free(w, ins)
            for i in range(TT):
                dve.wait_ge(h_o, i + 1)
                bank = bank_of(w)
                free(w, dve.tensor_copy(TS[:, i, :].rearrange("p (b n) -> p b n", b=2), ps[:, bank:bank + 2, :]))
                dve.sem_inc(head_out, 1)
            dve.sem_inc(heads_done, 1)
            head_norm(w, V_HNORM)
            to_features(w, vec[:, V_HNORM:V_HNORM + 8])

            def expert_start():
                w.depth = N_RAW_E
                los(w, LEAD)

            out_matrix(w, 3, expert_start)
            norm_scale(mod[:, 3, :], vec[:, V_NORM2 + 8:V_NORM2 + 16])
            normalise(X)
            to_features(w, scl, mod[:, 2, :], split=False)
            dve.wait_ge(small_mm, 2)
            bank = bank_of(w)
            free(w, dve.tensor_copy(lgt, ps[:, bank, 0:16].rearrange("p (i e) -> p i e", i=TT)))

            def over(a):
                return a.rearrange("p (i o) -> p i o", o=1).to_broadcast([128, TT, N_EXPERTS])

            rank = cst[:, C_RANK:C_RANK + 8].rearrange("p (o e) -> p o e", o=1).to_broadcast([128, TT, N_EXPERTS])
            for which, src in ((0, lgt), (1, lg2)):
                link(dve.tensor_reduce(mm2[:, which, :], src, AX.X, ALU.max))
                link(dve.tensor_tensor(oh[:, which], src, over(mm2[:, which, :]), ALU.is_equal))
                link(dve.tensor_tensor(oh[:, which], oh[:, which], rank, ALU.mult))
                link(dve.tensor_reduce(mm2[:, 7, :], oh[:, which], AX.X, ALU.max))
                link(dve.tensor_tensor(oh[:, which], rank, over(mm2[:, 7, :]), ALU.is_equal))
                if which == 0:
                    link(dve.scalar_tensor_tensor(lg2, oh[:, 0], -BIG, lgt, ALU.mult, ALU.add))
            dve.tensor_tensor(mm2[:, 2, :], mm2[:, 1, :], mm2[:, 0, :], ALU.subtract).then_inc(g_vec, 1)
            dve.wait_ge(g_act, 3)
            link(dve.tensor_scalar(mm2[:, 4, :], mm2[:, 3, :], 1.0, None, ALU.add))
            link(dve.reciprocal(mm2[:, 5, :], mm2[:, 4, :]))
            link(dve.tensor_tensor(mm2[:, 6, :], mm2[:, 5, :], mm2[:, 3, :], ALU.mult))
            link(dve.tensor_tensor(lgt, oh[:, 0], over(mm2[:, 5, :]), ALU.mult))
            link(dve.tensor_tensor(lg2, oh[:, 1], over(mm2[:, 6, :]), ALU.mult))
            dve.tensor_tensor(gates[:, :, 0:8], lgt, lg2, ALU.add)
            dve.tensor_scalar(upto, cst[:, C_CAUSALT:C_CAUSALT + 128], 0.0, None, ALU.is_equal)
            dve.tensor_tensor_scan(numbers, ones[:, :], ones[:, :], 0.0, ALU.mult, ALU.add)
            dve.memset(slot_of, 0.0)
            both(dve.tensor_tensor(oh[:, 0], oh[:, 0], oh[:, 1], ALU.add), tokens_set, 1)
            dve.wait_ge(small_mm, 3)
            bank = bank_of(w)
            dve.tensor_tensor(slot_of[:, :, 0:8], ps[:, bank, 0:16].rearrange("p (i e) -> p i e", i=TT), oh[:, 0], ALU.mult)
            free(w, dve.tensor_reduce(mm2[:, 0, 0:1], ps[:, bank, 16:24], AX.X, ALU.max))
            both(dve.tensor_scalar(crowded[:, :], mm2[:, 0, 0:1], 128.0, None, ALU.is_gt), crowd_set, 1)

            def choose(e, tiles):
                cut = slice(e, e + 1) if isinstance(e, int) else bass.ds(e, 1)
                link(dve.tensor_copy(slot_cur, slot_of[:, :, cut].rearrange("p i o -> p (i o)")))
                for i in range(TT):
                    ins = dve.tensor_scalar(chosen[:, i, 0:128 * tiles], numbers[:, 0:128 * tiles], slot_cur[:, i:i + 1],
                                            None, ALU.is_equal)
                ins.then_inc(pick_set, 1)

            def expert_low(v, n, tiles):
                dve.wait_ge(e_high, n)
                dve.sem_inc(ps_free, 2)
                v.next_pair(), v.next_pair()
                dve.tensor_tensor(AL[:, :, 0:128 * tiles], AF[:, :, 0:128 * tiles], AH[:, :, 0:128 * tiles].bitcast(fp),
                                  ALU.subtract).then_inc(e_in, 1)

            def expert(v, e, tiles):
                first = v.unit - LEAD

                def product(c):
                    dve.wait_ge(e_silu, 3 * e + c + 1)
                    dve.wait_ge(w_used, first + 4 * c + 4)
                    _, _ = v.next_pair()
                    bank = bank_of(v)
                    v.next_pair()
                    n = E_COLS[c][1]
                    dve.tensor_tensor(e_hid[:, c % 2, 0:tiles, 0:n], e_hid[:, c % 2, 0:tiles, 0:n],
                                      ps[:, bank:bank + tiles, 0:n], ALU.mult).then_inc(e_prod, 1)
                    dve.wait_ge(e_prod, 3 * e + c + 1)
                    dve.sem_inc(ps_free, 2)

                def split(c):
                    dve.wait_ge(e_tp, 3 * e + c + 1)
                    bank = bank_of(v)
                    nb = E_COLS[c][1] // 128
                    src = ps[:, bank:bank + 2, :].rearrange("p b (k t) -> p (b k) t", k=2)[:, 0:nb, 0:128 * tiles]
                    hh, hl = (a[:, 4 * c:4 * c + nb, 0:128 * tiles] for a in (HH, HL))
                    link(dve.tensor_copy(hh, src))
                    dve.tensor_tensor(hl, src, hh.bitcast(fp), ALU.subtract).then_inc(e_hidden, 1)
                    dve.wait_ge(e_hidden, 3 * e + c + 1)
                    v.next_pair()
                    dve.sem_inc(ps_free, 1)

                for j in range(LEAD, 18 + LEAD):
                    lo(v, E_JOBS[j % 18])
                    if j == 3:
                        dve.wait_ge(place_tp, e + 1)
                        bank = bank_of(v)
                        free(v, dve.tensor_copy(place[:, 0:tiles, :].rearrange("p j t -> p (j t)"),
                                                ps[:, bank, 0:SEQ * tiles]))
                        dve.sem_inc(place_set, 1)
                        choose(e + 1, tiles)
                        link(dve.tensor_copy(gcur, gates[:, :, bass.ds(e, 1)].rearrange("p i o -> p (i o)")))
                    if j == 6:
                        product(0)
                    if j == 10:
                        product(1)
                        split(0)
                    if j == 13:
                        product(2)
                        split(1)
                    if j == 14:
                        expert_low(v, e + 2, tiles)
                        split(2)
                    if j == 17:
                        dve.wait_ge(e_set, 2 * e + 1)
                        dve.sem_inc(ps_free, 1)
                        v.next_pair()
                dve.wait_ge(e_set, 2 * e + 2)
                dve.sem_inc(ps_free, 1)
                v.next_pair()
                for c in range(2):
                    dve.wait_ge(e_back, 2 * e + c + 1)
                    bank = bank_of(v)
                    cut = slice(512 * c, 512 * c + 512)
                    for i in range(TT):
                        ins = dve.scalar_tensor_tensor(Y[:, i, cut], ps[:, bank + i, :], gcur[:, i:i + 1], Y[:, i, cut],
                                                       ALU.mult, ALU.add)
                    if c == 0:
                        free(v, ins)
                    else:
                        ins.then_inc(ps_free, 1)

            choose(0, TT)
            dve.wait_ge(sum_clear, 2)
            dve.wait_ge(crowd_set, 1)
            crowd = dve.value_load(crowded[0:1, 0:1], min_val=0, max_val=1)
            expert_low(w, 1, TT)
            assert w.pair == PAIR_MOE
            LINKS = 5

            def experts(tiles):
                base = steps[0]
                with dve.Fori(0, N_EXPERTS) as e:
                    steps[0] = base + e * LINKS
                    dve.wait_ge(ps_free, w.pair + e * E_PAIRS)
                    expert(w.after_groups(e, E_PAIRS), e, tiles)
                steps[0] = base

            with dve.If(crowd > 0):
                experts(TT)
            with dve.Else():
                experts(1)
            steps[0] += LINKS * N_EXPERTS
            w = w.after_groups(N_EXPERTS, E_PAIRS)
            w.depth = N_RAW
            dve.wait_ge(ps_free, w.pair)
            normalise(memx)
            for i in range(TT):
                ins = dve.tensor_tensor(Y[:, i, :], Y[:, i, :], GB[:, 1, :], ALU.mult)
            link(ins)
            to_features(w, vec[:, V_GMEM:V_GMEM + 8])
            both(dve.tensor_tensor(X[:, :, :], X[:, :, :], Y, ALU.add), x_ready, 4)
            first_unit = w.unit - LEAD
            los(w, 2)
            normalise(X)
            dve.wait_ge(ts_ready, counts["ts"])
            dve.wait_ge(late_in, 16)
            for i in range(TT):
                ins = dve.tensor_tensor(X[:, i, :], TS[:, i, :], fwb, ALU.mult)
            both(ins, x_ready, 5)
            for c in range(2):
                if c == 1:
                    normalise(X)
                    los(w, 2)
                dve.wait_ge(w_used, first_unit + 2 * c + 2)
                bank = bank_of(w)
                free(w, dve.tensor_copy(mkv[:, c], ps[:, bank:bank + 2, :]))
            to_features(w, vec[:, V_GMIX:V_GMIX + 8])
            def forget_gates():
                dve.wait_ge(small_mm, 4)
                bank = bank_of(w)
                free(w, dve.tensor_scalar(frow[:, 0, :], ps[0:40, bank, 0:SEQ], bias8[0:40, 3:4], None, ALU.add))
                both(dve.scalar_tensor_tensor(frow[:, 1, :], frow[:, 0, :], -1.0, frow[:, 0, :], ALU.mult, ALU.max), g_vec, 4)
                dve.wait_ge(g_act, 4)
                link(dve.scalar_tensor_tensor(frow[:, 1, :], frow[:, 0, :], 0.0, frow[:, 2, :], ALU.min, ALU.subtract))
                link(dve.memset(fcum, 0.0))
                link(dve.tensor_tensor_scan(frow[:, 3, :], ones[0:40, :], frow[:, 1, :], 0.0, ALU.mult, ALU.add))
                dve.tensor_scalar(fox_r, fcum, cst[:, C_FOX:C_FOX + 1], cst[:, C_FOX + 1:C_FOX + 2],
                                  ALU.mult, ALU.add)
                for h in range(A_HEADS):
                    ins = dve.tensor_scalar(fox_l[:, h, :], fcum, cst[:, C_FOX + 2 + h:C_FOX + 3 + h],
                                            cst[:, C_FOX + 10 + h:C_FOX + 11 + h], ALU.mult, ALU.add)
                ins.then_inc(fox_set, 1)

            def norm_block(n):
                blk, g0, dh = NORMED[n][:3]
                counts["sq"] += 1
                dve.wait_ge(sq_done, counts["sq"])
                nh = 512 // dh
                a = (mkv[:, 0] if blk is None else qkv[:, blk]).rearrange("p i (h d) -> p i h d", d=dh)
                sq = GB[:, 0, :].rearrange("p (g d) -> p g d", d=dh)
                link(dve.tensor_reduce(ss[:, 0:2 * nh], sq, AX.X, ALU.add))
                root(2 * nh, dh)
                fa = a.rearrange("p i h d -> p (i h) d")
                link(dve.tensor_tensor(fa, fa, rs[:, 0:2 * nh].rearrange("p (g o) -> p g o", o=1)
                                       .to_broadcast([128, 2 * nh, dh]), ALU.mult))
                ins = dve.tensor_tensor(fa, fa, gains[:, g0:g0 + dh].rearrange("p (o d) -> p o d", o=1)
                                        .to_broadcast([128, 2 * nh, dh]), ALU.mult)
                if blk in (0, 1):
                    link(ins)
                    x1, x2 = a[:, :, :, 0:8], a[:, :, :, 8:16]
                    tr = TS[:, 0, 0:512].rearrange("p (r i h d) -> p r i h d", r=4, i=TT, h=A_HEADS)

                    def table(c0):
                        return cst[:, c0:c0 + 16].rearrange("p (i o d) -> p i o d", i=TT, o=1)\
                            .to_broadcast([128, TT, A_HEADS, 8])
                    for r, (x_, c0) in enumerate(((x1, C_COS), (x2, C_SIN), (x2, C_COS), (x1, C_SIN))):
                        ins = dve.tensor_tensor(tr[:, r], x_, table(c0), ALU.mult)
                    link(ins)
                    dve.tensor_tensor(x1, tr[:, 0], tr[:, 1], ALU.subtract)
                    ins = dve.tensor_tensor(x2, tr[:, 2], tr[:, 3], ALU.add)
                both(ins, qk_ready, n + 1)

            def copy_block(n):
                b, which = NORMED[n][3:5]
                counts["tp"] += 1
                dve.wait_ge(tp_done, counts["tp"])
                bank = bank_of(w)
                free(w, dve.tensor_copy(acc[:, b, 1024 * which:1024 * which + 1024]
                                        .rearrange("p (b n) -> p b n", b=2), ps[:, bank:bank + 2, :]))
                dve.sem_inc(qk_set, 1)

            first_unit = w.unit - LEAD
            for j in range(7):
                los(w, 2)
                dve.wait_ge(w_used, first_unit + 2 * j + 2)
                bank = bank_of(w)
                free(w, dve.tensor_copy(qkv[:, j], ps[:, bank:bank + 2, :]))
                if j in NORM_BEHIND:
                    dve.sem_inc(qk_raw, 1)
                if j == 0:
                    forget_gates()
                if j - 1 in NORM_BEHIND:
                    copy_block(NORM_BEHIND[j - 1])
                if j in NORM_BEHIND:
                    norm_block(NORM_BEHIND[j])
            copy_block(len(NORMED) - 1)
            outs = 0
            for b, (gh0, heads, dh, causal, fox) in enumerate(BRANCHES):
                n0 = 128 if causal else 256
                per = 128 // dh
                for step in range(heads + 4):
                    if 1 <= step <= heads:
                        gh = gh0 + step - 1
                        m0 = 2 * (gh % 2)
                        dve.wait_ge(t_exp, gh + 1)
                        link(dve.reciprocal(rsum[:, 4 + m0:6 + m0], rsum[:, m0:m0 + 2]))
                        dve.tensor_scalar(prb[:, gh % 2, 0:n0], prb[:, gh % 2, 0:n0], rsum[:, 4 + m0:5 + m0], None, ALU.mult)
                        dve.tensor_scalar(prb[:, gh % 2, n0:n0 + 256], prb[:, gh % 2, n0:n0 + 256],
                                          rsum[:, 5 + m0:6 + m0], None, ALU.mult).then_inc(t_p, 1)
                    if 2 <= step <= heads + 1:
                        gh = gh0 + step - 2
                        dve.wait_ge(t_tp, gh + 1)
                        at_least(dve, t_o, gh - 1)
                        bank = t_bank_s(gh) + 1
                        assert bank == bank_of(w) + 1
                        w.next_pair()
                        n = 384 if causal else 512
                        dve.tensor_copy(pts[:, gh % 2, 0:n], ps[:, bank, 0:n]).then_inc(t_pt, 1)
                        dve.wait_ge(t_pt, gh + 1)
                        dve.sem_inc(ps_free, 1)
                    if step < heads:
                        gh = gh0 + step
                        dve.wait_ge(t_s, gh + 1)
                        at_least(dve, t_exp, gh - 1)
                        bank = t_bank_s(gh)
                        m0 = 2 * (gh % 2)
                        dve.tensor_reduce(nmx[:, 4 + m0:5 + m0], ps[:, bank, 0:n0], AX.X, ALU.max)
                        link(dve.tensor_reduce(nmx[:, 5 + m0:6 + m0], ps[:, bank, n0:n0 + 256], AX.X, ALU.max))
                        dve.tensor_scalar(nmx[:, m0:m0 + 2], nmx[:, 4 + m0:6 + m0], -(dh ** -0.5), None, ALU.mult)\
                           .then_inc(t_max, 1)
                    h = step - 4
                    if 0 <= h and h % per == 0:
                        kt = h // per
                        dve.wait_ge(t_o, gh0 + h + per)
                        bank = bank_of(w)
                        outs += 1
                        hh, hl = HH[:, 4 * b + kt, :], HL[:, 4 * b + kt, :]
                        link(dve.tensor_copy(hh, ps[:, bank, 0:SEQ]))
                        both(dve.tensor_tensor(hl, ps[:, bank, 0:SEQ], hh.bitcast(fp), ALU.subtract), t_y, outs)
                        w.next_pair()
                        dve.sem_inc(ps_free, 1)
            first_unit = w.unit - LEAD
            for b in range(3):
                for c in range(2):
                    los(w, 2)
                    dve.wait_ge(w_used, first_unit + 6 * b + 2 * c + 2)
                    bank = bank_of(w)
                    free(w, dve.tensor_copy(sg[:, :, 512 * c:512 * c + 512], ps[:, bank:bank + 2, :]))
                dve.sem_inc(b_raw, 1)
                los(w, 1)
                dve.wait_ge(b_sig, b + 1)
                for c in range(2):
                    if c == 1:
                        los(w, 1)
                    dve.wait_ge(w_used, first_unit + 6 * b + 4 + c + 1)
                    bank = bank_of(w)
                    cut = slice(512 * c, 512 * c + 512)
                    dst = TS[:, :, cut] if b == 0 else tok(flatA[:, 0:1024])
                    free(w, dve.tensor_tensor(dst, ps[:, bank:bank + 2, :], sg[:, :, cut], ALU.mult))
                    if b:
                        link(dve.tensor_tensor(TS[:, :, cut], TS[:, :, cut], dst, ALU.add))
            counts["ts"] += 1
            dve.sem_inc(ts_ready, 1)
            to_features(w)
            first_unit = w.unit - LEAD
            for c in range(2):
                los(w, 2)
                dve.wait_ge(w_used, first_unit + 2 * c + 2)
                bank = bank_of(w)
                cut = slice(512 * c, 512 * c + 512)
                free(w, dve.tensor_tensor(X[:, :, cut], X[:, :, cut], ps[:, bank:bank + 2, :], ALU.add))
            dve.sem_inc(x_ready, 1)
            normalise(X)
            to_features(w, vec[:, V_GFFN:V_GFFN + 8])
            link(dve.tensor_copy(gcur, ones2))
            dve.wait_ge(sum_clear, 3)
            w = groups(w, 2, last=True)
            add_layer(1, s=out_ready)


_INPUTS = ["x", "c", "ada_w", "ada_b", "norm1_w", "norm2_w", "final_norm_w", "m_w_in", "m_i_bias", "m_f_bias",
           "m_conv_w", "m_conv_b", "m_norm_w", "m_w_out", "h_w_in", "h_lb_logits", "h_norm_w", "h_w_out",
           "ffn_w_gate", "ffn_w_up", "ffn_w_down", "moe_router", "moe_w_gate", "moe_w_up", "moe_w_down", "mem_2",
           "g_mix_2", "w_in_2", "b_forget_2", "g_q_moba_2", "g_k_moba_2", "g_q_fox_2", "g_k_fox_2", "g_q_mem_2",
           "g_k_mem_2", "g_mem_2", "w_mem_kv_2", "w_br_moba_2", "w_br_fox_2", "w_br_mem_2", "w_out_2", "g_ffn_2",
           "w_gate_2", "w_up_2", "w_down_2"]


def kernel(**inputs):
    import concourse.bacc as bacc
    from concourse.bass_utils import run_bass_kernel_spmd

    nc = bacc.Bacc("TRN2", target_bir_lowering=False, num_devices=1, dynamic_dma_scratch_size=256)
    arrays = {f"in_{n}": np.ascontiguousarray(inputs[n]) for n in _INPUTS}
    arrays["in_shape_consts"] = shape_constants()
    t = {n[3:]: nc.dram_tensor(n, a.shape, mybir.dt.from_np(a.dtype), kind="ExternalInput").ap()
         for n, a in arrays.items()}
    out = nc.dram_tensor("out_x", (1, SEQ, D), mybir.dt.float32, kind="ExternalOutput").ap()
    build(nc, t, out)
    r = run_bass_kernel_spmd(nc, [arrays], core_ids=[0])
    return r.results[0]["out_x"]
```
